# Optimizing a Trainium2 kernel written in Bass

```python
import jax, jax.numpy as jnp
from jax import lax
import numpy as np

D_MODEL = 1024
BATCH = 1
SEQ = 256
DEPTH = 1

HEAD_DIM = 64
BLOCK = 128
DIL_PATTERNS = ((128, 1), (512, 4), (2048, 16))
N_DIL_GROUPS = 3
DIL_HEADS_PER_GROUP = 8
DIL_HEADS = N_DIL_GROUPS * DIL_HEADS_PER_GROUP
DIL_WIDTH = DIL_HEADS * HEAD_DIM
DIL_MERGED = DIL_HEADS_PER_GROUP * HEAD_DIM
SWA_WINDOW = 128
SWA_Q_HEADS = 16
SWA_KV_HEADS = 2
SWA_Q_WIDTH = SWA_Q_HEADS * HEAD_DIM
SWA_KV_WIDTH = SWA_KV_HEADS * HEAD_DIM
IN_WIDTHS = (DIL_WIDTH, DIL_WIDTH, DIL_WIDTH, SWA_Q_WIDTH, SWA_KV_WIDTH, SWA_KV_WIDTH, D_MODEL, D_MODEL)
IN_WIDTH = sum(IN_WIDTHS)
MOE_GROUPS = 4
EXPERTS_PER_GROUP = 8
N_EXPERTS = MOE_GROUPS * EXPERTS_PER_GROUP
TOP_K = 2
D_EXPERT = 512
RMS_EPS = 1e-6


def rmsnorm(x, gain):
    x32 = x.astype(jnp.float32)
    y = x32 * lax.rsqrt(jnp.mean(x32 * x32, axis=-1, keepdims=True) + RMS_EPS)
    return (y * gain.astype(jnp.float32)).astype(x.dtype)

def alibi_slopes(n):
    return (2.0 ** (-8.0 * np.arange(1, n + 1) / n)).astype(np.float32)

def split_cols(proj, widths):
    offs = [0]
    for w in widths:
        offs.append(offs[-1] + w)
    return [proj[..., offs[i]:offs[i + 1]] for i in range(len(widths))]

def banded_attention(q, k, v, slopes, max_back, unit, sinks=None):
    b, s, l, hq, hd = q.shape
    hkv = k.shape[3]
    rep = hq // hkv
    nb = -(-l // BLOCK)
    lp = nb * BLOCK
    pad = [(0, 0), (0, 0), (0, lp - l), (0, 0), (0, 0)]
    qb = jnp.pad(q, pad).reshape(b, s, nb, BLOCK, hkv, rep, hd)
    kb = jnp.pad(k, pad).reshape(b, s, nb, BLOCK, hkv, hd)
    vb = jnp.pad(v, pad).reshape(b, s, nb, BLOCK, hkv, hd)

    def with_prev(z):
        prev = jnp.pad(z[:, :, :-1], [(0, 0), (0, 0), (1, 0), (0, 0), (0, 0), (0, 0)])
        return jnp.concatenate([prev, z], axis=3)

    kk, vv = with_prev(kb), with_prev(vb)
    scores = jnp.einsum('bsnqgrd,bsnkgd->bsngrqk', qb, kk,
                        preferred_element_type=jnp.float32) * (hd ** -0.5)
    a = np.arange(BLOCK)[:, None]
    c = np.arange(2 * BLOCK)[None, :]
    delta = a + BLOCK - c
    band = (delta >= 0) & (delta <= max_back)
    valid = band[None] & ((np.arange(nb)[:, None, None] > 0) | (c >= BLOCK)[None])
    bias = (-slopes.reshape(hkv, rep)[:, :, None, None] * (delta * unit)[None, None]).astype(np.float32)
    scores = jnp.where(valid[None, None, :, None, None], scores + bias, -jnp.inf)
    m = scores.max(axis=-1)
    if sinks is not None:
        sink = sinks.astype(jnp.float32).reshape(hkv, rep)[:, :, None]
        m = jnp.maximum(m, sink)
    p = jnp.exp(scores - m[..., None])
    denom = p.sum(axis=-1)
    if sinks is not None:
        denom = denom + jnp.exp(sink - m)
    out = jnp.einsum('bsngrqk,bsnkgd->bsnqgrd', p, vv.astype(jnp.float32))
    denom_t = jnp.moveaxis(denom, -1, 3)
    out = (out / denom_t[..., None]).reshape(b, s, lp, hq, hd)[:, :, :l]
    lse = (jnp.moveaxis(m, -1, 3) + jnp.log(denom_t)).reshape(b, s, lp, hq)[:, :, :l]
    return out.astype(q.dtype), lse

def dilated_attention(q, k, v):
    b, t = q.shape[:2]
    slopes = alibi_slopes(DIL_HEADS)
    outs, lses = [], []
    for gi, (window, dil) in enumerate(DIL_PATTERNS):
        lo, hi = gi * DIL_HEADS_PER_GROUP, (gi + 1) * DIL_HEADS_PER_GROUP
        l = t // dil

        def to_streams(z):
            return z[:, :, lo:hi].reshape(b, l, dil, DIL_HEADS_PER_GROUP, HEAD_DIM).transpose(0, 2, 1, 3, 4)

        o, lse = banded_attention(to_streams(q), to_streams(k), to_streams(v),
                                  slopes[lo:hi], window // dil, dil)
        outs.append(o.transpose(0, 2, 1, 3, 4).reshape(b, t, DIL_HEADS_PER_GROUP, HEAD_DIM))
        lses.append(lse.transpose(0, 2, 1, 3).reshape(b, t, DIL_HEADS_PER_GROUP))
    alpha = jax.nn.softmax(jnp.stack(lses, axis=2), axis=2)
    y = jnp.einsum('btgh,btghd->bthd', alpha.astype(q.dtype), jnp.stack(outs, axis=2))
    return y.reshape(b, t, DIL_MERGED)

def swa_sink_attention(q, k, v, sinks):
    b, t = q.shape[:2]
    out, _ = banded_attention(q[:, None], k[:, None], v[:, None], alibi_slopes(SWA_Q_HEADS),
                              SWA_WINDOW - 1, 1, sinks=sinks)
    return out[:, 0].reshape(b, t, SWA_Q_WIDTH)

def hier_moe(h, w_group, b_group, w_router, b_router, w_e_gate, w_e_up, w_e_down):
    b, t, d = h.shape
    hf = h.reshape(b * t, d)
    g_logits = (hf @ w_group).astype(jnp.float32) + b_group.astype(jnp.float32)
    g_probs = jax.nn.softmax(g_logits, axis=-1)
    g_top = jnp.argmax(g_logits, axis=-1)
    g_w = jnp.take_along_axis(g_probs, g_top[:, None], axis=1)
    e_logits = ((hf @ w_router).astype(jnp.float32) + b_router.astype(jnp.float32)).reshape(
        -1, MOE_GROUPS, EXPERTS_PER_GROUP)
    e_logits = jnp.take_along_axis(e_logits, g_top[:, None, None], axis=1)[:, 0]
    e_w, e_idx = lax.top_k(jax.nn.softmax(e_logits, axis=-1), TOP_K)
    e_w = e_w / e_w.sum(axis=-1, keepdims=True)
    ids = g_top[:, None] * EXPERTS_PER_GROUP + e_idx
    gates = jnp.einsum('nk,nke->ne', g_w * e_w, jax.nn.one_hot(ids, N_EXPERTS, dtype=jnp.float32))
    out = jnp.zeros_like(hf)
    for e in range(N_EXPERTS):
        a = jax.nn.silu(hf @ w_e_gate[e]) * (hf @ w_e_up[e])
        out = out + gates[:, e:e + 1].astype(hf.dtype) * (a @ w_e_down[e])
    return out.reshape(b, t, d)

def first_inputs(seed: int = 0) -> dict:
    key = jax.random.key(seed)
    ks = jax.random.split(key, 20)
    f32 = jnp.float32

    def nrm(k, shape, fan_in):
        return jax.random.normal(k, shape, f32) * (fan_in ** -0.5)

    return {
        'x': jax.random.normal(ks[0], (BATCH, SEQ, D_MODEL), f32),
        'g_mix': 1.0 + 0.05 * jax.random.normal(ks[1], (DEPTH, D_MODEL), f32),
        'w_in': nrm(ks[2], (DEPTH, D_MODEL, IN_WIDTH), D_MODEL),
        'sinks': jax.random.normal(ks[3], (DEPTH, SWA_Q_HEADS), f32),
        'w_br_dil': nrm(ks[4], (DEPTH, DIL_MERGED, D_MODEL), DIL_MERGED),
        'w_br_swa': nrm(ks[5], (DEPTH, SWA_Q_WIDTH, D_MODEL), SWA_Q_WIDTH),
        'w_out': nrm(ks[6], (DEPTH, D_MODEL, D_MODEL), D_MODEL),
        'g_ffn': 1.0 + 0.05 * jax.random.normal(ks[7], (DEPTH, D_MODEL), f32),
        'w_group': nrm(ks[8], (DEPTH, D_MODEL, MOE_GROUPS), D_MODEL),
        'b_group': 0.01 * jax.random.normal(ks[9], (DEPTH, MOE_GROUPS), f32),
        'w_router': nrm(ks[10], (DEPTH, D_MODEL, N_EXPERTS), D_MODEL),
        'b_router': 0.01 * jax.random.normal(ks[11], (DEPTH, N_EXPERTS), f32),
        'w_e_gate': nrm(ks[12], (DEPTH, N_EXPERTS, D_MODEL, D_EXPERT), D_MODEL),
        'w_e_up': nrm(ks[13], (DEPTH, N_EXPERTS, D_MODEL, D_EXPERT), D_MODEL),
        'w_e_down': nrm(ks[14], (DEPTH, N_EXPERTS, D_EXPERT, D_MODEL), D_EXPERT),
        'g_final': 1.0 + 0.05 * jax.random.normal(ks[15], (D_MODEL,), f32),
    }

def first_block(x, g_mix, w_in, sinks, w_br_dil, w_br_swa, w_out, g_ffn, w_group, b_group,
              w_router, b_router, w_e_gate, w_e_up, w_e_down, g_final):
    b, t, _ = x.shape
    for l in range(DEPTH):
        h = rmsnorm(x, g_mix[l])
        proj = h @ w_in[l]
        q_d, k_d, v_d, q_s, k_s, v_s, gate_d, gate_s = split_cols(proj, IN_WIDTHS)
        y_dil = dilated_attention(q_d.reshape(b, t, DIL_HEADS, HEAD_DIM),
                                  k_d.reshape(b, t, DIL_HEADS, HEAD_DIM),
                                  v_d.reshape(b, t, DIL_HEADS, HEAD_DIM))
        y_swa = swa_sink_attention(q_s.reshape(b, t, SWA_Q_HEADS, HEAD_DIM),
                                   k_s.reshape(b, t, SWA_KV_HEADS, HEAD_DIM),
                                   v_s.reshape(b, t, SWA_KV_HEADS, HEAD_DIM), sinks[l])
        mixed = (jax.nn.sigmoid(gate_d) * (y_dil @ w_br_dil[l])
                 + jax.nn.sigmoid(gate_s) * (y_swa @ w_br_swa[l]))
        x = x + mixed @ w_out[l]
        x = x + hier_moe(rmsnorm(x, g_ffn[l]), w_group[l], b_group[l], w_router[l], b_router[l],
                         w_e_gate[l], w_e_up[l], w_e_down[l])
    return rmsnorm(x, g_final)


DEPTH_2 = 2

N_EVEN = (DEPTH_2 + 1) // 2
N_ODD = DEPTH_2 // 2

POOL_DIM = D_MODEL // 2
POOL_WINDOWS = (2, 4, 8, 16)
N_POOL_GROUPS = len(POOL_WINDOWS)
POOL_GROUP_DIM = POOL_DIM // N_POOL_GROUPS

MLA_HEADS = 8
QK_NOPE_DIM = 64
QK_ROPE_DIM = 32
QK_DIM = QK_NOPE_DIM + QK_ROPE_DIM
V_HEAD_DIM = 64
Q_LORA_RANK = 256
KV_LORA_RANK = 128
ROPE_BASE = 10000.0
Q_BLOCK = 128

EVEN_IN_DIM = POOL_DIM + Q_LORA_RANK + KV_LORA_RANK + QK_ROPE_DIM
EVEN_MIX_DIM = POOL_DIM + MLA_HEADS * V_HEAD_DIM

LRU_WIDTH = D_MODEL
LRU_HEADS = 4
LRU_HEAD_DIM = LRU_WIDTH // LRU_HEADS
CONV_WIDTH = 4
LRU_C = 8.0

MEM_TOKENS = 256
MEM_HEADS = 4
MEM_HEAD_DIM = D_MODEL // MEM_HEADS

D_FF = -(-8 * D_MODEL // (3 * 256)) * 256

NEG_INF = -1e30


def rms_norm(x, g):
    xf = x.astype(jnp.float32)
    y = xf * lax.rsqrt(jnp.mean(xf * xf, axis=-1, keepdims=True) + RMS_EPS)
    return (y * g).astype(x.dtype)

def rope_tables(positions):
    inv_freq = ROPE_BASE ** (-jnp.arange(0, QK_ROPE_DIM, 2, dtype=jnp.float32) / QK_ROPE_DIM)
    ang = positions.astype(jnp.float32)[..., None] * inv_freq
    return jnp.cos(ang), jnp.sin(ang)

def apply_rope(t, cos, sin):
    t1, t2 = jnp.split(t.astype(jnp.float32), 2, axis=-1)
    out = jnp.concatenate([t1 * cos - t2 * sin, t2 * cos + t1 * sin], axis=-1)
    return out.astype(t.dtype)

def pool_mixer(u, pool_w, pool_scale):
    B, S, _ = u.shape
    ug = u.reshape(B, S, N_POOL_GROUPS, POOL_GROUP_DIM)
    uf = ug.astype(jnp.float32)
    csum = jnp.concatenate([jnp.zeros((B, 1, N_POOL_GROUPS, POOL_GROUP_DIM), jnp.float32),
                            jnp.cumsum(uf, axis=1)], axis=1)
    t = jnp.arange(S)
    means = []
    for g, w in enumerate(POOL_WINDOWS):
        lo = jnp.maximum(t + 1 - w, 0)
        win_sum = csum[:, 1:, g] - csum[:, lo, g]
        cnt = jnp.minimum(t + 1, w).astype(jnp.float32)
        means.append(win_sum / cnt[None, :, None])
    pooled = (jnp.stack(means, axis=2) - uf).astype(u.dtype)
    y = jnp.einsum('bsgc,gcd->bsgd', pooled, pool_w).reshape(B, S, POOL_DIM)
    return y * pool_scale.astype(y.dtype)

def mla_causal_attention(q_nope, q_rope, k_nope, k_rope, v):
    B, S, H, _ = q_nope.shape
    nb = S // Q_BLOCK
    qn = q_nope.reshape(B, nb, Q_BLOCK, H, QK_NOPE_DIM).transpose(1, 0, 2, 3, 4)
    qr = q_rope.reshape(B, nb, Q_BLOCK, H, QK_ROPE_DIM).transpose(1, 0, 2, 3, 4)
    starts = jnp.arange(nb, dtype=jnp.int32) * Q_BLOCK
    kpos = jnp.arange(S, dtype=jnp.int32)
    scale = QK_DIM ** -0.5

    def one_block(args):
        qn_b, qr_b, start = args
        s = (jnp.einsum('bqhd,bkhd->bhqk', qn_b, k_nope).astype(jnp.float32)
             + jnp.einsum('bqhr,bkr->bhqk', qr_b, k_rope).astype(jnp.float32)) * scale
        qpos = start + jnp.arange(Q_BLOCK, dtype=jnp.int32)
        mask = kpos[None, :] <= qpos[:, None]
        s = jnp.where(mask[None, None], s, NEG_INF)
        p = jax.nn.softmax(s, axis=-1).astype(v.dtype)
        return jnp.einsum('bhqk,bkhd->bqhd', p, v)

    out = lax.map(one_block, (qn, qr, starts))
    return out.transpose(1, 0, 2, 3, 4).reshape(B, S, H * V_HEAD_DIM)

def even_mixer(h, cos, sin, w_in, pool_w, pool_scale, q_norm, w_q_up, kv_norm, w_kv_up, w_out):
    B, S, _ = h.shape
    z = h @ w_in
    u, cq, ckv, kr = jnp.split(z, [POOL_DIM, POOL_DIM + Q_LORA_RANK,
                                   POOL_DIM + Q_LORA_RANK + KV_LORA_RANK], axis=-1)
    y_pool = pool_mixer(u, pool_w, pool_scale)
    q = (rms_norm(cq, q_norm) @ w_q_up).reshape(B, S, MLA_HEADS, QK_DIM)
    q_nope, q_rope = jnp.split(q, [QK_NOPE_DIM], axis=-1)
    kv = (rms_norm(ckv, kv_norm) @ w_kv_up).reshape(B, S, MLA_HEADS, QK_NOPE_DIM + V_HEAD_DIM)
    k_nope, v = jnp.split(kv, [QK_NOPE_DIM], axis=-1)
    q_rope = apply_rope(q_rope, cos[:, :, None, :], sin[:, :, None, :])
    k_rope = apply_rope(kr, cos, sin)
    y_att = mla_causal_attention(q_nope, q_rope, k_nope, k_rope, v)
    return jnp.concatenate([y_pool, y_att], axis=-1) @ w_out

def causal_depthwise_conv(xb, conv_w, conv_b):
    y = lax.conv_general_dilated(xb, conv_w[:, None, :].astype(xb.dtype), window_strides=(1,),
                                 padding=((CONV_WIDTH - 1, 0),),
                                 dimension_numbers=('NWC', 'WIO', 'NWC'),
                                 feature_group_count=xb.shape[-1])
    return y + conv_b.astype(y.dtype)

def linear_scan_combine(c1, c2):
    a1, b1 = c1
    a2, b2 = c2
    return a1 * a2, a2 * b1 + b2

def odd_mixer(h, reset, w_in, conv_w, conv_b, w_rgate, b_rgate, w_igate, b_igate, lam, w_out):
    B, S, _ = h.shape
    z = h @ w_in
    gate_branch, xb = jnp.split(z, [LRU_WIDTH], axis=-1)
    xb = causal_depthwise_conv(xb, conv_w, conv_b)
    xg = xb.reshape(B, S, LRU_HEADS, LRU_HEAD_DIM)
    r = jax.nn.sigmoid(jnp.einsum('bshc,hcd->bshd', xg, w_rgate).reshape(B, S, LRU_WIDTH) + b_rgate)
    i = jax.nn.sigmoid(jnp.einsum('bshc,hcd->bshd', xg, w_igate).reshape(B, S, LRU_WIDTH) + b_igate)
    log_a = -LRU_C * r.astype(jnp.float32) * jax.nn.softplus(-lam.astype(jnp.float32))
    a = jnp.exp(log_a)
    mult = jnp.sqrt(jnp.maximum(-jnp.expm1(2.0 * log_a), 0.0))
    a = jnp.where(reset, 0.0, a)
    mult = jnp.where(reset, 1.0, mult)
    b = mult * (i * xb).astype(jnp.float32)
    _, hseq = lax.associative_scan(linear_scan_combine, (a, b), axis=1)
    y = jax.nn.gelu(gate_branch) * hseq.astype(h.dtype)
    return y @ w_out

def mem_cross_attention(h, mem, norm_mem, w_q, w_kv, w_o):
    B, S, _ = h.shape
    m = rms_norm(mem, norm_mem)
    q = (h @ w_q).reshape(B, S, MEM_HEADS, MEM_HEAD_DIM)
    k, v = jnp.split(m @ w_kv, 2, axis=-1)
    k = k.reshape(B, -1, MEM_HEADS, MEM_HEAD_DIM)
    v = v.reshape(B, -1, MEM_HEADS, MEM_HEAD_DIM)
    s = jnp.einsum('bqhd,bkhd->bhqk', q, k).astype(jnp.float32) * (MEM_HEAD_DIM ** -0.5)
    p = jax.nn.softmax(s, axis=-1).astype(v.dtype)
    o = jnp.einsum('bhqk,bkhd->bqhd', p, v).reshape(B, S, D_MODEL)
    return o @ w_o

def swiglu(h, w_gate_up, w_down):
    g, u = jnp.split(h @ w_gate_up, 2, axis=-1)
    return (jax.nn.silu(g) * u) @ w_down

def second_inputs(seed: int = 0) -> dict:
    key = jax.random.key(seed)
    ks = iter(jax.random.split(key, 48))
    f32 = jnp.float32

    def w(shape, fan_in):
        return jax.random.normal(next(ks), shape, f32) * fan_in ** -0.5

    def gain(shape):
        return 1.0 + 0.02 * jax.random.normal(next(ks), shape, f32)

    def bias(shape):
        return 0.02 * jax.random.normal(next(ks), shape, f32)

    E, O, L = N_EVEN, N_ODD, DEPTH_2
    x = jax.random.normal(next(ks), (BATCH, SEQ, D_MODEL), f32)
    mem = jax.random.normal(next(ks), (BATCH, MEM_TOKENS, D_MODEL), f32)
    positions = jnp.broadcast_to(jnp.arange(SEQ, dtype=jnp.int32), (BATCH, SEQ))
    a_c = jax.random.uniform(next(ks), (O, LRU_WIDTH), f32, 0.9, 0.999)
    s_l = a_c ** (1.0 / LRU_C)
    lam = jnp.log(s_l) - jnp.log1p(-s_l)
    return {
        "x": x,
        "mem": mem,
        "positions": positions,
        "ev_norm": gain((E, D_MODEL)),
        "ev_w_in": w((E, D_MODEL, EVEN_IN_DIM), D_MODEL),
        "ev_pool_w": w((E, N_POOL_GROUPS, POOL_GROUP_DIM, POOL_GROUP_DIM), POOL_GROUP_DIM),
        "ev_pool_scale": gain((E, POOL_DIM)),
        "ev_q_norm": gain((E, Q_LORA_RANK)),
        "ev_w_q_up": w((E, Q_LORA_RANK, MLA_HEADS * QK_DIM), Q_LORA_RANK),
        "ev_kv_norm": gain((E, KV_LORA_RANK)),
        "ev_w_kv_up": w((E, KV_LORA_RANK, MLA_HEADS * (QK_NOPE_DIM + V_HEAD_DIM)), KV_LORA_RANK),
        "ev_w_out": w((E, EVEN_MIX_DIM, D_MODEL), EVEN_MIX_DIM),
        "od_norm": gain((O, D_MODEL)),
        "od_w_in": w((O, D_MODEL, 2 * LRU_WIDTH), D_MODEL),
        "od_conv_w": w((O, CONV_WIDTH, LRU_WIDTH), CONV_WIDTH),
        "od_conv_b": bias((O, LRU_WIDTH)),
        "od_w_rgate": w((O, LRU_HEADS, LRU_HEAD_DIM, LRU_HEAD_DIM), LRU_HEAD_DIM),
        "od_b_rgate": bias((O, LRU_WIDTH)),
        "od_w_igate": w((O, LRU_HEADS, LRU_HEAD_DIM, LRU_HEAD_DIM), LRU_HEAD_DIM),
        "od_b_igate": bias((O, LRU_WIDTH)),
        "od_lambda": lam,
        "od_w_out": w((O, LRU_WIDTH, D_MODEL), LRU_WIDTH),
        "xa_norm_x": gain((L, D_MODEL)),
        "xa_norm_mem": gain((L, D_MODEL)),
        "xa_w_q": w((L, D_MODEL, D_MODEL), D_MODEL),
        "xa_w_kv": w((L, D_MODEL, 2 * D_MODEL), D_MODEL),
        "xa_w_o": w((L, D_MODEL, D_MODEL), D_MODEL),
        "ffn_norm": gain((L, D_MODEL)),
        "ffn_w_gate_up": w((L, D_MODEL, 2 * D_FF), D_MODEL),
        "ffn_w_down": w((L, D_FF, D_MODEL), D_FF),
        "final_norm": gain((D_MODEL,)),
    }

def second_block(x, mem, positions,
              ev_norm, ev_w_in, ev_pool_w, ev_pool_scale, ev_q_norm, ev_w_q_up,
              ev_kv_norm, ev_w_kv_up, ev_w_out,
              od_norm, od_w_in, od_conv_w, od_conv_b, od_w_rgate, od_b_rgate,
              od_w_igate, od_b_igate, od_lambda, od_w_out,
              xa_norm_x, xa_norm_mem, xa_w_q, xa_w_kv, xa_w_o,
              ffn_norm, ffn_w_gate_up, ffn_w_down, final_norm):
    cos, sin = rope_tables(positions)
    reset = (positions == 0)[..., None]
    for layer in range(DEPTH_2):
        j = layer // 2
        if layer % 2 == 0:
            h = rms_norm(x, ev_norm[j])
            x = x + even_mixer(h, cos, sin, ev_w_in[j], ev_pool_w[j], ev_pool_scale[j],
                               ev_q_norm[j], ev_w_q_up[j], ev_kv_norm[j], ev_w_kv_up[j],
                               ev_w_out[j])
        else:
            h = rms_norm(x, od_norm[j])
            x = x + odd_mixer(h, reset, od_w_in[j], od_conv_w[j], od_conv_b[j],
                              od_w_rgate[j], od_b_rgate[j], od_w_igate[j], od_b_igate[j],
                              od_lambda[j], od_w_out[j])
        x = x + mem_cross_attention(rms_norm(x, xa_norm_x[layer]), mem, xa_norm_mem[layer],
                                    xa_w_q[layer], xa_w_kv[layer], xa_w_o[layer])
        x = x + swiglu(rms_norm(x, ffn_norm[layer]), ffn_w_gate_up[layer], ffn_w_down[layer])
    return rms_norm(x, final_norm)


def setup_inputs(seed=0):
    out = dict(first_inputs(seed))
    for name, value in second_inputs(seed + 1).items():
        if name != "x":
            out[name + "_2"] = value
    return out


def reference(
    x, g_mix, w_in, sinks, w_br_dil, w_br_swa, w_out, g_ffn, w_group, b_group, w_router,
    b_router, w_e_gate, w_e_up, w_e_down, g_final, mem_2, positions_2, ev_norm_2, ev_w_in_2,
    ev_pool_w_2, ev_pool_scale_2, ev_q_norm_2, ev_w_q_up_2, ev_kv_norm_2, ev_w_kv_up_2,
    ev_w_out_2, od_norm_2, od_w_in_2, od_conv_w_2, od_conv_b_2, od_w_rgate_2, od_b_rgate_2,
    od_w_igate_2, od_b_igate_2, od_lambda_2, od_w_out_2, xa_norm_x_2, xa_norm_mem_2, xa_w_q_2,
    xa_w_kv_2, xa_w_o_2, ffn_norm_2, ffn_w_gate_up_2, ffn_w_down_2, final_norm_2,
):
    x = first_block(
        x, g_mix, w_in, sinks, w_br_dil, w_br_swa, w_out, g_ffn, w_group, b_group, w_router,
        b_router, w_e_gate, w_e_up, w_e_down, g_final,
    )
    return second_block(
        x, mem_2, positions_2, ev_norm_2, ev_w_in_2, ev_pool_w_2, ev_pool_scale_2, ev_q_norm_2,
        ev_w_q_up_2, ev_kv_norm_2, ev_w_kv_up_2, ev_w_out_2, od_norm_2, od_w_in_2, od_conv_w_2,
        od_conv_b_2, od_w_rgate_2, od_b_rgate_2, od_w_igate_2, od_b_igate_2, od_lambda_2,
        od_w_out_2, xa_norm_x_2, xa_norm_mem_2, xa_w_q_2, xa_w_kv_2, xa_w_o_2, ffn_norm_2,
        ffn_w_gate_up_2, ffn_w_down_2, final_norm_2,
    )


_drawn_inputs = setup_inputs


def setup_inputs(seed=0):
    import zlib

    import numpy as np

    out = dict(_drawn_inputs(seed))
    spreads = {}
    factors = {'b_group': 5.099,
     'b_router': 3.162,
     'ev_norm_2': 4.15,
     'ev_pool_scale_2': 4.615,
     'ev_q_norm_2': 8.0,
     'ev_kv_norm_2': 8.0,
     'od_norm_2': 6.097,
     'od_b_rgate_2': 8.0,
     'od_b_igate_2': 8.0,
     'xa_norm_x_2': 8.0,
     'xa_norm_mem_2': 8.0,
     'ffn_norm_2': 3.079,
     'final_norm_2': 2.782}
    for name, (base, spread) in spreads.items():
        noise = np.random.default_rng([zlib.crc32(name.encode()), seed]).standard_normal(out[name].shape)
        drawn = base * np.exp(spread * noise) if base else spread * noise
        out[name] = __import__('jax').numpy.asarray(drawn.astype(out[name].dtype))
    for name, factor in factors.items():
        out[name] = (out[name] * factor).astype(out[name].dtype)
    return out
```

```python
from contextlib import ExitStack

import numpy as np

import concourse.bass as bass
from concourse import mybir

F32 = mybir.dt.float32
F32R = mybir.dt.float32r
I32 = mybir.dt.int32
ALU = mybir.AluOpType
ACT = mybir.ActivationFunctionType
AX = mybir.AxisListType

P = 128
T = 256
D = 1024
DC = D // P
HD = 64
GROUPS = ((128, 1), (512, 4), (2048, 16))
DIL_HEADS = 8
SWA_HEADS = 16
SWA_WINDOW = 128
N_EXP, N_GRP, D_EXP = 32, 4, 512
D_FF = 2816
MLA_H, NOPE, ROPE, QK = 8, 64, 32, 96
XA_H, XA_HD = 4, 256
EPS = 1e-6
LRU_C = 8.0
FAR = -1e30

RAW = 6
HL = 3
UNIT = 2048

VECS = {}
_at = 0
for _n, _c in (("g_mix", 8), ("g_ffn", 8), ("g_final", 8), ("ev_norm", 8), ("pool_scale", 4), ("q_norm", 2),
               ("kv_norm", 1), ("od_norm", 8), ("conv_w", 32), ("conv_b", 8), ("b_r", 8), ("b_i", 8), ("lam", 8),
               ("xa_x0", 8), ("xa_x1", 8), ("xa_m0", 8), ("xa_m1", 8), ("ffn0", 8), ("ffn1", 8), ("final", 8)):
    VECS[_n] = (_at, _c)
    _at += _c
NV = _at


def shape_constants():
    q = np.arange(P)[:, None]
    c = np.arange(T)[None, :]
    back = (q + P - c).astype(np.float32)
    pats = []
    for window, dil in GROUPS:
        ok = (back >= 0) & (back <= (window // dil) * dil) & (back % dil == 0)
        pats.append(np.where(ok, back, 1e30))
    pats.append(np.where((back >= 0) & (back <= SWA_WINDOW - 1), back, 1e30))
    first = np.concatenate([*pats, np.eye(P),
                            np.broadcast_to(np.arange(N_GRP, 0, -1), (P, N_GRP)),
                            np.broadcast_to(np.arange(N_EXP, 0, -1), (P, N_EXP))], 1).astype(np.float32)
    causal = np.where(back >= 0, 0.0, FAR)
    swap = np.zeros((P, QK))
    for m in range(NOPE, QK):
        swap[m + 16 if m < NOPE + 16 else m - 16, m] = 1
    put = np.zeros((P, 2, QK))
    for r in range(ROPE):
        put[r, 0, NOPE + r] = 1
        put[(r + 16) % ROPE, 1, NOPE + r] = 1
    freq = np.zeros((P, 2))
    inv = np.float32(10000.0) ** (-np.arange(0, ROPE, 2, dtype=np.float32) / np.float32(ROPE))
    freq[NOPE:QK, 0] = np.concatenate([inv, inv])
    freq[NOPE:QK, 1] = np.repeat([-1.0, 1.0], 16)
    cnt = np.stack([1.0 / np.minimum(np.arange(T) + 1, w) for w in (2, 4, 8, 16)]).astype(np.float32)
    second = np.concatenate([causal, swap, put.reshape(P, -1), freq,
                             np.broadcast_to(cnt.reshape(1, -1), (P, 4 * T))], 1).astype(np.float32)
    return first, second


def slopes(n):
    return (2.0 ** (-8.0 * np.arange(1, n + 1) / n)).astype(np.float32)


def build(nc, t, out):
    with ExitStack() as ctx:
        def sb(name, shape, dt=F32):
            return ctx.enter_context(nc.sbuf_tensor(name, shape, dt))

        def sem(name):
            return ctx.enter_context(nc.semaphore(name))

        raw = [sb(f"raw{i}", [P, UNIT]) for i in range(RAW)]
        whi = [sb(f"whi{i}", [P, UNIT], F32R) for i in range(HL)]
        wlo = [sb(f"wlo{i}", [P, UNIT], F32R) for i in range(HL)]
        xh = sb("xh", [P, DC, T], F32R)
        xl = sb("xl", [P, DC, T], F32R)
        ah = sb("ah", [P, 4, T], F32R)
        al = sb("al", [P, 4, T], F32R)
        x = sb("x", [P, DC, T])
        arena = sb("arena", [P, 62 * T])
        scr = sb("scr", [P, 9 * T])
        c1 = sb("c1", [P, 1024 + P + N_GRP + N_EXP])
        vec = sb("vec", [P, NV])
        rows = sb("rows", [P, SWA_HEADS + N_GRP + N_EXP])
        ones = sb("ones", [P, P])
        rstd = sb("rstd", [P, T])
        sm = sb("sm", [P, 2, 24])
        ps = ctx.enter_context(nc.psum_tensor("ps", [P, 8, 512], F32))

        pat = c1[:, 0:1024].rearrange("p (g k) -> p g k", g=4)
        ident = c1[:, 1024:1152]
        gkey = c1[:, 1152:1156]
        ekey = c1[:, 1156:1188]
        sink_row = rows[:, 0:16]
        bias_row = rows[:, 16:52]

        def vcol(name, c):
            a = VECS[name][0] + c
            return vec[:, a:a + 1]

        def area(at, *shape):
            n = int(np.prod(shape))
            v = arena[:, at:at + n]
            if len(shape) == 2:
                v = v.rearrange("p (a b) -> p a b", a=shape[0])
            elif len(shape) == 3:
                v = v.rearrange("p (a b c) -> p a b c", a=shape[0], b=shape[1])
            return v

        def chunks(at, n):
            return area(at, n, T)

        qd, kd = chunks(0, 12), chunks(12 * T, 12)
        vd = area(24 * T, 2, 1536)
        qs = chunks(36 * T, 8)
        ks, vs = chunks(44 * T, 1), area(45 * T, 2, P)
        sg = chunks(46 * T, 16)
        gb = area(8 * T, N_EXP, T)
        lg = area(40 * T, 2, 36)
        gt = area(41 * T, T)
        rt = area(42 * T, 2, T)
        gates = rt[:, :, 192:224]
        mem = chunks(0, 8)
        c2 = area(44 * T, T + QK + 2 * QK + 2 + 4 * T)
        causal = c2[:, 0:T]
        swap = c2[:, T:T + QK]
        put = c2[:, T + QK:T + 3 * QK].rearrange("p (a b) -> p a b", a=2)
        freq = c2[:, T + 3 * QK:T + 3 * QK + 2]
        icnt = c2[:, T + 3 * QK + 2:].rearrange("p (g t) -> p g t", g=4)
        posi, posf = area(52 * T, T), area(53 * T, T)

        raw_landed = [sem(f"raw_landed{i}") for i in range(RAW)]
        hi_ready, lo_ready, unit_used = sem("hi_ready"), sem("lo_ready"), sem("unit_used")
        lin_evac = [sem("lin_evac0"), sem("lin_evac1")]
        consts_landed, x_landed, second_landed, out_landed = (sem("consts_landed"), sem("x_landed"),
                                                              sem("second_landed"), sem("out_landed"))
        ones_set = sem("ones_set")
        sq_ready, ss_ready, ms_ready, rstd_ready = sem("sq_ready"), sem("ss_ready"), sem("ms_ready"), sem("rstd_ready")
        h_ready, xh_ready, xl_ready = sem("h_ready"), sem("xh_ready"), sem("xl_ready")
        dve_step = sem("dve_step")
        silu_done, hid_scaled, hid_ready, ah_ready, al_ready = (sem("silu_done"), sem("hid_scaled"), sem("hid_ready"),
                                                                sem("ah_ready"), sem("al_ready"))
        att_scored, att_biased, att_max, att_exp, att_probs = (sem("att_scored"), sem("att_biased"), sem("att_max"),
                                                               sem("att_exp"), sem("att_probs"))
        att_turned, att_pt, att_mixed, att_out = sem("att_turned"), sem("att_pt"), sem("att_mixed"), sem("att_out")
        (kswap_mm, kswap_there, moe_starts, route_grp, route_grp_exp, route_two, route_two_exp, gates_there, gates_mm,
         gt_there, row_mm, rows_act, rows_dve, pool_out, kr_there, kr_mm, kr_turned, mq_there, mq_mm, mq_turned,
         angles, trig, kv_out, lru_ab, lru_r, lru_i, lam_abs, lam_exp, lam_scale, lru_t, lru_t_max, lru_root,
         lru_gelu, result) = [sem(n) for n in (
             "kswap_mm kswap_there moe_starts route_grp route_grp_exp route_two route_two_exp gates_there gates_mm "
             "gt_there row_mm rows_act rows_dve pool_out kr_there kr_mm kr_turned mq_there mq_mm mq_turned "
             "angles trig kv_out lru_ab lru_r lru_i lam_abs lam_exp lam_scale lru_t lru_t_max lru_root "
             "lru_gelu result").split()]

        units = []

        def kview(w):
            return w.rearrange("(k p) n -> p k n", p=P)

        def cut(w, kc, step, n=None):
            v = kview(w)
            n = n or w.shape[-1]
            first = len(units)
            for a in range(0, n, step):
                b = min(a + step, n)
                units.append((v[:, :, a:b], kc, b - a))
            return range(first, len(units))

        u_in = cut(t["w_in"][0], DC, 256)
        u_br = []
        wd_, ws_ = kview(t["w_br_dil"][0]), kview(t["w_br_swa"][0])
        for a in range(0, D, 256):
            u_br.append(len(units))
            units.append((wd_[:, :, a:a + 256], 4, 256))
            units.append((ws_[:, :, a:a + 256], 8, 256))
        u_out = cut(t["w_out"][0], DC, 256)
        u_router = len(units)
        units.append((t["w_route"].rearrange("p (k n) -> p k n", k=DC), DC, 36))
        moe = (len(units), 2 * N_EXP)
        for j in range(3 * 2 * N_EXP):
            units.append(None)

        def second_attention(l):
            um = cut(t["xa_w_kv_2"][l], DC, 256)
            uq = cut(t["xa_w_q_2"][l], DC, 256)
            uo = cut(t["xa_w_o_2"][l], DC, 256)
            return um, uq, uo

        def gated_ffn(l):
            at = (len(units), D_FF // 256)
            for j in range(3 * (D_FF // 256)):
                units.append(None)
            return at

        u_ev = cut(t["ev_w_in_2"][0], DC, 256)
        u_pool = len(units)
        units.append((t["ev_pool_w_2"][0].rearrange("g p n -> p g n"), 4, P))
        u_qup = len(units)
        units.append((kview(t["ev_w_q_up_2"][0]), 2, 768))
        u_kvup = len(units)
        units.append((kview(t["ev_w_kv_up_2"][0]), 1, 1024))
        u_evo = cut(t["ev_w_out_2"][0], DC, 256)
        u_xa = [second_attention(0)]
        ffn = [gated_ffn(0)]
        u_od = cut(t["od_w_in_2"][0], DC, 256)
        u_rg = len(units)
        for w in ("od_w_rgate_2", "od_w_igate_2"):
            units.append((t[w][0].rearrange("h (k p) n -> p (h k) n", p=P), DC, 256))
        u_odo = cut(t["od_w_out_2"][0], DC, 256)
        u_xa.append(second_attention(1))
        ffn.append(gated_ffn(1))

        trio0 = [0, moe[1], moe[1] + ffn[0][1]]

        def wview(buf, u, kc, n):
            return buf[u % HL][:, 0:kc * n].rearrange("p (k n) -> p k n", k=kc)

        def usize(u):
            return units[u][1] * units[u][2] if units[u] else UNIT

        def score_bank(step, g):
            at = g * T if len(step["scores"]) == 3 else g * 512
            return ps[:, at // 512, at % 512:at % 512 + step["nk"]]

        def attention(kind, l=0):
            steps = []
            if kind == "dil":
                sl = slopes(24)
                for hh in range(DIL_HEADS):
                    lo = HD * (hh % 2)
                    for qt in range(2):
                        nk = P * (qt + 1)
                        sc, bi, pv = [], [], []
                        for g in range(3):
                            c = 4 * g + hh // 2
                            sc.append([(qd[lo:lo + HD, c, qt * P:qt * P + P], kd[lo:lo + HD, c, 0:nk])])
                            bi.append((g, float(sl[8 * g + hh]) * 8.0))
                            for kt in range(qt + 1):
                                pv.append((vd[:, kt, (8 * g + hh) * HD:(8 * g + hh + 1) * HD], g, kt))
                        steps.append(dict(nk=nk, qt=qt, scores=sc, bias=bi, merged=True, sink=None, scale=0.125,
                                          pv=[(lo, 0, pv)], last=hh % 2 == 1 and qt == 1,
                                          y=[qd[:, hh // 2, :]]))
            elif kind == "swa":
                sl = slopes(SWA_HEADS)
                for c in range(8):
                    for qt in range(2):
                        nk = P * (qt + 1)
                        sc, bi, pv = [], [], []
                        for i in range(2):
                            h = 2 * c + i
                            kv = h // 8
                            kk = ks[:, 0, :] if kv == i else kswap[:, 0, :]
                            sc.append([(qs[HD * i:HD * i + HD, c, qt * P:qt * P + P], kk[HD * i:HD * i + HD, 0:nk])])
                            bi.append((3, float(sl[h]) * 8.0))
                            pv.append((HD * i, 0, [(vs[:, kt, kv * HD:(kv + 1) * HD], i, kt) for kt in range(qt + 1)]))
                        steps.append(dict(nk=nk, qt=qt, scores=sc, bias=bi, merged=False, sink=2 * c, scale=0.125,
                                          pv=pv, last=qt == 1, y=[qs[:, c, :]]))
            elif kind == "mla":
                for c in range(4):
                    for qt in range(2):
                        nk = P * (qt + 1)
                        sc, pv = [], []
                        for i in range(2):
                            h = 2 * c + i
                            sc.append([(mq[0:QK, h, qt * P:qt * P + P], mk[0:QK, h, 0:nk])])
                            pv.append((HD * i, 0, [(mv[:, kt, h * HD:(h + 1) * HD], i, kt) for kt in range(qt + 1)]))
                        steps.append(dict(nk=nk, qt=qt, scores=sc, bias="causal", merged=False, sink=None,
                                          scale=float(QK) ** -0.5, pv=pv, last=qt == 1, y=[my[:, c, :]]))
            else:
                for h in range(XA_H):
                    for qt in range(2):
                        sc = [[(xq[:, 2 * h + k, qt * P:qt * P + P], xk[:, 2 * h + k, :]) for k in range(2)]]
                        pv = [(0, k, [(xv[:, kt, (2 * h + k) * P:(2 * h + k + 1) * P], 0, kt) for kt in range(2)])
                              for k in range(2)]
                        steps.append(dict(nk=T, qt=qt, scores=sc, bias=None, merged=False, sink=None,
                                          scale=float(XA_HD) ** -0.5, pv=pv, last=qt == 1,
                                          y=[xq[:, 2 * h, :], xq[:, 2 * h + 1, :]]))
            return steps

        lat = chunks(25 * T, 3)
        kr = area(28 * T, T)
        cosr, sinr = area(29 * T, T), area(30 * T, T)
        pooled = [area(8 * T + 1088 * b, 4, 16 + T) for b in range(3)]
        ypool = chunks(21 * T, 4)
        mk, mv = chunks(8 * T, 8), area(16 * T, 2, 512)
        mq, my = chunks(31 * T, 8), chunks(39 * T, 4)
        xq, xk, xv = chunks(8 * T, 8), chunks(16 * T, 8), area(24 * T, 2, 1024)
        lgate, lxb, lxc = chunks(8 * T, 8), area(16 * T, 8, T + 4), chunks(25 * T, 8)
        lr, li, lrc = chunks(33 * T, 8), chunks(41 * T, 8), chunks(54 * T, 8)
        reset, lsm = area(49 * T, T), area(50 * T, 10, 8)
        kswap = rstd[:, :].rearrange("p (a b) -> p a b", a=1)
        S = [scr[:, b * 768:(b + 1) * 768].rearrange("p (g k) -> p g k", g=3) for b in range(2)]
        PT = scr[:, 1536:2304].rearrange("p (b q) -> p b q", q=P)
        hbuf = scr[:, 0:2048].rearrange("p (c t) -> p c t", c=8)
        sil = [scr[:, 0:512], scr[:, 512:1024]]
        hid = [scr[:, 1024:1536], scr[:, 1536:2048]]
        ang = hbuf[:, 0:6, :]

        steps_a = attention("dil") + attention("swa")
        steps_m = attention("mla")
        steps_x = attention("xa")

        block = ctx.enter_context(nc.Block())

        @block.sync
        def _(sp):
            sp.dma_start(x[:], kview(t["xT"])).then_inc(x_landed, 16)
            sp.dma_start(vec[:], t["vecs"]).then_inc(consts_landed, 16)

            def load(u, src, base=None, i=None):
                if i is not None:
                    sp.wait_ge(lo_ready, i * 6 + (u - RAW + 1))
                elif u >= RAW:
                    sp.wait_ge(lo_ready, u - RAW + 1)
                kc, n = src.shape[1], src.shape[2]
                sp.dma_start(raw[u % RAW][:, 0:kc * n].rearrange("p (k n) -> p k n", k=kc),
                             src).then_inc(raw_landed[u % RAW], 16)

            def load_gated(p0, n, g, uu, d):
                load(p0, g(0, 0))
                load(p0 + 1, uu(0, 0))
                with sp.Fori(0, (n - 1) // 2) as i:
                    load(p0 + 2, g(i, 1), i=i)
                    load(p0 + 3, uu(i, 1), i=i)
                    load(p0 + 4, d(i, 0), i=i)
                    load(p0 + 5, g(i, 2), i=i)
                    load(p0 + 6, uu(i, 2), i=i)
                    load(p0 + 7, d(i, 1), i=i)
                if n % 2 == 0:
                    load(p0 + 3 * n - 4, g(n // 2 - 1, 1))
                    load(p0 + 3 * n - 3, uu(n // 2 - 1, 1))
                    load(p0 + 3 * n - 2, d(n // 2 - 1, 0))
                    load(p0 + 3 * n - 1, d(n // 2 - 1, 1))
                else:
                    load(p0 + 3 * n - 1, d(n // 2, 0))

            wg = t["w_e_gate"][0].rearrange("e (k p) n -> e p k n", p=P)
            wu = t["w_e_up"][0].rearrange("e (k p) n -> e p k n", p=P)
            wdn = t["w_e_down"][0].rearrange("e (h k p) n -> (e h) p k n", p=P, h=2)

            def expert_cols(w):
                return lambda i, c: w[i + c // 2][:, :, (c % 2) * 256:(c % 2) * 256 + 256]

            def expert_rows(i, c):
                return wdn[i * 2 + c]

            def ffn_cols(l, half):
                w = t["ffn_w_gate_up_2"][l][:, half * D_FF:(half + 1) * D_FF]
                first = kview(w[:, 0:256])
                rest = w[:, 256:].rearrange("(k p) (j b n) -> b j p k n", p=P, b=2, n=256)
                return lambda i, c: rest[c - 1][i] if c else first

            def ffn_rows(l):
                w = t["ffn_w_down_2"][l]
                pairs = w[0:D_FF - 256].rearrange("(j b k p) n -> b j p k n", p=P, k=2, b=2)
                last = kview(w[D_FF - 256:])
                return lambda i, c: last if isinstance(i, int) else pairs[c][i]

            u = 0
            while u < len(units):
                if u == moe[0]:
                    load_gated(u, moe[1], expert_cols(wg), expert_cols(wu), expert_rows)
                    u += 3 * moe[1]
                elif u in (ffn[0][0], ffn[1][0]):
                    l = 0 if u == ffn[0][0] else 1
                    load_gated(u, ffn[l][1], ffn_cols(l, 0), ffn_cols(l, 1), ffn_rows(l))
                    u += 3 * ffn[l][1]
                else:
                    load(u, units[u][0])
                    u += 1
                if u == RAW:
                    sp.dma_start(c1[:], t["const1"]).then_inc(consts_landed, 16)
                    sp.dma_start(rows[:, 0:16], t["sinks"].partition_broadcast(P)).then_inc(consts_landed, 16)
                    sp.dma_start(rows[:, 16:52], t["b_route"].partition_broadcast(P)).then_inc(consts_landed, 16)
            sp.wait_ge(result, 1)
            sp.dma_start(out.rearrange("(c p) t -> p c t", p=P), hbuf).then_inc(out_landed, 16)
            sp.wait_ge(out_landed, 16)

        @block.tensor
        def _(pe):
            st = dict(lin=0, norm=0, step=0, xl=0, y=0)

            def weights_in(u, i=None):
                add = 0 if i is None else i * 6
                pe.wait_ge(hi_ready, add + u + 1)
                pe.wait_ge(lo_ready, add + u + 1)

            def triple(o, parts, first=True, last=True, group=True):
                mm = None
                for a, (wh, wl, h, l) in enumerate(parts):
                    mm = nc.tensor.matmul(o, wh, h, start=first and a == 0, stop=False, skip_group_check=not group)
                    nc.tensor.matmul(o, wh, l, start=False, stop=False, skip_group_check=not group)
                    mm = nc.tensor.matmul(o, wl, h, start=False, stop=last and a == len(parts) - 1,
                                          skip_group_check=not group)
                return mm

            def lin_bank():
                m = st["lin"]
                st["lin"] += 1
                if m >= 2:
                    pe.wait_ge(lin_evac[m % 2], m // 2)
                return ps[:, 6 + m % 2, :].rearrange("p (c t) -> p c t", c=2)

            def feature_unit(u, hsrc=None, lsrc=None, k0=0):
                hsrc, lsrc = hsrc or xh, lsrc or xl
                _, kc, n = units[u]
                weights_in(u)
                o = lin_bank()
                wh, wl = wview(whi, u, kc, n), wview(wlo, u, kc, n)
                for b in range(-(-n // P)):
                    w = min(P, n - b * P)
                    mm = triple(o[0:w, b, :], [(wh[:, k, b * P:b * P + w], wl[:, k, b * P:b * P + w],
                                                hsrc[:, k0 + k, :], lsrc[:, k0 + k, :]) for k in range(kc)])
                mm.then_inc(unit_used, 1)

            def token_unit(u, a=0, n=None):
                _, kc, full = units[u]
                n = n or full
                weights_in(u)
                o = lin_bank()
                wh, wl = wview(whi, u, kc, full), wview(wlo, u, kc, full)
                for tt in range(2):
                    for k in range(kc):
                        h, l = xh[:, k, tt * P:tt * P + P], xl[:, k, tt * P:tt * P + P]
                        nc.tensor.matmul(o[:, tt, 0:n], h, wh[:, k, a:a + n], start=k == 0, stop=False)
                        nc.tensor.matmul(o[:, tt, 0:n], l, wh[:, k, a:a + n], start=False, stop=False)
                        mm = nc.tensor.matmul(o[:, tt, 0:n], h, wl[:, k, a:a + n], start=False, stop=k == kc - 1)
                mm.then_inc(unit_used, 1)

            def norm(c, split=True):
                pe.wait_ge(sq_ready, st["norm"] + 1)
                for k in range(c):
                    mm = nc.tensor.matmul(ps[:, 5, 0:T], ones[:], hbuf[:, k, :], start=k == 0, stop=k == c - 1)
                mm.then_inc(ss_ready, 1)
                st["norm"] += 1
                if split:
                    split_in()

            def split_in():
                st["xl"] += 1
                pe.wait_ge(xl_ready, st["xl"])

            def all_out():
                for b in range(2):
                    pe.wait_ge(lin_evac[b], (st["lin"] + 1 - b) // 2)

            def score(s, step):
                if s >= 1:
                    pe.wait_ge(att_biased, s)
                for g, pairs in enumerate(step["scores"]):
                    o = score_bank(step, g)
                    for a, (q, k) in enumerate(pairs):
                        mm = nc.tensor.matmul(o, q, k, start=a == 0, stop=a == len(pairs) - 1)
                mm.then_inc(att_scored, 1)

            def turn(s, step):
                pe.wait_ge(att_probs, s + 1)
                if s >= 1:
                    pe.wait_ge(att_pt, s)
                b = 0
                for g in range(len(step["scores"])):
                    for kt in range(step["nk"] // P):
                        mm = nc.tensor.transpose(ps[:, 2 + b // 4, (b % 4) * P:(b % 4) * P + P],
                                                 S[s % 2][:, g, kt * P:kt * P + P], ident)
                        b += 1
                mm.then_inc(att_turned, 1)

            def mix(s, step, y):
                pe.wait_ge(att_pt, s + 1)
                if y >= 1 and step.get("opens"):
                    pe.wait_ge(att_out, y)
                per = step["nk"] // P
                for lo, k, pv in step["pv"]:
                    for a, (v, g, kt) in enumerate(pv):
                        w = v.shape[1]
                        mm = nc.tensor.matmul(ps[lo:lo + w, 4, k * T + step["qt"] * P:k * T + step["qt"] * P + P],
                                              v, PT[:, g * per + kt, :], start=a == 0, stop=a == len(pv) - 1)
                mm.then_inc(att_mixed, 1)

            def attend(steps, between=None):
                base = st["step"]
                score(base, steps[0])
                for a, step in enumerate(steps):
                    s = base + a
                    if a + 1 < len(steps):
                        score(s + 1, steps[a + 1])
                    if between:
                        between(a)
                    turn(s, step)
                    step["opens"] = a == 0 or steps[a - 1]["last"]
                    mix(s, step, st["y"])
                    if step["last"]:
                        st["y"] += 1
                st["step"] += len(steps)

            def gated(p0, n, trio):
                def gu(u, j, jj, i=None):
                    for w, bank in ((u, 4 + (2 * j) % 4), (u + 1, 5 + (2 * j) % 4)):
                        weights_in(w, i)
                        if w == u and jj is not None:
                            pe.wait_ge(hid_ready, jj)
                        wh, wl = wview(whi, w, DC, T), wview(wlo, w, DC, T)
                        for b in range(2):
                            mm = triple(ps[:, bank, b * T:(b + 1) * T],
                                        [(wh[:, k, b * P:b * P + P], wl[:, k, b * P:b * P + P], xh[:, k, :],
                                          xl[:, k, :]) for k in range(DC)])
                        mm.then_inc(unit_used, 1)

                def down(u, j, jj, i=None, first=False, last=False):
                    weights_in(u, i)
                    pe.wait_ge(al_ready, jj)
                    wh, wl = wview(whi, u, 2, D), wview(wlo, u, 2, D)
                    for c in range(DC):
                        mm = triple(ps[:, c // 2, (c % 2) * T:(c % 2 + 1) * T],
                                    [(wh[:, k, c * P:c * P + P], wl[:, k, c * P:c * P + P],
                                      ah[:, 2 * (j % 2) + k, :], al[:, 2 * (j % 2) + k, :]) for k in range(2)],
                                    first=first and c % 2 == 0, last=last, group=False)
                    mm.then_inc(unit_used, 1)

                gu(p0, 0, None)
                gu(p0 + 2, 1, None)
                down(p0 + 4, 0, trio + 1, first=True)
                body = (n - 2) // 2
                with pe.Fori(0, body) as i:
                    gu(p0 + 5, 2, i * 2 + (trio + 1), i)
                    down(p0 + 7, 1, i * 2 + (trio + 2), i)
                    gu(p0 + 8, 3, i * 2 + (trio + 2), i)
                    down(p0 + 10, 2, i * 2 + (trio + 3), i)
                at = 2 + 2 * body
                while at < n:
                    gu(p0 + 3 * at - 1, at, trio + at - 1)
                    down(p0 + 3 * at + 1, at - 1, trio + at)
                    at += 1
                down(p0 + 3 * n - 1, n - 1, trio + n, last=True)

            pe.wait_ge(ones_set, 1)
            norm(8)
            for u in u_in[0:12]:
                feature_unit(u)
            for u in u_in[12:18]:
                token_unit(u)
            for u in u_in[18:22]:
                feature_unit(u)
            u = u_in[22]
            weights_in(u)
            o = lin_bank()
            wh, wl = wview(whi, u, DC, 256), wview(wlo, u, DC, 256)
            triple(o[:, 0, :], [(wh[:, k, 0:P], wl[:, k, 0:P], xh[:, k, :], xl[:, k, :]) for k in range(DC)])
            for tt in range(2):
                for k in range(DC):
                    h, l = xh[:, k, tt * P:tt * P + P], xl[:, k, tt * P:tt * P + P]
                    oo = o[:, 1, tt * P:tt * P + P]
                    nc.tensor.matmul(oo, h, wh[:, k, P:256], start=k == 0, stop=False)
                    nc.tensor.matmul(oo, l, wh[:, k, P:256], start=False, stop=False)
                    mm = nc.tensor.matmul(oo, h, wl[:, k, P:256], start=False, stop=k == DC - 1)
            mm.then_inc(unit_used, 1)
            all_out()
            nc.tensor.matmul(ps[0:HD, 5, 0:T], ident[:, HD:P], ks[:, 0, :], start=True, stop=True)
            nc.tensor.matmul(ps[HD:P, 5, 0:T], ident[:, 0:HD], ks[:, 0, :], start=True,
                             stop=True).then_inc(kswap_mm, 1)
            pe.wait_ge(kswap_there, 1)

            def gates_between(a):
                if a % 4 == 0:
                    feature_unit(u_in[23 + a // 4])

            attend(steps_a, gates_between)
            split_in()
            split_in()
            for u in u_br:
                feature_unit(u, ah, al)
                feature_unit(u + 1)
            split_in()
            for u in u_out:
                feature_unit(u)
            norm(8)
            token_unit(u_router)
            pe.wait_ge(gates_there, 1)
            for tt in range(2):
                mm = nc.tensor.transpose(ps[0:N_EXP, 5, tt * P:tt * P + P], gates[:, tt, :], ident)
            mm.then_inc(gates_mm, 1)
            pe.wait_ge(gt_there, 1)
            for e in range(N_EXP):
                if e % 2 == 0 and e >= 4:
                    pe.wait_ge((rows_act, rows_dve)[(e // 2) % 2], e // 4)
                mm = nc.tensor.matmul(ps[:, (e // 2) % 2, (e % 2) * T:(e % 2 + 1) * T],
                                      ident[0:N_EXP, e:e + 1].broadcast_to([N_EXP, P]), gt[0:N_EXP, :],
                                      start=True, stop=True)
                if e % 2:
                    mm.then_inc(row_mm, 1)
            pe.wait_ge(rows_act, N_EXP // 4)
            pe.wait_ge(rows_dve, N_EXP // 4)
            gated(moe[0], moe[1], trio0[0])
            norm(8, split=False)

            norm(8)
            for u in u_ev:
                feature_unit(u)
            split_in()
            weights_in(u_pool)
            wh, wl = wview(whi, u_pool, 4, P), wview(wlo, u_pool, 4, P)
            for g in range(4):
                mm = triple(ps[:, g // 2, (g % 2) * T:(g % 2 + 1) * T],
                            [(wh[:, g, :], wl[:, g, :], ah[:, g, :], al[:, g, :])])
            mm.then_inc(unit_used, 1)
            norm(2)
            weights_in(u_qup)
            wh, wl = wview(whi, u_qup, 2, 768), wview(wlo, u_qup, 2, 768)
            pe.wait_ge(pool_out, 1)
            for h in range(MLA_H):
                mm = triple(ps[0:QK, h // 2, (h % 2) * T:(h % 2 + 1) * T],
                            [(wh[:, k, h * QK:(h + 1) * QK], wl[:, k, h * QK:(h + 1) * QK], xh[:, k, :], xl[:, k, :])
                             for k in range(2)])
            mm.then_inc(unit_used, 1)
            pe.wait_ge(kr_there, 1)
            for a in range(2):
                mm = nc.tensor.matmul(ps[0:QK, 4, a * T:(a + 1) * T], put[0:ROPE, a, :], kr[0:ROPE, :],
                                      start=True, stop=True)
            mm.then_inc(kr_mm, 1)
            pe.wait_ge(kr_turned, 1)
            pe.wait_ge(mq_there, 1)
            all_out()
            for h in range(MLA_H):
                mm = nc.tensor.matmul(ps[0:QK, 4 + h // 2, (h % 2) * T:(h % 2 + 1) * T], swap[0:QK, :],
                                      mq[0:QK, h, :], start=True, stop=True)
            mm.then_inc(mq_mm, 1)
            pe.wait_ge(mq_turned, 1)
            norm(1)
            weights_in(u_kvup)
            wh, wl = wview(whi, u_kvup, 1, 1024), wview(wlo, u_kvup, 1, 1024)
            for h in range(MLA_H):
                triple(ps[0:NOPE, h // 2, (h % 2) * T:(h % 2 + 1) * T],
                       [(wh[:, 0, h * P:h * P + NOPE], wl[:, 0, h * P:h * P + NOPE], xh[:, 0, :], xl[:, 0, :])])
            vh = wh[:, 0, :].rearrange("p (h n) -> p h n", h=MLA_H)[:, :, NOPE:P]
            vl = wl[:, 0, :].rearrange("p (h n) -> p h n", h=MLA_H)[:, :, NOPE:P]
            for tt in range(2):
                o = ps[:, 6 + tt, :].rearrange("p (h n) -> p h n", h=MLA_H)
                h, l = xh[:, 0, tt * P:tt * P + P], xl[:, 0, tt * P:tt * P + P]
                nc.tensor.matmul(o, h, vh, start=True, stop=False)
                nc.tensor.matmul(o, l, vh, start=False, stop=False)
                mm = nc.tensor.matmul(o, h, vl, start=False, stop=True)
            mm.then_inc(unit_used, 1)
            pe.wait_ge(kv_out, 1)
            attend(steps_m)
            split_in()
            split_in()
            for u in u_evo:
                feature_unit(u)

            def cross(l):
                norm(8)
                for u in u_xa[l][0][0:4]:
                    feature_unit(u)
                for u in u_xa[l][0][4:8]:
                    token_unit(u)
                norm(8)
                for u in u_xa[l][1]:
                    feature_unit(u)
                all_out()
                attend(steps_x)
                split_in()
                for u in u_xa[l][2]:
                    feature_unit(u)

            cross(0)
            norm(8)
            gated(ffn[0][0], ffn[0][1], trio0[1])
            norm(8)
            for u in u_od:
                feature_unit(u)
            split_in()
            for a in range(2):
                u = u_rg + a
                weights_in(u)
                wh, wl = wview(whi, u, DC, 256), wview(wlo, u, DC, 256)
                for c in range(DC):
                    h = c // 2
                    mm = triple(ps[:, 4 * a + c // 2, (c % 2) * T:(c % 2 + 1) * T],
                                [(wh[:, 2 * h + k, (c % 2) * P:(c % 2) * P + P],
                                  wl[:, 2 * h + k, (c % 2) * P:(c % 2) * P + P], xh[:, 2 * h + k, :],
                                  xl[:, 2 * h + k, :]) for k in range(2)])
                mm.then_inc(unit_used, 1)
            split_in()
            for u in u_odo:
                feature_unit(u)
            cross(1)
            norm(8)
            gated(ffn[1][0], ffn[1][1], trio0[2])
            norm(8, split=False)

        @block.scalar
        def _(act):
            st = dict(hi=0, lin=0, step=0, split=0, norm=0)

            def hi(u, i=None):
                act.wait_ge(raw_landed[u % RAW], (0 if i is None else i * 16) + 16 * (u // RAW + 1))
                if i is not None or u >= HL:
                    act.wait_ge(unit_used, (0 if i is None else i * 6) + (u - HL + 1))
                n = usize(u)
                nc.scalar.activation(whi[u % HL][:, 0:n], raw[u % RAW][:, 0:n], ACT.Copy).then_inc(hi_ready, 1)

            def ahead(u):
                while st["hi"] < min(u + HL, len(units)):
                    hi(st["hi"])
                    st["hi"] += 1

            def split_high(src, dst, used=None):
                st["split"] += 1
                act.wait_ge(h_ready, st["split"])
                if used is not None:
                    act.wait_ge(unit_used, used)
                nc.scalar.activation(dst, src, ACT.Copy).then_inc(xh_ready, 1)

            def norm(c, split=True):
                st["norm"] += 1
                act.wait_ge(ms_ready, st["norm"])
                nc.scalar.activation(rstd[:], rstd[:], ACT.Sqrt).then_inc(rstd_ready, 1)
                if split:
                    split_high(hbuf[:, 0:c, :], xh[:, 0:c, :])

            def evac(u, m, dst, func=ACT.Copy):
                act.wait_ge(unit_used, u + 1)
                nc.scalar.activation(dst, ps[:, 6 + m % 2, :].rearrange("p (c t) -> p c t", c=2),
                                     func).then_inc(lin_evac[m % 2], 1)

            def stage(us, dst=None):
                for a, u in enumerate(us):
                    ahead(u)
                    if dst and st["lin"] % 2 == 0:
                        evac(u, st["lin"], dst(a))
                    st["lin"] += 1

            def exps(s, step):
                act.wait_ge(att_max, s + 1)
                b, nk = s % 2, step["nk"]
                n = len(step["scores"])
                if step["sink"] is not None:
                    for g in range(2):
                        nc.scalar.activation(sm[:, b, 12 + g:13 + g],
                                             sink_row[:, step["sink"] + g:step["sink"] + g + 1],
                                             ACT.Exp, bias=sm[:, b, 3 + g:4 + g])
                if step["merged"]:
                    last = nc.scalar.activation(S[b][:, 0:n, 0:nk], S[b][:, 0:n, 0:nk], ACT.Exp,
                                                bias=sm[:, b, 3:4], scale=step["scale"], accum_out=sm[:, b, 6:7])
                else:
                    for g in range(n):
                        last = nc.scalar.activation(S[b][:, g, 0:nk], S[b][:, g, 0:nk], ACT.Exp,
                                                    bias=sm[:, b, 3 + g:4 + g], scale=step["scale"],
                                                    accum_out=sm[:, b, 6 + g:7 + g])
                last.then_inc(att_exp, 1)

            def copy_turned(s, step):
                act.wait_ge(att_turned, s + 1)
                if s >= 1:
                    act.wait_ge(att_mixed, s)
                n = len(step["scores"]) * step["nk"] // P
                last = nc.scalar.activation(PT[:, 0:min(n, 4), :],
                                            ps[:, 2, 0:min(n, 4) * P].rearrange("p (b q) -> p b q", q=P), ACT.Copy)
                if n > 4:
                    last = nc.scalar.activation(PT[:, 4:n, :],
                                                ps[:, 3, 0:(n - 4) * P].rearrange("p (b q) -> p b q", q=P), ACT.Copy)
                last.then_inc(att_pt, 1)

            def attend(steps, between=None):
                base = st["step"]
                exps(base, steps[0])
                for a, step in enumerate(steps):
                    if a + 1 < len(steps):
                        exps(base + a + 1, steps[a + 1])
                    copy_turned(base + a, step)
                    if between:
                        between(a)
                st["step"] += len(steps)

            def gated(p0, n, trio):
                def gate(u, j, free, i=None):
                    act.wait_ge(unit_used, (0 if i is None else i * 6) + (u + 2))
                    if free is not None:
                        act.wait_ge(hid_ready, free)
                    nc.scalar.activation(sil[j % 2], ps[:, 4 + (2 * j) % 4, :], ACT.Silu).then_inc(silu_done, 1)

                def high(j, ready, used=None, i=None):
                    act.wait_ge(hid_ready, ready)
                    if used is not None:
                        act.wait_ge(unit_used, (0 if i is None else i * 6) + used)
                    nc.scalar.activation(ah[:, 2 * (j % 2):2 * (j % 2) + 2, :],
                                         hid[j % 2].rearrange("p (c t) -> p c t", c=2), ACT.Copy).then_inc(ah_ready, 1)

                ahead(p0)
                gate(p0, 0, None)
                hi(p0 + 3)
                high(0, trio + 1)
                hi(p0 + 4)
                hi(p0 + 5)
                gate(p0 + 2, 1, None)
                hi(p0 + 6)
                high(1, trio + 2)
                body = (n - 2) // 2
                with act.Fori(0, body) as i:
                    for j in (2, 3):
                        u = p0 + 3 * j - 1
                        hi(u + 2, i)
                        hi(u + 3, i)
                        gate(u, j, i * 2 + (trio + j - 1), i)
                        hi(u + 4, i)
                        high(j, i * 2 + (trio + j + 1), u, i)
                for j in range(2 + 2 * body, n):
                    u = p0 + 3 * j - 1
                    hi(u + 2)
                    hi(u + 3)
                    gate(u, j, trio + j - 1)
                    if u + 4 < len(units):
                        hi(u + 4)
                    high(j, trio + j + 1, u)
                st["hi"] = min(p0 + 3 * n + 1, len(units))

            norm(8)
            stage(u_in[0:6], lambda a: qd[:, 2 * a:2 * a + 2, :])
            stage(u_in[6:12], lambda a: kd[:, 2 * a:2 * a + 2, :])
            stage(u_in[12:18], lambda a: vd[:, :, a * 256:(a + 1) * 256])
            stage(u_in[18:22], lambda a: qs[:, 2 * a:2 * a + 2, :])
            stage(u_in[22:23])

            def gates_out(a):
                k = a // 4
                if a % 4 == 3:
                    u = u_in[23 + k]
                    ahead(u)
                    evac(u, st["lin"], sg[:, 2 * k:2 * k + 2, :], ACT.Sigmoid)
                    st["lin"] += 1

            attend(steps_a, gates_out)
            split_high(qd[:, 0:4, :], ah[:])
            split_high(qs, xh[:], u_in[-1] + 1)
            stage(range(u_br[0], u_br[-1] + 2))
            split_high(hbuf, xh[:], u_br[-1] + 2)
            stage(u_out)
            norm(8)
            stage([u_router])
            act.wait_ge(route_grp, 1)
            nc.scalar.activation(rt[:, :, 4:8], rt[:, :, 4:8], ACT.Exp).then_inc(route_grp_exp, 1)
            act.wait_ge(route_two, 1)
            nc.scalar.activation(rt[:, :, 24:25], rt[:, :, 23:24], ACT.Exp).then_inc(route_two_exp, 1)
            for e in range(0, N_EXP, 4):
                act.wait_ge(row_mm, e // 2 + 1)
                nc.scalar.activation(gb[:, e:e + 2, :], ps[:, 0, :].rearrange("p (c t) -> p c t", c=2),
                                     ACT.Copy).then_inc(rows_act, 1)
            gated(moe[0], moe[1], trio0[0])
            norm(8, split=False)
            norm(8)
            stage(u_ev)
            split_high(ypool, ah[:])
            ahead(u_pool)
            norm(2)
            ahead(u_qup)
            act.wait_ge(angles, 1)
            nc.scalar.activation(sinr[0:QK, :], sinr[0:QK, :], ACT.Sin)
            nc.scalar.activation(cosr[0:QK, :], cosr[0:QK, :], ACT.Sin).then_inc(trig, 1)
            norm(1)
            ahead(u_kvup)
            attend(steps_m)
            split_high(ypool, xh[:, 0:4, :], u_kvup + 1)
            split_high(my, xh[:, 4:8, :])
            stage(u_evo)

            def cross(l):
                norm(8)
                stage(u_xa[l][0][0:4], lambda a: xk[:, 2 * a:2 * a + 2, :])
                stage(u_xa[l][0][4:8], lambda a: xv[:, :, a * 256:(a + 1) * 256])
                norm(8)
                stage(u_xa[l][1], lambda a: xq[:, 2 * a:2 * a + 2, :])
                attend(steps_x)
                split_high(xq, xh[:], u_xa[l][1][-1] + 1)
                stage(u_xa[l][2])

            cross(0)
            norm(8)
            gated(ffn[0][0], ffn[0][1], trio0[1])
            act.wait_ge(lam_abs, 1)
            nc.scalar.activation(lsm[:, 1, :], lsm[:, 0, :], ACT.Exp, scale=-1.0).then_inc(lam_exp, 1)
            norm(8)
            stage(u_od)
            split_high(lxc, xh[:], u_od[-1] + 1)
            ahead(u_rg)
            act.wait_ge(unit_used, u_rg + 1)
            for c in range(DC):
                last = nc.scalar.activation(lr[:, c, :], ps[:, c // 2, (c % 2) * T:(c % 2 + 1) * T], ACT.Sigmoid,
                                            bias=vcol("b_r", c))
            last.then_inc(lru_r, 1)
            ahead(u_rg + 1)
            act.wait_ge(unit_used, u_rg + 2)
            for c in range(DC):
                last = nc.scalar.activation(li[:, c, :], ps[:, 4 + c // 2, (c % 2) * T:(c % 2 + 1) * T], ACT.Sigmoid,
                                            bias=vcol("b_i", c))
            last.then_inc(lru_i, 1)
            act.wait_ge(lam_scale, 1)
            act.wait_ge(lru_r, 1)
            for c in range(DC):
                last = nc.scalar.activation(lr[:, c, :], lr[:, c, :], ACT.Tanh, scale=lsm[:, 7, c:c + 1])
            last.then_inc(lru_t, 1)
            nc.scalar.activation(lgate, lgate, ACT.Gelu_apprx_tanh).then_inc(lru_gelu, 1)
            act.wait_ge(lru_t_max, 1)
            nc.scalar.activation(lxc, lr, ACT.Sqrt).then_inc(lru_root, 1)
            split_high(lgate, xh[:], u_rg + 2)
            stage(u_odo)
            cross(1)
            norm(8)
            gated(ffn[1][0], ffn[1][1], trio0[2])
            norm(8, split=False)

        @block.vector
        def _(dve):
            st = dict(lo=0, lin=0, step=0, split=0, norm=0, chain=0, y=0)
            v = nc.vector

            def link(ins):
                st["chain"] += 1
                ins.then_inc(dve_step, 1)
                dve.wait_ge(dve_step, st["chain"])

            def lo(u, i=None):
                dve.wait_ge(hi_ready, (0 if i is None else i * 6) + (u + 1))
                if i is not None or u >= HL:
                    dve.wait_ge(unit_used, (0 if i is None else i * 6) + (u - HL + 1))
                n = usize(u)
                v.tensor_tensor(wlo[u % HL][:, 0:n], raw[u % RAW][:, 0:n], whi[u % HL][:, 0:n].bitcast(F32),
                                ALU.subtract).then_inc(lo_ready, 1)

            def ahead(u):
                while st["lo"] < min(u + HL, len(units)):
                    lo(st["lo"])
                    st["lo"] += 1

            def split_low(src, high, low, used=None):
                st["split"] += 1
                dve.wait_ge(xh_ready, st["split"])
                if used is not None:
                    dve.wait_ge(unit_used, used)
                v.tensor_tensor(low, src, high.bitcast(F32), ALU.subtract).then_inc(xl_ready, 1)

            def norm(src, c, width, gain, dst=None):
                st["norm"] += 1
                k = st["norm"]
                v.tensor_tensor(hbuf[:, 0:c, :], src, src, ALU.mult).then_inc(sq_ready, 1)
                dve.wait_ge(ss_ready, k)
                link(v.tensor_scalar(rstd[:], ps[:, 5, 0:T], 1.0 / width, EPS, ALU.mult, ALU.add))
                v.reciprocal(rstd[:], rstd[:]).then_inc(ms_ready, 1)
                dve.wait_ge(rstd_ready, k)
                to = hbuf if dst is None else dst
                for a in range(c):
                    last = v.scalar_tensor_tensor(out=to[:, a, :], in0=src[:, a, :], scalar=vcol(gain, a),
                                                  in1=rstd[:], op0=ALU.mult, op1=ALU.mult)
                if dst is None:
                    last.then_inc(h_ready, 1)
                    split_low(hbuf[:, 0:c, :], xh[:, 0:c, :], xl[:, 0:c, :])
                return last

            def bank(m):
                return ps[:, 6 + m % 2, :].rearrange("p (c t) -> p c t", c=2)

            def stage(us, dst=None):
                for a, u in enumerate(us):
                    ahead(u)
                    m = st["lin"]
                    if dst and m % 2 == 1:
                        dve.wait_ge(unit_used, u + 1)
                        v.tensor_copy(dst(a), bank(m)).then_inc(lin_evac[m % 2], 1)
                    st["lin"] += 1

            def all_out():
                for b in range(2):
                    dve.wait_ge(lin_evac[b], (st["lin"] + 1 - b) // 2)

            def residual(us):
                for a, u in enumerate(us):
                    ahead(u)
                    m = st["lin"]
                    dve.wait_ge(unit_used, u + 1)
                    v.tensor_tensor(x[:, 2 * a:2 * a + 2, :], bank(m), x[:, 2 * a:2 * a + 2, :],
                                    ALU.add).then_inc(lin_evac[m % 2], 1)
                    st["lin"] += 1
                all_out()

            def bias_max(s, step):
                dve.wait_ge(att_scored, s + 1)
                if s >= 2:
                    dve.wait_ge(att_turned, s - 1)
                b, nk, n = s % 2, step["nk"], len(step["scores"])
                for g in range(n):
                    src = score_bank(step, g)
                    dst = S[b][:, g, 0:nk]
                    if step["bias"] is None:
                        last = v.tensor_copy(dst, src)
                    elif step["bias"] == "causal":
                        last = v.tensor_tensor(dst, src, causal[:, T - nk:T], ALU.add)
                    else:
                        pi, slope = step["bias"][g]
                        last = v.scalar_tensor_tensor(out=dst, in0=pat[:, pi, T - nk:T], scalar=-slope, in1=src,
                                                      op0=ALU.mult, op1=ALU.add)
                last.then_inc(att_biased, 1)
                dve.wait_ge(att_biased, s + 1)
                if step["merged"]:
                    link(v.tensor_reduce(sm[:, b, 0:1], S[b][:, 0:n, 0:nk], AX.XY, ALU.max))
                    n = 1
                else:
                    link(v.tensor_reduce(sm[:, b, 0:n], S[b][:, 0:n, 0:nk], AX.X, ALU.max))
                if step["sink"] is not None:
                    link(v.scalar_tensor_tensor(out=sm[:, b, 0:n], in0=sm[:, b, 0:n], scalar=step["scale"],
                                                in1=sink_row[:, step["sink"]:step["sink"] + n],
                                                op0=ALU.mult, op1=ALU.max))
                    v.tensor_scalar(sm[:, b, 3:3 + n], sm[:, b, 0:n], -1.0, None, ALU.mult).then_inc(att_max, 1)
                else:
                    v.tensor_scalar(sm[:, b, 3:3 + n], sm[:, b, 0:n], -step["scale"], None,
                                    ALU.mult).then_inc(att_max, 1)

            def probs(s, step):
                dve.wait_ge(att_exp, s + 1)
                b, nk, n = s % 2, step["nk"], len(step["scores"])
                k = 1 if step["merged"] else n
                if step["sink"] is not None:
                    link(v.tensor_tensor(sm[:, b, 6:6 + k], sm[:, b, 6:6 + k], sm[:, b, 12:12 + k], ALU.add))
                link(v.reciprocal(sm[:, b, 9:9 + k], sm[:, b, 6:6 + k]))
                if step["merged"]:
                    last = v.tensor_scalar(S[b][:, 0:n, 0:nk], S[b][:, 0:n, 0:nk], sm[:, b, 9:10], None, ALU.mult)
                else:
                    for g in range(n):
                        last = v.tensor_scalar(S[b][:, g, 0:nk], S[b][:, g, 0:nk], sm[:, b, 9 + g:10 + g], None,
                                               ALU.mult)
                last.then_inc(att_probs, 1)

            def attend(steps, y_of, between=None):
                base = st["step"]

                def out(a):
                    step = steps[a]
                    if step["last"]:
                        dve.wait_ge(att_mixed, base + a + 1)
                        w = len(step["y"])
                        v.tensor_copy(y_of(st["yk"], w), ps[:, 4, 0:w * T].rearrange("p (c t) -> p c t",
                                                                                    c=w)).then_inc(att_out, 1)
                        st["y"] += 1
                        st["yk"] += w

                st["yk"] = 0
                bias_max(base, steps[0])
                for a, step in enumerate(steps):
                    if a + 1 < len(steps):
                        bias_max(base + a + 1, steps[a + 1])
                    if a >= 1:
                        out(a - 1)
                    probs(base + a, step)
                    if between:
                        between(a)
                out(len(steps) - 1)
                dve.wait_ge(att_out, st["y"])
                st["step"] += len(steps)

            def gated(p0, n, trio, expert):
                def hidden(u, j, g, free=False, i=None):
                    dve.wait_ge(unit_used, (0 if i is None else i * 6) + (u + 2))
                    if free:
                        dve.wait_ge(al_ready, g - 1)
                    o = hid[j % 2].rearrange("p (c t) -> p c t", c=2)
                    up_ps = ps[:, 5 + (2 * j) % 4, :].rearrange("p (c t) -> p c t", c=2)
                    s = sil[j % 2].rearrange("p (c t) -> p c t", c=2)
                    if expert:
                        at = (8 + j // 2) * T if i is None else i * T + (8 + j // 2) * T
                        row = arena[:, bass.ds(at, T)].unsqueeze(1).broadcast_to([P, 2, T])
                        v.tensor_tensor(o, up_ps, row, ALU.mult).then_inc(hid_scaled, 1)
                        dve.wait_ge(hid_scaled, g + 1)
                        dve.wait_ge(silu_done, g + 1)
                        v.tensor_tensor(o, o, s, ALU.mult).then_inc(hid_ready, 1)
                    else:
                        dve.wait_ge(silu_done, g + 1)
                        v.tensor_tensor(o, up_ps, s, ALU.mult).then_inc(hid_ready, 1)

                def low(j, g, used=None, i=None):
                    dve.wait_ge(ah_ready, g + 1)
                    if used is not None:
                        dve.wait_ge(unit_used, (0 if i is None else i * 6) + used)
                    v.tensor_tensor(al[:, 2 * (j % 2):2 * (j % 2) + 2, :],
                                    hid[j % 2].rearrange("p (c t) -> p c t", c=2),
                                    ah[:, 2 * (j % 2):2 * (j % 2) + 2, :].bitcast(F32),
                                    ALU.subtract).then_inc(al_ready, 1)

                ahead(p0)
                hidden(p0, 0, trio)
                lo(p0 + 3)
                low(0, trio)
                lo(p0 + 4)
                lo(p0 + 5)
                hidden(p0 + 2, 1, trio + 1)
                lo(p0 + 6)
                low(1, trio + 1)
                body = (n - 2) // 2
                with dve.Fori(0, body) as i:
                    for j in (2, 3):
                        u = p0 + 3 * j - 1
                        lo(u + 2, i)
                        lo(u + 3, i)
                        hidden(u, j, i * 2 + (trio + j), True, i)
                        lo(u + 4, i)
                        low(j, i * 2 + (trio + j), u, i)
                for j in range(2 + 2 * body, n):
                    u = p0 + 3 * j - 1
                    lo(u + 2)
                    lo(u + 3)
                    hidden(u, j, trio + j, True)
                    if u + 4 < len(units):
                        lo(u + 4)
                    low(j, trio + j, u)
                st["lo"] = min(p0 + 3 * n + 1, len(units))
                dve.wait_ge(unit_used, p0 + 3 * n)
                link(v.tensor_tensor(x[:], ps[:, 0:4, :].rearrange("p b (c t) -> p (b c) t", c=2), x[:], ALU.add))

            v.memset(ones[:], 1.0).then_inc(ones_set, 1)
            dve.wait_ge(x_landed, 16)
            dve.wait_ge(consts_landed, 64)
            norm(x[:], 8, D, "g_mix")
            stage(u_in[0:6], lambda a: qd[:, 2 * a:2 * a + 2, :])
            stage(u_in[6:12], lambda a: kd[:, 2 * a:2 * a + 2, :])
            stage(u_in[12:18], lambda a: vd[:, :, a * 256:(a + 1) * 256])
            stage(u_in[18:22], lambda a: qs[:, 2 * a:2 * a + 2, :])
            ahead(u_in[22])
            dve.wait_ge(unit_used, u_in[22] + 1)
            v.tensor_copy(ks, bank(22)[:, 0:1, :])
            v.tensor_copy(vs, bank(22)[:, 1, :].rearrange("p (a b) -> p a b", a=2)).then_inc(lin_evac[0], 1)
            st["lin"] += 1
            dve.wait_ge(kswap_mm, 1)
            v.tensor_copy(kswap[:, 0, :], ps[:, 5, 0:T]).then_inc(kswap_there, 1)

            def gates_ahead(a):
                if a % 4 == 3:
                    ahead(u_in[23 + a // 4])
                    st["lin"] += 1

            def y_a(k, w):
                return qd[:, k:k + w, :] if k < 4 else qs[:, k - 4:k - 4 + w, :]

            attend(steps_a, y_a, gates_ahead)
            all_out()
            dve.sem_inc(h_ready, 2)
            split_low(qd[:, 0:4, :], ah[:], al[:])
            split_low(qs, xh[:], xl[:], u_in[-1] + 1)
            for k, u in enumerate(u_br):
                two = slice(2 * k, 2 * k + 2)
                sd, ss = sg[:, two, :], sg[:, 8 + 2 * k:10 + 2 * k, :]
                ahead(u)
                m = st["lin"]
                dve.wait_ge(unit_used, u + 1)
                v.tensor_tensor(hbuf[:, two, :], bank(m), sd, ALU.mult).then_inc(lin_evac[m % 2], 1)
                ahead(u + 1)
                dve.wait_ge(unit_used, u + 2)
                v.tensor_tensor(ss, bank(m + 1), ss, ALU.mult).then_inc(lin_evac[(m + 1) % 2], 1)
                st["lin"] += 2
                all_out()
                last = v.tensor_tensor(hbuf[:, two, :], hbuf[:, two, :], ss, ALU.add)
            last.then_inc(h_ready, 1)
            split_low(hbuf, xh[:], xl[:], u_br[-1] + 2)
            residual(u_out)
            dve.sem_inc(moe_starts, 1)
            norm(x[:], 8, D, "g_ffn")

            def col(a, n=1):
                return rt[:, :, a:a + n]

            def wide(a, n):
                return col(a).broadcast_to([P, 2, n])

            gkeys = gkey.unsqueeze(1).broadcast_to([P, 2, N_GRP])
            ekeys = ekey.unsqueeze(1).broadcast_to([P, 2, N_EXP])
            ahead(u_router)
            dve.wait_ge(unit_used, u_router + 1)
            m = st["lin"]
            v.tensor_tensor(lg, bank(m)[:, :, 0:36], bias_row.unsqueeze(1).broadcast_to([P, 2, 36]),
                            ALU.add).then_inc(lin_evac[m % 2], 1)
            st["lin"] += 1
            all_out()
            gl = lg[:, :, 0:N_GRP]
            el = lg[:, :, N_GRP:].rearrange("p a (g e) -> p a g e", g=N_GRP)

            def first_max(dst, src, n, keys, top, key, kmax):
                link(v.tensor_reduce(col(top), src, AX.X, ALU.max))
                link(v.tensor_tensor(col(key, n), src, wide(top, n), ALU.is_equal))
                link(v.tensor_tensor(col(key, n), col(key, n), keys, ALU.mult))
                link(v.tensor_reduce(col(kmax), col(key, n), AX.X, ALU.max))
                link(v.tensor_tensor(dst, col(key, n), wide(kmax, n), ALU.is_equal))

            first_max(col(12, 4), gl, N_GRP, gkeys, 0, 8, 3)
            v.tensor_tensor(col(4, 4), gl, wide(0, 4), ALU.subtract).then_inc(route_grp, 1)
            dve.wait_ge(route_grp_exp, 1)
            link(v.tensor_reduce(col(1), col(4, 4), AX.X, ALU.add))
            link(v.reciprocal(col(2), col(1)))
            link(v.tensor_scalar(col(16, 4), col(12, 4), -FAR, FAR, ALU.mult, ALU.add))
            for a in range(2):
                pen = rt[:, a, 16:20].unsqueeze(2).broadcast_to([P, N_GRP, 8])
                link(v.tensor_tensor(rt[:, a, 32:64].rearrange("p (g e) -> p g e", g=N_GRP), el[:, a], pen, ALU.add))
            first_max(col(96, 32), col(32, 32), N_EXP, ekeys, 20, 64, 21)
            link(v.scalar_tensor_tensor(out=col(128, 32), in0=col(96, 32), scalar=2 * FAR, in1=col(32, 32),
                                        op0=ALU.mult, op1=ALU.add))
            first_max(col(160, 32), col(128, 32), N_EXP, ekeys, 22, 64, 21)
            v.tensor_tensor(col(23), col(22), col(20), ALU.subtract).then_inc(route_two, 1)
            dve.wait_ge(route_two_exp, 1)
            link(v.tensor_scalar(col(25), col(24), 1.0, None, ALU.add))
            link(v.reciprocal(col(25), col(25)))
            link(v.tensor_tensor(col(25), col(25), col(2), ALU.mult))
            link(v.tensor_tensor(col(26), col(25), col(24), ALU.mult))
            link(v.tensor_tensor(col(96, 32), col(96, 32), wide(25, 32), ALU.mult))
            link(v.tensor_tensor(col(160, 32), col(160, 32), wide(26, 32), ALU.mult))
            v.tensor_tensor(gates, col(96, 32), col(160, 32), ALU.add).then_inc(gates_there, 1)
            dve.wait_ge(gates_mm, 1)
            v.tensor_copy(gt[0:N_EXP, :], ps[0:N_EXP, 5, 0:T]).then_inc(gt_there, 1)
            for e in range(2, N_EXP, 4):
                dve.wait_ge(row_mm, e // 2 + 1)
                v.tensor_copy(gb[:, e:e + 2, :], ps[:, 1, :].rearrange("p (c t) -> p c t",
                                                                      c=2)).then_inc(rows_dve, 1)
            dve.wait_ge(rows_act, N_EXP // 4)
            dve.wait_ge(rows_dve, N_EXP // 4)
            gated(moe[0], moe[1], trio0[0], True)
            link(norm(x[:], 8, D, "g_final", dst=x))

            for b in range(3):
                link(v.memset(pooled[b][:, :, 0:16], 0.0))
            norm(x[:], 8, D, "ev_norm")
            dve.wait_ge(second_landed, 48)
            link(v.tensor_copy(posf, posi.bitcast(I32)))
            for a, u in enumerate(u_ev):
                ahead(u)
                m = st["lin"]
                dve.wait_ge(unit_used, u + 1)
                if a < 2:
                    last = v.tensor_copy(pooled[0][:, 2 * a:2 * a + 2, 16:], bank(m))
                elif a == 2:
                    last = v.tensor_copy(lat[:, 0:2, :], bank(m))
                else:
                    v.tensor_copy(lat[:, 2, :], bank(m)[:, 0, :])
                    last = v.tensor_copy(kr[0:ROPE, :], bank(m)[0:ROPE, 1, :])
                last.then_inc(lin_evac[m % 2], 1)
                st["lin"] += 1
            all_out()
            dve.sem_inc(kr_there, 1)
            p0_, p1_, p2_ = pooled
            for g, (dst, src, back) in enumerate(((p1_, p0_, 1), (p2_, p1_, 2), (p1_, p2_, 4), (p2_, p1_, 8))):
                link(v.tensor_tensor(dst[:, g:, 16:], src[:, g:, 16:], src[:, g:, 16 - back:16 - back + T], ALU.add))
            for g in range(4):
                src = (p1_, p2_)[g % 2][:, g, 16:]
                link(v.tensor_tensor(src, src, icnt[:, g, :], ALU.mult))
                last = v.tensor_tensor(ypool[:, g, :], src, p0_[:, g, 16:], ALU.subtract)
            last.then_inc(h_ready, 1)
            two_pi_hi, magic = 6.28125, 12582912.0
            two_pi_lo = 2 * np.pi - two_pi_hi
            a0, a1 = cosr[0:QK, :], sinr[0:QK, :]
            turns = rstd[0:QK, :]
            link(v.tensor_scalar(a0, posf[0:QK, :], freq[0:QK, 0:1], None, ALU.mult))
            link(v.tensor_copy(a1, a0))
            for dst, quarter in ((a1, 0.0), (a0, 0.25)):
                link(v.tensor_scalar(turns, dst, float(1 / (2 * np.pi)), quarter, ALU.mult, ALU.add))
                link(v.tensor_scalar(turns, turns, magic, None, ALU.add))
                link(v.tensor_scalar(turns, turns, magic, None, ALU.subtract))
                link(v.scalar_tensor_tensor(out=dst, in0=turns, scalar=-two_pi_hi, in1=dst, op0=ALU.mult, op1=ALU.add))
                link(v.scalar_tensor_tensor(out=dst, in0=turns, scalar=-float(two_pi_lo), in1=dst, op0=ALU.mult,
                                            op1=ALU.add))
                link(v.tensor_scalar(dst, dst, float(quarter * 2 * np.pi), 3.1415925, ALU.add, ALU.min))
                link(v.tensor_scalar(dst, dst, -3.1415925, None, ALU.max))
            dve.sem_inc(angles, 1)
            split_low(ypool, ah[:], al[:])
            ahead(u_pool)
            dve.wait_ge(unit_used, u_pool + 1)
            for g in range(4):
                last = v.tensor_scalar(ypool[:, g, :], ps[:, g // 2, (g % 2) * T:(g % 2 + 1) * T],
                                       vcol("pool_scale", g), None, ALU.mult)
            last.then_inc(pool_out, 1)
            norm(lat[:, 0:2, :], 2, 256, "q_norm")
            ahead(u_qup)
            dve.wait_ge(unit_used, u_qup + 1)
            eight = lambda rows_, b: ps[0:rows_, b:b + 4, :].rearrange("p b (c t) -> p (b c) t", c=2)
            v.tensor_copy(mq[0:QK, :, :], eight(QK, 0)).then_inc(mq_there, 1)
            dve.wait_ge(trig, 1)
            link(v.tensor_scalar(sinr[0:QK, :], sinr[0:QK, :], freq[0:QK, 1:2], None, ALU.mult))
            dve.wait_ge(kr_mm, 1)
            link(v.tensor_tensor(kr[0:QK, :], ps[0:QK, 4, 0:T], cosr[0:QK, :], ALU.mult))
            link(v.tensor_tensor(hbuf[0:QK, 0, :], ps[0:QK, 4, T:2 * T], sinr[0:QK, :], ALU.mult))
            link(v.tensor_tensor(kr[0:QK, :], kr[0:QK, :], hbuf[0:QK, 0, :], ALU.add))
            dve.sem_inc(kr_turned, 1)
            cos8 = cosr[0:QK, :].unsqueeze(1).broadcast_to([QK, MLA_H, T])
            sin8 = sinr[0:QK, :].unsqueeze(1).broadcast_to([QK, MLA_H, T])
            dve.wait_ge(mq_mm, 1)
            link(v.tensor_tensor(hbuf[0:QK, :, :], eight(QK, 4), sin8, ALU.mult))
            link(v.tensor_tensor(mq[0:QK, :, :], mq[0:QK, :, :], cos8, ALU.mult))
            v.tensor_tensor(mq[0:QK, :, :], mq[0:QK, :, :], hbuf[0:QK, :, :], ALU.add).then_inc(mq_turned, 1)
            dve.wait_ge(mq_turned, 1)
            norm(lat[:, 2:3, :], 1, P, "kv_norm")
            ahead(u_kvup)
            dve.wait_ge(unit_used, u_kvup + 1)
            v.tensor_copy(mk[0:NOPE, :, :], eight(NOPE, 0))
            v.tensor_copy(mk[NOPE:QK, :, :], kr[NOPE:QK, :].unsqueeze(1).broadcast_to([ROPE, MLA_H, T]))
            v.tensor_copy(mv, ps[:, 6:8, :]).then_inc(kv_out, 1)
            attend(steps_m, lambda k, w: my[:, k:k + w, :])
            dve.sem_inc(h_ready, 2)
            split_low(ypool, xh[:, 0:4, :], xl[:, 0:4, :], u_kvup + 1)
            split_low(my, xh[:, 4:8, :], xl[:, 4:8, :])
            residual(u_evo)

            def cross(l):
                norm(mem, 8, D, f"xa_m{l}")
                stage(u_xa[l][0][0:4], lambda a: xk[:, 2 * a:2 * a + 2, :])
                stage(u_xa[l][0][4:8], lambda a: xv[:, :, a * 256:(a + 1) * 256])
                norm(x[:], 8, D, f"xa_x{l}")
                stage(u_xa[l][1], lambda a: xq[:, 2 * a:2 * a + 2, :])
                attend(steps_x, lambda k, w: xq[:, k:k + w, :])
                dve.sem_inc(h_ready, 1)
                split_low(xq, xh[:], xl[:], u_xa[l][1][-1] + 1)
                residual(u_xa[l][2])

            cross(0)
            norm(x[:], 8, D, "ffn0")
            gated(ffn[0][0], ffn[0][1], trio0[1], False)

            lam = vec[:, VECS["lam"][0]:VECS["lam"][0] + 8]
            row = lambda k: lsm[:, k, :]
            link(v.tensor_scalar(row(5), lam, -1.0, None, ALU.mult))
            v.tensor_tensor(row(0), row(5), lam, ALU.max).then_inc(lam_abs, 1)
            link(v.tensor_scalar(row(5), row(5), 0.0, None, ALU.max))
            dve.wait_ge(lam_exp, 1)
            link(v.tensor_scalar(row(2), row(1), 2.0, None, ALU.add))
            link(v.reciprocal(row(2), row(2)))
            link(v.tensor_tensor(row(2), row(2), row(1), ALU.mult))
            link(v.tensor_tensor(row(3), row(2), row(2), ALU.mult))
            link(v.tensor_scalar(row(4), row(3), 1.0 / 17, None, ALU.mult))
            for odd in range(15, 1, -2):
                link(v.scalar_tensor_tensor(out=row(4), in0=row(4), scalar=1.0 / odd, in1=row(3), op0=ALU.add,
                                            op1=ALU.mult))
            link(v.scalar_tensor_tensor(out=row(4), in0=row(4), scalar=1.0, in1=row(2), op0=ALU.add, op1=ALU.mult))
            link(v.scalar_tensor_tensor(out=row(4), in0=row(4), scalar=2.0, in1=row(5), op0=ALU.mult, op1=ALU.add))
            v.tensor_scalar(row(7), row(4), LRU_C / 2, None, ALU.mult).then_inc(lam_scale, 1)
            link(v.tensor_scalar(reset, posf, 0.0, None, ALU.is_equal))
            link(v.memset(lxb[:, :, 0:4], 0.0))
            norm(x[:], 8, D, "od_norm")
            for a, u in enumerate(u_od):
                ahead(u)
                m = st["lin"]
                dve.wait_ge(unit_used, u + 1)
                dst = lgate[:, 2 * a:2 * a + 2, :] if a < 4 else lxb[:, 2 * a - 8:2 * a - 6, 4:]
                v.tensor_copy(dst, bank(m)).then_inc(lin_evac[m % 2], 1)
                st["lin"] += 1
            all_out()
            for j in range(4):
                for c in range(DC):
                    src = lxb[:, c, 1 + j:1 + j + T]
                    w = vcol("conv_w", j * 8 + c)
                    if j == 0:
                        last = v.tensor_scalar(lxc[:, c, :], src, w, vcol("conv_b", c), ALU.mult, ALU.add)
                    else:
                        last = v.scalar_tensor_tensor(out=lxc[:, c, :], in0=src, scalar=w, in1=lxc[:, c, :],
                                                      op0=ALU.mult, op1=ALU.add)
                link(last)
            dve.sem_inc(h_ready, 1)
            split_low(lxc, xh[:], xl[:], u_od[-1] + 1)
            ahead(u_rg)
            ahead(u_rg + 1)
            dve.wait_ge(lru_i, 1)
            link(v.tensor_tensor(li, li, lxc, ALU.mult))
            dve.wait_ge(lru_t, 1)
            v.tensor_tensor(lr, lr, reset.unsqueeze(1).broadcast_to([P, DC, T]), ALU.max).then_inc(lru_t_max, 1)
            dve.wait_ge(lru_t_max, 1)
            link(v.tensor_scalar(lrc, lr, 1.0, None, ALU.add))
            link(v.reciprocal(lrc, lrc))
            dve.wait_ge(lru_root, 1)
            link(v.scalar_tensor_tensor(out=lxc, in0=lxc, scalar=2.0, in1=lrc, op0=ALU.mult, op1=ALU.mult))
            link(v.tensor_scalar(lr, lrc, 2.0, -1.0, ALU.mult, ALU.add))
            link(v.tensor_tensor(li, li, lxc, ALU.mult))
            for c in range(DC):
                last = v.tensor_tensor_scan(lrc[:, c, :], lr[:, c, :], li[:, c, :], 0.0, ALU.mult, ALU.add)
            link(last)
            dve.wait_ge(lru_gelu, 1)
            v.tensor_tensor(lgate, lgate, lrc, ALU.mult).then_inc(h_ready, 1)
            split_low(lgate, xh[:], xl[:], u_rg + 2)
            residual(u_odo)
            cross(1)
            norm(x[:], 8, D, "ffn1")
            gated(ffn[1][0], ffn[1][1], trio0[2], False)
            norm(x[:], 8, D, "final", dst=hbuf).then_inc(result, 1)

        @block.gpsimd
        def _(pool):
            pool.wait_ge(moe_starts, 1)
            pool.dma_start(mem, kview(t["memT"])).then_inc(second_landed, 16)
            pool.dma_start(c2, t["const2"]).then_inc(second_landed, 16)
            pool.dma_start(posi.bitcast(I32), t["positions_2"].partition_broadcast(P)).then_inc(second_landed, 16)


_BIG = ["w_in", "w_br_dil", "w_br_swa", "w_out", "w_e_gate", "w_e_up", "w_e_down", "ev_w_in_2", "ev_pool_w_2",
        "ev_w_q_up_2", "ev_w_kv_up_2", "ev_w_out_2", "od_w_in_2", "od_w_rgate_2", "od_w_igate_2", "od_w_out_2",
        "xa_w_q_2", "xa_w_kv_2", "xa_w_o_2", "ffn_w_gate_up_2", "ffn_w_down_2"]


def kernel(**inputs):
    import concourse.bacc as _bacc
    from concourse.bass_utils import run_bass_kernel_spmd as _run

    a = {k: np.asarray(v) for k, v in inputs.items()}
    arrays = {k: np.ascontiguousarray(a[k]) for k in _BIG}
    arrays["xT"] = np.ascontiguousarray(a["x"][0].T)
    arrays["memT"] = np.ascontiguousarray(a["mem_2"][0].T)
    arrays["positions_2"] = a["positions_2"].reshape(T)
    arrays["sinks"] = a["sinks"].reshape(SWA_HEADS)
    arrays["b_route"] = np.concatenate([a["b_group"][0], a["b_router"][0]])
    arrays["w_route"] = np.ascontiguousarray(
        np.concatenate([a["w_group"][0], a["w_router"][0]], 1).reshape(DC, P, 36).transpose(1, 0, 2).reshape(P, -1))
    cols = {"g_mix": a["g_mix"], "g_ffn": a["g_ffn"], "g_final": a["g_final"], "ev_norm": a["ev_norm_2"],
            "pool_scale": a["ev_pool_scale_2"], "q_norm": a["ev_q_norm_2"], "kv_norm": a["ev_kv_norm_2"],
            "od_norm": a["od_norm_2"], "conv_w": a["od_conv_w_2"], "conv_b": a["od_conv_b_2"],
            "b_r": a["od_b_rgate_2"], "b_i": a["od_b_igate_2"], "lam": a["od_lambda_2"],
            "xa_x0": a["xa_norm_x_2"][0], "xa_x1": a["xa_norm_x_2"][1], "xa_m0": a["xa_norm_mem_2"][0],
            "xa_m1": a["xa_norm_mem_2"][1], "ffn0": a["ffn_norm_2"][0], "ffn1": a["ffn_norm_2"][1],
            "final": a["final_norm_2"]}
    arrays["vecs"] = np.ascontiguousarray(np.concatenate([cols[n].reshape(-1, P).T for n in VECS], 1))
    arrays["const1"], arrays["const2"] = shape_constants()

    nc = _bacc.Bacc("TRN2", target_bir_lowering=False, num_devices=1)
    t = {k: nc.dram_tensor(f"{k}_dram", v.shape, mybir.dt.from_np(v.dtype), kind="ExternalInput").ap()
         for k, v in arrays.items()}
    out = nc.dram_tensor("out_dram", (D, T), F32, kind="ExternalOutput").ap()
    build(nc, t, out)
    r = _run(nc, [{f"{k}_dram": v for k, v in arrays.items()}], core_ids=[0])
    return np.ascontiguousarray(r.results[0]["out_dram"].T).reshape(1, T, D)
```

```python
from contextlib import ExitStack

import numpy as np

import concourse.bass as bass
from concourse import mybir

F32 = mybir.dt.float32
F32R = mybir.dt.float32r
I32 = mybir.dt.int32
ALU = mybir.AluOpType
ACT = mybir.ActivationFunctionType
AX = mybir.AxisListType

P = 128
T = 256
D = 1024
DC = D // P
HD = 64
GROUPS = ((128, 1), (512, 4), (2048, 16))
DIL_HEADS = 8
SWA_HEADS = 16
SWA_WINDOW = 128
N_EXP, N_GRP, D_EXP = 32, 4, 512
EXTRA = 2 * T // (P + 1)
TILES = N_EXP + EXTRA
D_FF = 2816
MLA_H, NOPE, ROPE, QK = 8, 64, 32, 96
XA_H, XA_HD = 4, 256
EPS = 1e-6
LRU_C = 8.0
FAR = -1e30

RAW = 6
HL = 3
UNIT = 2048

VECS = {}
_at = 0
for _n, _c in (("g_mix", 8), ("g_ffn", 8), ("g_final", 8), ("ev_norm", 8), ("pool_scale", 4), ("q_norm", 2),
               ("kv_norm", 1), ("od_norm", 8), ("conv_w", 32), ("conv_b", 8), ("b_r", 8), ("b_i", 8), ("lam", 8),
               ("xa_x0", 8), ("xa_x1", 8), ("xa_m0", 8), ("xa_m1", 8), ("ffn0", 8), ("ffn1", 8), ("final", 8)):
    VECS[_n] = (_at, _c)
    _at += _c
NV = _at


def shape_constants():
    q = np.arange(P)[:, None]
    c = np.arange(T)[None, :]
    back = (q + P - c).astype(np.float32)
    pats = []
    for window, dil in GROUPS:
        ok = (back >= 0) & (back <= (window // dil) * dil) & (back % dil == 0)
        pats.append(np.where(ok, back, 1e30))
    pats.append(np.where((back >= 0) & (back <= SWA_WINDOW - 1), back, 1e30))
    first = np.concatenate([*pats, np.eye(P),
                            np.broadcast_to(np.arange(N_GRP, 0, -1), (P, N_GRP)),
                            np.broadcast_to(np.arange(N_EXP, 0, -1), (P, N_EXP))], 1).astype(np.float32)
    causal = np.where(back >= 0, 0.0, FAR)
    swap = np.zeros((P, QK))
    for m in range(NOPE, QK):
        swap[m + 16 if m < NOPE + 16 else m - 16, m] = 1
    put = np.zeros((P, 2, QK))
    for r in range(ROPE):
        put[r, 0, NOPE + r] = 1
        put[(r + 16) % ROPE, 1, NOPE + r] = 1
    freq = np.zeros((P, 2))
    inv = np.float32(10000.0) ** (-np.arange(0, ROPE, 2, dtype=np.float32) / np.float32(ROPE))
    freq[NOPE:QK, 0] = np.concatenate([inv, inv])
    freq[NOPE:QK, 1] = np.repeat([-1.0, 1.0], 16)
    cnt = np.stack([1.0 / np.minimum(np.arange(T) + 1, w) for w in (2, 4, 8, 16)]).astype(np.float32)
    second = np.concatenate([causal, swap, put.reshape(P, -1), freq,
                             np.broadcast_to(cnt.reshape(1, -1), (P, 4 * T))], 1).astype(np.float32)
    route = np.concatenate([np.broadcast_to(np.arange(P), (P, P)), np.triu(np.ones((P, P)), 1),
                            np.broadcast_to(np.arange(N_EXP), (P, N_EXP))], 1).astype(np.float32)
    return first, second, route


def slopes(n):
    return (2.0 ** (-8.0 * np.arange(1, n + 1) / n)).astype(np.float32)


def build(nc, t, out):
    with ExitStack() as ctx:
        def sb(name, shape, dt=F32):
            return ctx.enter_context(nc.sbuf_tensor(name, shape, dt))

        def sem(name):
            return ctx.enter_context(nc.semaphore(name))

        arena_at = -(-nc.sbuf_base // 32) * 32
        arena = sb("arena", [P, 62 * T])

        def over(name, at, shape, dt):
            return nc.alloc_sbuf_tensor_at(name, shape, dt, offset=arena_at + 4 * at)

        raw = [sb(f"raw{i}", [P, UNIT]) for i in range(RAW)]
        whi = [sb(f"whi{i}", [P, UNIT], F32R) for i in range(HL)]
        wlo = [sb(f"wlo{i}", [P, UNIT], F32R) for i in range(HL)]
        xh = sb("xh", [P, DC, T], F32R)
        xl = sb("xl", [P, DC, T], F32R)
        ah = sb("ah", [P, 4, T], F32R)
        al = sb("al", [P, 4, T], F32R)
        x = sb("x", [P, DC, T])
        scr = sb("scr", [P, 9 * T])
        c1 = sb("c1", [P, 1024 + P + N_GRP + N_EXP])
        vec = sb("vec", [P, NV])
        rows = sb("rows", [P, SWA_HEADS + N_GRP + N_EXP])
        ones = sb("ones", [P, P])
        rstd = sb("rstd", [P, T])
        sm = sb("sm", [P, 3, 24])
        ps = ctx.enter_context(nc.psum_tensor("ps", [P, 8, 512], F32))

        pat = c1[:, 0:1024].rearrange("p (g k) -> p g k", g=4)
        ident = c1[:, 1024:1152]
        gkey = c1[:, 1152:1156]
        ekey = c1[:, 1156:1188]
        sink_row = rows[:, 0:16]
        bias_row = rows[:, 16:52]

        def vcol(name, c):
            a = VECS[name][0] + c
            return vec[:, a:a + 1]

        def area(at, *shape):
            n = int(np.prod(shape))
            v = arena[:, at:at + n]
            if len(shape) == 2:
                v = v.rearrange("p (a b) -> p a b", a=shape[0])
            elif len(shape) == 3:
                v = v.rearrange("p (a b c) -> p a b c", a=shape[0], b=shape[1])
            return v

        def chunks(at, n):
            return area(at, n, T)

        qd, kd = chunks(0, 12), chunks(12 * T, 12)
        vd = area(24 * T, 2, 1536)
        qs = chunks(36 * T, 8)
        ks, vs = chunks(44 * T, 1), area(45 * T, 2, P)
        sg = chunks(46 * T, 16)
        lg = area(40 * T, 2, 36)
        route = area(54 * T, 2 * P + N_EXP)
        slot_no, before, exp_no = route[:, 0:P], route[:, P:2 * P], route[:, 2 * P:]
        counts = area(56 * T, 3, N_EXP)
        rank = area(56 * T + 96, 2, TILES)
        gate = area(56 * T + 200, 2, TILES)
        picks = area(56 * T + 300, 8, N_EXP)
        pick_f, pick_i = area(58 * T + 100, 4), area(58 * T + 108, 4).bitcast(I32)
        weigh = area(58 * T + 116, 4, 2, N_EXP)
        slot_gate = area(60 * T, 2)
        gate_hl = over("gate_hl", 60 * T + 8, [P, 2, TILES, 2], F32R)
        pick = [over(f"pick{b}", 8 * T + b * T, [P, 2, P], F32R) for b in range(2)]
        turned = [over(f"turned{b}", 10 * T + b * 272, [P, 258], F32R) for b in range(2)]
        got_h = [over(f"got_h{b}", (13 + 8 * b) * T, [P, DC, P], F32R) for b in range(2)]
        got_l = [over(f"got_l{b}", (17 + 8 * b) * T, [P, DC, P], F32R) for b in range(2)]
        y_h = [over(f"y_h{b}", (29 + 4 * b) * T, [P, 512], F32R) for b in range(2)]
        y_l = [over(f"y_l{b}", (31 + 4 * b) * T, [P, 512], F32R) for b in range(2)]
        hid_h = [ah[:, 2 * b:2 * b + 2, :].rearrange("p a t -> p (a t)").rearrange("p (k s) -> p k s", k=4)
                 for b in range(2)]
        hid_l = [al[:, 2 * b:2 * b + 2, :].rearrange("p a t -> p (a t)").rearrange("p (k s) -> p k s", k=4)
                 for b in range(2)]
        tok_h = xh[:].rearrange("p c t -> p (c t)").rearrange("p (i d) -> p i d", i=2)
        tok_l = xl[:].rearrange("p c t -> p (c t)").rearrange("p (i d) -> p i d", i=2)
        rt = area(42 * T, 2, T)
        gates = rt[:, :, 192:224]
        mem = chunks(0, 8)
        c2 = area(45 * T, T + QK + 2 * QK + 2 + 4 * T)
        causal = c2[:, 0:T]
        swap = c2[:, T:T + QK]
        put = c2[:, T + QK:T + 3 * QK].rearrange("p (a b) -> p a b", a=2)
        freq = c2[:, T + 3 * QK:T + 3 * QK + 2]
        icnt = c2[:, T + 3 * QK + 2:].rearrange("p (g t) -> p g t", g=4)
        posi, posf = area(52 * T, T), area(53 * T, T)
        mem_rstd = area(52 * T, T)

        raw_landed = [sem(f"raw_landed{i}") for i in range(RAW)]
        hi_ready, lo_ready, unit_used = sem("hi_ready"), sem("lo_ready"), sem("unit_used")
        lin_evac = [sem("lin_evac0"), sem("lin_evac1")]
        consts_landed, x_landed, second_landed = sem("consts_landed"), sem("x_landed"), sem("second_landed")
        vec_landed, out_landed, x_again = sem("vec_landed"), sem("out_landed"), sem("x_again")
        ones_set = sem("ones_set")
        sq_ready, ss_ready, ms_ready, rstd_ready = sem("sq_ready"), sem("ss_ready"), sem("ms_ready"), sem("rstd_ready")
        h_ready, xh_ready, xl_ready = sem("h_ready"), sem("xh_ready"), sem("xl_ready")
        dve_step = sem("dve_step")
        silu_done, hid_ready, ah_ready, al_ready = (sem("silu_done"), sem("hid_ready"),
                                                                sem("ah_ready"), sem("al_ready"))
        att_scored, att_biased, att_max, att_exp, att_probs = (sem("att_scored"), sem("att_biased"), sem("att_max"),
                                                               sem("att_exp"), sem("att_probs"))
        att_turned, att_pt, att_mixed, att_out = sem("att_turned"), sem("att_pt"), sem("att_mixed"), sem("att_out")
        (pick_ready, turn_mm, turned_there, gath_mm, gath_act, gath_dve, r_silu, r_hid, r_hid_mm, r_hid_h, r_hid_l,
         r_y_h, r_y_l, ranks_go, ranks_mm, extra_there, gate_h_there, tok_mm, route_landed) = [sem(n) for n in (
             "pick_ready turn_mm turned_there gath_mm gath_act gath_dve r_silu r_hid r_hid_mm r_hid_h r_hid_l "
             "r_y_h r_y_l ranks_go ranks_mm extra_there gate_h_there tok_mm route_landed").split()]
        (mem_again, pool_in, pooled_there, mk_there, mk_rope_there, pool_step,
         kswap_mm, kswap_there, moe_starts, route_grp, route_grp_exp, route_two, route_two_exp, pool_out, kr_there, mk_mm, kr_mm, kr_turned, mq_there, mq_mm, mq_turned,
         angles, trig, kv_out, lru_ab, lru_a, lru_kept, lru_r, lru_x, lru_i, lam_abs, lam_exp, lam_scale, lru_t, lru_t_max, lru_root,
         lru_gelu, result) = [sem(n) for n in (
             "mem_again pool_in pooled_there mk_there mk_rope_there pool_step "
             "kswap_mm kswap_there moe_starts route_grp route_grp_exp route_two route_two_exp "
             "pool_out kr_there mk_mm kr_mm kr_turned mq_there mq_mm mq_turned "
             "angles trig kv_out lru_ab lru_a lru_kept lru_r lru_x lru_i lam_abs lam_exp lam_scale lru_t lru_t_max lru_root "
             "lru_gelu result").split()]

        units = []

        def kview(w):
            return w.rearrange("(k p) n -> p k n", p=P)

        def cut(w, kc, step, n=None):
            v = kview(w)
            n = n or w.shape[-1]
            first = len(units)
            for a in range(0, n, step):
                b = min(a + step, n)
                units.append((v[:, :, a:b], kc, b - a))
            return range(first, len(units))

        u_in = cut(t["w_in"][0], DC, 256)
        u_br = []
        wd_, ws_ = kview(t["w_br_dil"][0]), kview(t["w_br_swa"][0])
        for a in range(0, D, 256):
            u_br.append(len(units))
            units.append((wd_[:, :, a:a + 256], 4, 256))
            units.append((ws_[:, :, a:a + 256], 8, 256))
        u_out = cut(t["w_out"][0], DC, 256)
        u_router = len(units)
        units.append((t["w_route"].rearrange("p (k n) -> p k n", k=DC), DC, 36))
        moe = len(units)
        for j in range(6 * TILES):
            units.append(None)

        def second_attention(l):
            uq = cut(t["xa_w_q_2"][l], DC, 256)
            uo = cut(t["xa_w_o_2"][l], DC, 256)
            return uq, uo

        def gated_ffn(l):
            at = (len(units), D_FF // 256)
            for j in range(3 * (D_FF // 256)):
                units.append(None)
            return at

        u_ev = cut(t["ev_w_in_2"][0], DC, 256)
        u_qup = len(units)
        units.append((kview(t["ev_w_q_up_2"][0]), 2, 768))
        u_kvup = len(units)
        units.append((kview(t["ev_w_kv_up_2"][0]), 1, 1024))
        u_pool = len(units)
        units.append((t["ev_pool_w_2"][0].rearrange("g p n -> p g n"), 4, P))
        u_kv = [cut(t["xa_w_kv_2"][0], DC, 256)]
        u_evo = cut(t["ev_w_out_2"][0], DC, 256)
        u_xa = [second_attention(0)]
        ffn = [gated_ffn(0)]
        u_od = [*cut(t["od_w_in_2"][0][:, D:], DC, 256), *cut(t["od_w_in_2"][0][:, 0:D], DC, 256)]
        u_rg = len(units)
        for w in ("od_w_rgate_2", "od_w_igate_2"):
            units.append((t[w][0].rearrange("h (k p) n -> p (h k) n", p=P), DC, 256))
        u_kv.append(cut(t["xa_w_kv_2"][1], DC, 256))
        u_odo = cut(t["od_w_out_2"][0], DC, 256)
        u_xa.append(second_attention(1))
        ffn.append(gated_ffn(1))

        trio0 = [0, ffn[0][1]]

        def wview(buf, u, kc, n):
            return buf[u % HL][:, 0:kc * n].rearrange("p (k n) -> p k n", k=kc)

        def usize(u):
            return units[u][1] * units[u][2] if units[u] else UNIT

        def score_bank(step, g):
            at = g * T if len(step["scores"]) == 3 else g * 512
            return ps[:, at // 512, at % 512:at % 512 + step["nk"]]

        def attention(kind, l=0):
            steps = []
            if kind == "dil":
                sl = slopes(24)
                for hh in range(DIL_HEADS):
                    lo = HD * (hh % 2)
                    for qt in range(2):
                        nk = P * (qt + 1)
                        sc, bi, pv = [], [], []
                        for g in range(3):
                            c = 4 * g + hh // 2
                            sc.append([(qd[lo:lo + HD, c, qt * P:qt * P + P], kd[lo:lo + HD, c, 0:nk])])
                            bi.append((g, float(sl[8 * g + hh]) * 8.0))
                            for kt in range(qt + 1):
                                pv.append((vd[:, kt, (8 * g + hh) * HD:(8 * g + hh + 1) * HD], g, kt))
                        steps.append(dict(nk=nk, qt=qt, scores=sc, bias=bi, merged=True, sink=None, scale=0.125,
                                          pv=[(lo, 0, pv)], last=hh % 2 == 1 and qt == 1,
                                          y=[qd[:, hh // 2, :]]))
            elif kind == "swa":
                sl = slopes(SWA_HEADS)
                for c in range(8):
                    for qt in range(2):
                        nk = P * (qt + 1)
                        sc, bi, pv = [], [], []
                        for i in range(2):
                            h = 2 * c + i
                            kv = h // 8
                            kk = ks[:, 0, :] if kv == i else kswap[:, 0, :]
                            sc.append([(qs[HD * i:HD * i + HD, c, qt * P:qt * P + P], kk[HD * i:HD * i + HD, 0:nk])])
                            bi.append((3, float(sl[h]) * 8.0))
                            pv.append((HD * i, 0, [(vs[:, kt, kv * HD:(kv + 1) * HD], i, kt) for kt in range(qt + 1)]))
                        steps.append(dict(nk=nk, qt=qt, scores=sc, bias=bi, merged=False, sink=2 * c, scale=0.125,
                                          pv=pv, last=qt == 1, y=[qs[:, c, :]]))
            elif kind == "mla":
                for c in range(4):
                    for qt in range(2):
                        nk = P * (qt + 1)
                        sc, pv = [], []
                        for i in range(2):
                            h = 2 * c + i
                            sc.append([(mq[0:QK, h, qt * P:qt * P + P], mk[0:QK, h, 0:nk])])
                            pv.append((HD * i, 0, [(mv[:, kt, h * HD:(h + 1) * HD], i, kt) for kt in range(qt + 1)]))
                        steps.append(dict(nk=nk, qt=qt, scores=sc, bias="causal", merged=False, sink=None,
                                          scale=float(QK) ** -0.5, pv=pv, last=qt == 1, y=[my[:, c, :]]))
            else:
                for h in range(XA_H):
                    for qt in range(2):
                        sc = [[(xq[:, 2 * h + k, qt * P:qt * P + P], xk[:, 2 * h + k, :]) for k in range(2)]]
                        pv = [(0, k, [(xv[l][:, kt, (2 * h + k) * P:(2 * h + k + 1) * P], 0, kt) for kt in range(2)])
                              for k in range(2)]
                        steps.append(dict(nk=T, qt=qt, scores=sc, bias=None, merged=False, sink=None,
                                          scale=float(XA_HD) ** -0.5, pv=pv, last=qt == 1,
                                          y=[xq[:, 2 * h, :], xq[:, 2 * h + 1, :]]))
            return steps

        lat = chunks(25 * T, 3)
        kr = area(28 * T, T)
        cosr, sinr, turns, spare = area(43 * T, T), area(44 * T, T), area(41 * T, T), area(42 * T, T)
        pooled = [area(8 * T + 1088 * b, 4, 16 + T) for b in range(3)]
        ypool = chunks(21 * T, 4)
        mk, mv = chunks(8 * T, 8), area(16 * T, 2, 512)
        mq, my = chunks(33 * T, 8), chunks(41 * T, 4)
        xq, xk = chunks(8 * T, 8), chunks(0, 8)
        xv = [area(25 * T, 2, 1024), area(16 * T, 2, 1024)]
        lgate, lxb, lxc = chunks(8 * T, 8), area(16 * T, 8, T + 4), chunks(25 * T, 8)
        lr, li, lrc = chunks(33 * T, 8), chunks(41 * T, 8), chunks(54 * T, 8)
        reset, keep, lsm = area(49 * T, T), area(51 * T, T), area(50 * T, 10, 8)
        kswap = rstd[:, :].rearrange("p (a b) -> p a b", a=1)
        S = [scr[:, b * 768:(b + 1) * 768].rearrange("p (g k) -> p g k", g=3) for b in range(3)]
        PT_first = [x[:, 3 * b:3 * b + 3, :].rearrange("p c (b q) -> p (c b) q", q=P) for b in range(2)]
        PT_later = [area((54 + 2 * b) * T, 4, P) for b in range(2)]
        hbuf = scr[:, 0:2048].rearrange("p (c t) -> p c t", c=8)
        sil = [scr[:, 0:512], scr[:, 512:1024]]
        hid = [scr[:, 1024:1536], scr[:, 1536:2048]]

        def lru_in(part, h, k):
            return part[:, 2 * h + k, :]

        steps_a = attention("dil") + attention("swa")
        steps_m = attention("mla")
        steps_x = [attention("xa", l) for l in range(2)]

        block = ctx.enter_context(nc.Block())

        @block.sync
        def _(sp):
            sp.dma_start(x[:], kview(t["xT"])).then_inc(x_landed, 16)
            sp.dma_start(vec[:], t["vecs"]).then_inc(vec_landed, 16)

            def load(u, src, i=None, step=6):
                if i is not None:
                    sp.wait_ge(lo_ready, i * step + (u - RAW + 1))
                elif u >= RAW:
                    sp.wait_ge(lo_ready, u - RAW + 1)
                kc, n = src.shape[1], src.shape[2]
                sp.dma_start(raw[u % RAW][:, 0:kc * n].rearrange("p (k n) -> p k n", k=kc),
                             src).then_inc(raw_landed[u % RAW], 16)

            def load_gated(p0, n, g, uu, d):
                load(p0, g(0, 0))
                load(p0 + 1, uu(0, 0))
                with sp.Fori(0, (n - 1) // 2) as i:
                    load(p0 + 2, g(i, 1), i=i)
                    load(p0 + 3, uu(i, 1), i=i)
                    load(p0 + 4, d(i, 0), i=i)
                    load(p0 + 5, g(i, 2), i=i)
                    load(p0 + 6, uu(i, 2), i=i)
                    load(p0 + 7, d(i, 1), i=i)
                if n % 2 == 0:
                    load(p0 + 3 * n - 4, g(n // 2 - 1, 1))
                    load(p0 + 3 * n - 3, uu(n // 2 - 1, 1))
                    load(p0 + 3 * n - 2, d(n // 2 - 1, 0))
                    load(p0 + 3 * n - 1, d(n // 2 - 1, 1))
                else:
                    load(p0 + 3 * n - 1, d(n // 2, 0))

            wg = t["w_e_gate"][0].rearrange("e (h k p) n -> h e p k n", p=P, h=2)
            wu = t["w_e_up"][0].rearrange("e (h k p) n -> h e p k n", p=P, h=2)
            wdn = t["w_e_down"][0].rearrange("e (k p) (h n) -> h e p k n", p=P, h=2)

            def load_experts(p0):
                for a in range(2):
                    load(p0 + 2 * a, wg[a][0])
                    load(p0 + 2 * a + 1, wu[a][0])

                def tile(u, e, before, i=None):
                    for a in range(2):
                        load(u + 3 * a, wg[a][e], i=i, step=12)
                        load(u + 3 * a + 1, wu[a][e], i=i, step=12)
                        load(u + 3 * a + 2, wdn[a][before], i=i, step=12)

                with sp.Fori(0, (N_EXP - 2) // 2) as i:
                    tile(p0 + 4, i * 2 + 1, i * 2, i)
                    tile(p0 + 10, i * 2 + 2, i * 2 + 1, i)
                tile(p0 + 6 * (N_EXP - 1) - 2, N_EXP - 1, N_EXP - 2)
                sp.wait_ge(extra_there, 1)
                e = [sp.value_load(pick_i[0:1, j:j + 1], min_val=0, max_val=N_EXP - 1) for j in range(EXTRA)]
                for j in range(EXTRA):
                    tile(p0 + 6 * (N_EXP + j) - 2, e[j], e[j - 1] if j else N_EXP - 1)
                for a in range(2):
                    load(p0 + 6 * TILES - 2 + a, wdn[a][e[-1]])

            def ffn_cols(l, half):
                w = t["ffn_w_gate_up_2"][l][:, half * D_FF:(half + 1) * D_FF]
                first = kview(w[:, 0:256])
                rest = w[:, 256:].rearrange("(k p) (j b n) -> b j p k n", p=P, b=2, n=256)
                return lambda i, c: rest[c - 1][i] if c else first

            def ffn_rows(l):
                w = t["ffn_w_down_2"][l]
                pairs = w[0:D_FF - 256].rearrange("(j b k p) n -> b j p k n", p=P, k=2, b=2)
                last = kview(w[D_FF - 256:])
                return lambda i, c: last if isinstance(i, int) else pairs[c][i]

            u = 0
            while u < len(units):
                if u == moe:
                    load_experts(u)
                    u += 6 * TILES
                elif u in (ffn[0][0], ffn[1][0]):
                    l = 0 if u == ffn[0][0] else 1
                    load_gated(u, ffn[l][1], ffn_cols(l, 0), ffn_cols(l, 1), ffn_rows(l))
                    u += 3 * ffn[l][1]
                else:
                    load(u, units[u][0])
                    u += 1
                if u == RAW:
                    sp.dma_start(c1[:], t["const1"]).then_inc(consts_landed, 16)
                    sp.dma_start(rows[:, 0:16], t["sinks"].partition_broadcast(P)).then_inc(consts_landed, 16)
                    sp.dma_start(rows[:, 16:52], t["b_route"].partition_broadcast(P)).then_inc(consts_landed, 16)
            for b in range(4):
                sp.wait_ge(result, b + 1)
                sp.dma_start(out.rearrange("(c p) t -> p c t", p=P)[:, 2 * b:2 * b + 2, :],
                             hbuf[:, 2 * b:2 * b + 2, :]).then_inc(out_landed, 16)
            sp.wait_ge(out_landed, 64)

        @block.tensor
        def _(pe):
            st = dict(lin=0, sq=0, step=0, xl=0, y=0, fresh=False)

            def weights_in(u, i=None, step=6):
                add = 0 if i is None else i * step
                pe.wait_ge(hi_ready, add + u + 1)
                pe.wait_ge(lo_ready, add + u + 1)

            def triple(o, parts, first=True, last=True, group=True):
                fresh, st["fresh"] = st["fresh"], False
                mm = None
                for a, (wh, wl, h, l) in enumerate(parts):
                    if fresh and a % 2 == 0:
                        split_in()
                    mm = nc.tensor.matmul(o, wh, h, start=first and a == 0, stop=False, skip_group_check=not group)
                    nc.tensor.matmul(o, wh, l, start=False, stop=False, skip_group_check=not group)
                    mm = nc.tensor.matmul(o, wl, h, start=False, stop=last and a == len(parts) - 1,
                                          skip_group_check=not group)
                return mm

            def lin_bank():
                m = st["lin"]
                st["lin"] += 1
                if m >= 2:
                    pe.wait_ge(lin_evac[m % 2], m // 2)
                return ps[:, 6 + m % 2, :].rearrange("p (c t) -> p c t", c=2)

            def feature_unit(u, hsrc=None, lsrc=None, k0=0, half=None):
                hsrc, lsrc = hsrc or xh, lsrc or xl
                _, kc, n = units[u]
                if half != 1:
                    weights_in(u)
                    st["bank"] = lin_bank()
                o = st["bank"]
                wh, wl = wview(whi, u, kc, n), wview(wlo, u, kc, n)
                for b in range(-(-n // P)) if half is None else [half]:
                    w = min(P, n - b * P)
                    mm = triple(o[0:w, b, :], [(wh[:, k, b * P:b * P + w], wl[:, k, b * P:b * P + w],
                                                hsrc[:, k0 + k, :], lsrc[:, k0 + k, :]) for k in range(kc)])
                if half != 0:
                    mm.then_inc(unit_used, 1)

            def token_unit(u, a=0, n=None):
                _, kc, full = units[u]
                n = n or full
                weights_in(u)
                o = lin_bank()
                wh, wl = wview(whi, u, kc, full), wview(wlo, u, kc, full)
                fresh, st["fresh"] = st["fresh"], False
                for tt in range(2):
                    for k in range(kc):
                        if fresh and tt == 0 and k % 2 == 0:
                            split_in()
                        h, l = xh[:, k, tt * P:tt * P + P], xl[:, k, tt * P:tt * P + P]
                        nc.tensor.matmul(o[:, tt, 0:n], h, wh[:, k, a:a + n], start=k == 0, stop=False)
                        nc.tensor.matmul(o[:, tt, 0:n], l, wh[:, k, a:a + n], start=False, stop=False)
                        mm = nc.tensor.matmul(o[:, tt, 0:n], h, wl[:, k, a:a + n], start=False, stop=k == kc - 1)
                mm.then_inc(unit_used, 1)

            def squares(k, c, at=0, bank=5):
                st["sq"] += 1
                pe.wait_ge(sq_ready, st["sq"])
                for k in range(k, min(k + 2, c)):
                    mm = nc.tensor.matmul(ps[:, bank, 0:T], ones[:], hbuf[:, at + k, :], start=k == 0,
                                          stop=k == c - 1)
                if k == c - 1:
                    mm.then_inc(ss_ready, 1)

            def norm(c, split=True):
                for k in range(0, c, 2):
                    squares(k, c)
                st["fresh"] = split

            def residual(us, split=True):
                for a, u in enumerate(us):
                    feature_unit(u)
                    if a >= 1:
                        squares(2 * a - 2, DC)
                squares(DC - 2, DC)
                st["fresh"] = split

            def split_in():
                st["xl"] += 1
                pe.wait_ge(xl_ready, st["xl"])

            def all_out():
                for b in range(2):
                    pe.wait_ge(lin_evac[b], (st["lin"] + 1 - b) // 2)

            def score(s, step):
                if s >= 1:
                    pe.wait_ge(att_biased, s)
                for g, pairs in enumerate(step["scores"]):
                    o = score_bank(step, g)
                    for a, (q, k) in enumerate(pairs):
                        mm = nc.tensor.matmul(o, q, k, start=a == 0, stop=a == len(pairs) - 1)
                mm.then_inc(att_scored, 1)

            def turn(s, step):
                pe.wait_ge(att_probs, s + 1)
                if s >= 1:
                    pe.wait_ge(att_pt, s)
                b = 0
                for g in range(len(step["scores"])):
                    for kt in range(step["nk"] // P):
                        mm = nc.tensor.transpose(ps[:, 2 + b // 4, (b % 4) * P:(b % 4) * P + P],
                                                 S[s % 3][:, g, kt * P:kt * P + P], ident)
                        b += 1
                mm.then_inc(att_turned, 1)

            def mix(s, step, PT):
                y = st["y"]
                pe.wait_ge(att_pt, s + 1)
                if y >= 2:
                    pe.wait_ge(att_out, y - 1)
                per = step["nk"] // P
                for lo, k, pv in step["pv"]:
                    for a, (v, g, kt) in enumerate(pv):
                        w = v.shape[1]
                        mm = nc.tensor.matmul(ps[lo:lo + w, 4 + y % 2, k * T + step["qt"] * P:k * T + step["qt"] * P + P],
                                              v, PT[s % 2][:, g * per + kt, :], start=a == 0, stop=a == len(pv) - 1)
                mm.then_inc(att_mixed, 1)
                if step["last"]:
                    st["y"] += 1

            def attend(steps, PT, between=None):
                base = st["step"]
                score(base, steps[0])
                score(base + 1, steps[1])
                for a, step in enumerate(steps):
                    s = base + a
                    if between:
                        between(a)
                    if a + 2 < len(steps):
                        score(s + 2, steps[a + 2])
                    turn(s, step)
                    if a >= 1:
                        mix(s - 1, steps[a - 1], PT)
                mix(base + len(steps) - 1, steps[-1], PT)
                st["step"] += len(steps)

            def gated(p0, n, trio):
                def gu(u, j, jj, i=None):
                    for w, bank in ((u, 4 + (2 * j) % 4), (u + 1, 5 + (2 * j) % 4)):
                        weights_in(w, i)
                        if w == u and jj is not None:
                            pe.wait_ge(hid_ready, jj)
                        wh, wl = wview(whi, w, DC, T), wview(wlo, w, DC, T)
                        for b in range(2):
                            mm = triple(ps[:, bank, b * T:(b + 1) * T],
                                        [(wh[:, k, b * P:b * P + P], wl[:, k, b * P:b * P + P], xh[:, k, :],
                                          xl[:, k, :]) for k in range(DC)])
                        mm.then_inc(unit_used, 1)

                def down(u, j, jj, i=None, first=False, last=False):
                    weights_in(u, i)
                    pe.wait_ge(al_ready, jj)
                    wh, wl = wview(whi, u, 2, D), wview(wlo, u, 2, D)
                    for c in range(DC):
                        mm = triple(ps[:, c // 2, (c % 2) * T:(c % 2 + 1) * T],
                                    [(wh[:, k, c * P:c * P + P], wl[:, k, c * P:c * P + P],
                                      ah[:, 2 * (j % 2) + k, :], al[:, 2 * (j % 2) + k, :]) for k in range(2)],
                                    first=first and c % 2 == 0, last=last, group=False)
                    mm.then_inc(unit_used, 1)

                gu(p0, 0, None)
                gu(p0 + 2, 1, None)
                down(p0 + 4, 0, trio + 1, first=True)
                body = (n - 2) // 2
                with pe.Fori(0, body) as i:
                    gu(p0 + 5, 2, i * 2 + (trio + 1), i)
                    down(p0 + 7, 1, i * 2 + (trio + 2), i)
                    gu(p0 + 8, 3, i * 2 + (trio + 2), i)
                    down(p0 + 10, 2, i * 2 + (trio + 3), i)
                at = 2 + 2 * body
                while at < n:
                    gu(p0 + 3 * at - 1, at, trio + at - 1)
                    down(p0 + 3 * at + 1, at - 1, trio + at)
                    at += 1
                down(p0 + 3 * n - 1, n - 1, trio + n, last=True)

            def experts(p0):
                def gather(r, q, m, i=None):
                    add = 0 if i is None else i * 2
                    if r == 0:
                        if i is not None or m >= 1:
                            pe.wait_ge(turned_there, add + m)
                        pe.wait_ge(pick_ready, add + m + 1)
                    else:
                        pe.wait_ge(gath_act, (0 if i is None else i * 6) + 3 * m + r)
                    src = tok_h if r < 2 else tok_l
                    for k in range(4):
                        c = 4 * (r % 2) + k
                        for tt in range(2):
                            mm = nc.tensor.matmul(ps[:, 7, k * P:k * P + P], src[:, tt, c * P:c * P + P],
                                                  pick[q][:, tt, :], start=tt == 0, stop=tt == 1)
                    mm.then_inc(gath_mm, 1)

                def product(bank, u, act_h, act_l, first, last, i=None):
                    weights_in(u, i, 12)
                    wh, wl = wview(whi, u, 4, 512), wview(wlo, u, 4, 512)
                    o = ps[:, bank, :]
                    for k in range(4):
                        nc.tensor.matmul(o, act_h[:, k, :], wh[:, k, :], start=first and k == 0, stop=False)
                        nc.tensor.matmul(o, act_h[:, k, :], wl[:, k, :], start=False, stop=False)
                        mm = nc.tensor.matmul(o, act_l[:, k, :], wh[:, k, :], start=False, stop=last and k == 3)
                    mm.then_inc(unit_used, 1)

                def turn_pick(q, m, i=None):
                    add = 0 if i is None else i * 2
                    if i is not None or m >= 1:
                        pe.wait_ge(r_hid_l, add + m)
                    pe.wait_ge(pick_ready, add + m + 1)
                    for tt in range(2):
                        nc.tensor.transpose(ps[:, 7, tt * P:tt * P + P], pick[q][:, tt, :].bitcast(F32), ident)
                    for tt in range(2):
                        gates_ = gate_hl[:, tt, bass.ds(add + m, 1), :] if i is not None else gate_hl[:, tt, m:m + 1, :]
                        mm = nc.tensor.matmul(ps[:, 7, T:T + 2], pick[q][:, tt, :],
                                              gates_.rearrange("p a b -> p (a b)"), start=tt == 0, stop=tt == 1)
                    mm.then_inc(turn_mm, 1)

                def turn_hidden(q, m, i=None):
                    add = 0 if i is None else i * 2
                    pe.wait_ge(r_hid, add + m + 1)
                    pe.wait_ge(turned_there, add + m + 1)
                    pe.wait_ge(gath_dve, add + m + 2) if m < TILES - 1 else None
                    for k in range(4):
                        mm = nc.tensor.transpose(ps[:, 7, k * P:k * P + P], hid[q][:, k * P:k * P + P], ident)
                    mm.then_inc(r_hid_mm, 1)

                def down(half, u, q, m, i=None):
                    add = 0 if i is None else i * 2
                    pe.wait_ge(r_hid_l, add + m + 1)
                    if i is not None or 2 * m + half >= 1:
                        pe.wait_ge(r_y_l, (0 if i is None else i * 4) + 2 * m + half)
                    product(6, u, hid_h[q], hid_l[q], True, True, i)

                def scatter(half, q, m, i=None, first=False, last=False):
                    pe.wait_ge(r_y_l, (0 if i is None else i * 4) + 2 * m + half + 1)
                    for c in range(4):
                        o = ps[:, 2 * half + c // 2, (c % 2) * T:(c % 2 + 1) * T]
                        nc.tensor.matmul(o, y_h[half][:, c * P:c * P + P], turned[q][:, 0:T],
                                         start=first and c % 2 == 0, stop=False, skip_group_check=True)
                        mm = nc.tensor.matmul(o, y_l[half][:, c * P:c * P + P], turned[q][:, 0:T], start=False,
                                              stop=last, skip_group_check=True)
                    return mm

                def tile(u, q, m, i=None, older=True, first=False, more=True):
                    o = 1 - q
                    product(4, u, got_h[q][:, 0:4, :], got_l[q][:, 0:4, :], True, False, i)
                    if older:
                        scatter(1, q, m - 2, i, first=first)
                    turn_pick(q, m, i)
                    if more:
                        gather(0, o, m + 1, i)
                    product(5, u + 1, got_h[q][:, 0:4, :], got_l[q][:, 0:4, :], True, False, i)
                    if more:
                        gather(1, o, m + 1, i)
                    down(0, u + 2, o, m - 1, i)
                    product(4, u + 3, got_h[q][:, 4:8, :], got_l[q][:, 4:8, :], False, True, i)
                    if more:
                        gather(2, o, m + 1, i)
                    scatter(0, o, m - 1, i, first=not older)
                    product(5, u + 4, got_h[q][:, 4:8, :], got_l[q][:, 4:8, :], False, True, i)
                    if more:
                        gather(3, o, m + 1, i)
                    down(1, u + 5, o, m - 1, i)
                    turn_hidden(q, m, i)

                for r in range(4):
                    gather(r, 0, 0)
                pe.wait_ge(gath_dve, 1)
                product(4, p0, got_h[0][:, 0:4, :], got_l[0][:, 0:4, :], True, False)
                turn_pick(0, 0)
                gather(0, 1, 1)
                product(5, p0 + 1, got_h[0][:, 0:4, :], got_l[0][:, 0:4, :], True, False)
                gather(1, 1, 1)
                product(4, p0 + 2, got_h[0][:, 4:8, :], got_l[0][:, 4:8, :], False, True)
                gather(2, 1, 1)
                product(5, p0 + 3, got_h[0][:, 4:8, :], got_l[0][:, 4:8, :], False, True)
                gather(3, 1, 1)
                turn_hidden(0, 0)
                tile(p0 + 4, 1, 1, older=False)
                tile(p0 + 10, 0, 2, first=True)
                with pe.Fori(0, (N_EXP - 4) // 2) as i:
                    tile(p0 + 16, 1, 3, i)
                    tile(p0 + 22, 0, 4, i)
                for m in range(N_EXP - 1, TILES):
                    tile(p0 + 6 * m - 2, m % 2, m, more=m < TILES - 1)
                m = TILES
                q = (m - 1) % 2
                scatter(1, 1 - q, m - 2)
                down(0, p0 + 6 * m - 2, q, m - 1)
                down(1, p0 + 6 * m - 1, q, m - 1)
                scatter(0, q, m - 1, last=True)
                scatter(1, q, m - 1, last=True).then_inc(r_hid_mm, 1)

            pe.wait_ge(ones_set, 1)
            norm(8)
            for u in u_in[0:12]:
                feature_unit(u)
            for u in u_in[12:18]:
                token_unit(u)
            for u in u_in[18:22]:
                feature_unit(u)
            u = u_in[22]
            weights_in(u)
            o = lin_bank()
            wh, wl = wview(whi, u, DC, 256), wview(wlo, u, DC, 256)
            triple(o[:, 0, :], [(wh[:, k, 0:P], wl[:, k, 0:P], xh[:, k, :], xl[:, k, :]) for k in range(DC)])
            for tt in range(2):
                for k in range(DC):
                    h, l = xh[:, k, tt * P:tt * P + P], xl[:, k, tt * P:tt * P + P]
                    oo = o[:, 1, tt * P:tt * P + P]
                    nc.tensor.matmul(oo, h, wh[:, k, P:256], start=k == 0, stop=False)
                    nc.tensor.matmul(oo, l, wh[:, k, P:256], start=False, stop=False)
                    mm = nc.tensor.matmul(oo, h, wl[:, k, P:256], start=False, stop=k == DC - 1)
            mm.then_inc(unit_used, 1)
            all_out()
            pe.wait_ge(consts_landed, 48)
            nc.tensor.matmul(ps[0:HD, 5, 0:T], ident[:, HD:P], ks[:, 0, :], start=True, stop=True)
            nc.tensor.matmul(ps[HD:P, 5, 0:T], ident[:, 0:HD], ks[:, 0, :], start=True,
                             stop=True).then_inc(kswap_mm, 1)
            pe.wait_ge(kswap_there, 1)

            def gates_between(a):
                if a % 2 == 0:
                    feature_unit(u_in[23 + a // 4], half=a % 4 // 2)

            attend(steps_a, PT_first, gates_between)
            split_in()
            for u in u_br:
                feature_unit(u, ah, al)
                if u == u_br[0]:
                    st["fresh"] = True
                feature_unit(u + 1)
            st["fresh"] = True
            residual(u_out)
            token_unit(u_router)
            pe.wait_ge(ranks_go, 1)
            members = rt[:, :, 224:256]
            o = ps[:, 5, 0:3 * N_EXP].rearrange("p (a e) -> p a e", a=3)
            nc.tensor.matmul(o[:, 0, :], before, members[:, 0, :], start=True, stop=True)
            nc.tensor.matmul(o[:, 1, :], ones[:], members[:, 0, :], start=True, stop=False)
            nc.tensor.matmul(o[:, 1, :], before, members[:, 1, :], start=False, stop=True)
            nc.tensor.matmul(o[:, 2, :], ones[:], members[:, 0, :], start=True, stop=False)
            nc.tensor.matmul(o[:, 2, :], ones[:], members[:, 1, :], start=False, stop=True).then_inc(ranks_mm, 1)
            for tt in range(2):
                for c in range(DC):
                    at = tt * D + c * P
                    mm = nc.tensor.transpose(ps[:, at // 512, at % 512:at % 512 + P], hbuf[:, c, tt * P:tt * P + P],
                                             ident)
            mm.then_inc(h_ready, 1)
            split_in()
            experts(moe)
            norm(8, split=False)

            norm(8)
            for a, u in enumerate(u_ev):
                feature_unit(u)
                if a == 0:
                    norm(8, split=False)
            squares(0, 2)
            squares(0, 1, at=2, bank=4)
            st["fresh"] = True
            weights_in(u_qup)
            wh, wl = wview(whi, u_qup, 2, 768), wview(wlo, u_qup, 2, 768)
            for h in range(MLA_H):
                mm = triple(ps[0:QK, h // 2, (h % 2) * T:(h % 2 + 1) * T],
                            [(wh[:, k, h * QK:(h + 1) * QK], wl[:, k, h * QK:(h + 1) * QK], xh[:, k, :], xl[:, k, :])
                             for k in range(2)])
            mm.then_inc(unit_used, 1)
            pe.wait_ge(kr_there, 1)
            for a in range(2):
                mm = nc.tensor.matmul(ps[0:QK, 5, a * T:(a + 1) * T], put[0:ROPE, a, :], kr[0:ROPE, :],
                                      start=True, stop=True)
            mm.then_inc(kr_mm, 1)
            pe.wait_ge(kr_turned, 1)
            pe.wait_ge(mq_there, 1)
            all_out()
            for h in range(MLA_H):
                mm = nc.tensor.matmul(ps[0:QK, 4 + h // 2, (h % 2) * T:(h % 2 + 1) * T], swap[0:QK, :],
                                      mq[0:QK, h, :], start=True, stop=True)
            mm.then_inc(mq_mm, 1)
            weights_in(u_kvup)
            split_in()
            wh, wl = wview(whi, u_kvup, 1, 1024), wview(wlo, u_kvup, 1, 1024)
            for h in range(MLA_H):
                mm = triple(ps[0:NOPE, h // 2, (h % 2) * T:(h % 2 + 1) * T],
                            [(wh[:, 0, h * P:h * P + NOPE], wl[:, 0, h * P:h * P + NOPE], xh[:, 2, :], xl[:, 2, :])])
            mm.then_inc(mk_mm, 1)
            vh = wh[:, 0, :].rearrange("p (h n) -> p h n", h=MLA_H)[:, :, NOPE:P]
            vl = wl[:, 0, :].rearrange("p (h n) -> p h n", h=MLA_H)[:, :, NOPE:P]
            pe.wait_ge(mq_turned, 1)
            for tt in range(2):
                o = ps[:, 6 + tt, :].rearrange("p (h n) -> p h n", h=MLA_H)
                h, l = xh[:, 2, tt * P:tt * P + P], xl[:, 2, tt * P:tt * P + P]
                nc.tensor.matmul(o, h, vh, start=True, stop=False)
                nc.tensor.matmul(o, l, vh, start=False, stop=False)
                mm = nc.tensor.matmul(o, h, vl, start=False, stop=True)
            mm.then_inc(unit_used, 1)
            split_in()
            weights_in(u_pool)
            pe.wait_ge(kv_out, 1)
            wh, wl = wview(whi, u_pool, 4, P), wview(wlo, u_pool, 4, P)
            for half in range(2):
                o = lin_bank()
                for b in range(2):
                    g = 2 * half + b
                    mm = triple(o[:, b, :], [(wh[:, g, :], wl[:, g, :], ah[:, g, :], al[:, g, :])])
            mm.then_inc(unit_used, 1)
            pe.wait_ge(mk_there, 1)
            pe.wait_ge(mk_rope_there, 1)

            def memory_unit(l, a):
                if a < 4:
                    feature_unit(u_kv[l][a])
                else:
                    token_unit(u_kv[l][a])

            def memory_between(a):
                if a == 0:
                    split_in()
                memory_unit(0, a)

            attend(steps_m, PT_later, memory_between)
            st["fresh"] = True
            residual(u_evo)

            def cross(l):
                feature_unit(u_xa[l][0][0])
                feature_unit(u_xa[l][0][1])
                all_out()

                def queries_between(a):
                    if a in (2, 4):
                        all_out()
                    if a in (0, 2):
                        feature_unit(u_xa[l][0][2 + a // 2])

                attend(steps_x[l], PT_later, queries_between)
                st["fresh"] = True
                residual(u_xa[l][1])

            cross(0)
            gated(ffn[0][0], ffn[0][1], trio0[0])
            norm(8)
            for u in u_od:
                feature_unit(u)
            for a in range(2):
                u = u_rg + a
                weights_in(u)
                wh, wl = wview(whi, u, DC, 256), wview(wlo, u, DC, 256)
                for c in range(DC):
                    h = c // 2
                    if a == 0 and c % 2 == 0:
                        split_in()
                    if a == 1 and c == 4:
                        pe.wait_ge(lru_r, 1)
                    sh, sl = (ah, al) if h < 2 else (xh, xl)
                    at = (2 * a + c // 4) % 3 * 2 + c % 4 // 2
                    mm = triple(ps[:, at, (c % 2) * T:(c % 2 + 1) * T],
                                [(wh[:, 2 * h + k, (c % 2) * P:(c % 2) * P + P],
                                  wl[:, 2 * h + k, (c % 2) * P:(c % 2) * P + P], lru_in(sh, h, k),
                                  lru_in(sl, h, k)) for k in range(2)])
                mm.then_inc(unit_used, 1)
            st["fresh"] = True
            for a in range(8):
                memory_unit(1, a)
            st["fresh"] = True
            residual(u_odo)
            cross(1)
            gated(ffn[1][0], ffn[1][1], trio0[1])
            norm(8, split=False)

        @block.scalar
        def _(act):
            st = dict(hi=0, lin=0, step=0, split=0, norm=0)

            def hi(u, i=None, step=6):
                act.wait_ge(raw_landed[u % RAW], (0 if i is None else i * (step // 6 * 16)) + 16 * (u // RAW + 1))
                if i is not None or u >= HL:
                    act.wait_ge(unit_used, (0 if i is None else i * step) + (u - HL + 1))
                n = usize(u)
                nc.scalar.activation(whi[u % HL][:, 0:n], raw[u % RAW][:, 0:n], ACT.Copy).then_inc(hi_ready, 1)

            def ahead(u):
                while st["hi"] < min(u + HL, len(units)):
                    hi(st["hi"])
                    st["hi"] += 1

            def split_high(src, dst, used=None):
                st["split"] += 1
                act.wait_ge(h_ready, st["split"])
                if used is not None:
                    act.wait_ge(unit_used, used)
                nc.scalar.activation(dst, src, ACT.Copy).then_inc(xh_ready, 1)

            def split_highs(src, used):
                for k in range(0, DC, 2):
                    split_high(src[:, k:k + 2, :], xh[:, k:k + 2, :], used)

            def norm(c, split=True, scale=None, at=0):
                st["norm"] += 1
                act.wait_ge(ms_ready, st["norm"])
                s = rstd[:] if scale is None else scale
                nc.scalar.activation(s, s, ACT.Sqrt).then_inc(rstd_ready, 1)
                for k in range(at, at + c if split else 0, 2):
                    split_high(hbuf[:, k:min(k + 2, at + c), :], xh[:, k:min(k + 2, at + c), :])

            def evac(u, m, dst, func=ACT.Copy):
                act.wait_ge(unit_used, u + 1)
                nc.scalar.activation(dst, ps[:, 6 + m % 2, :].rearrange("p (c t) -> p c t", c=2),
                                     func).then_inc(lin_evac[m % 2], 1)

            def stage(us, dst=None, every=False, func=ACT.Copy):
                for a, u in enumerate(us):
                    ahead(u)
                    if dst and (every or st["lin"] % 2 == 0):
                        evac(u, st["lin"], dst(a), func)
                    st["lin"] += 1

            def exps(s, step):
                act.wait_ge(att_max, s + 1)
                b, nk = s % 3, step["nk"]
                n = len(step["scores"])
                if step["sink"] is not None:
                    for g in range(2):
                        nc.scalar.activation(sm[:, b, 12 + g:13 + g],
                                             sink_row[:, step["sink"] + g:step["sink"] + g + 1],
                                             ACT.Exp, bias=sm[:, b, 3 + g:4 + g])
                if step["merged"]:
                    last = nc.scalar.activation(S[b][:, 0:n, 0:nk], S[b][:, 0:n, 0:nk], ACT.Exp,
                                                bias=sm[:, b, 3:4], scale=step["scale"], accum_out=sm[:, b, 6:7])
                else:
                    for g in range(n):
                        last = nc.scalar.activation(S[b][:, g, 0:nk], S[b][:, g, 0:nk], ACT.Exp,
                                                    bias=sm[:, b, 3 + g:4 + g], scale=step["scale"],
                                                    accum_out=sm[:, b, 6 + g:7 + g])
                last.then_inc(att_exp, 1)

            def copy_turned(s, step, PT):
                act.wait_ge(att_turned, s + 1)
                if s >= 2:
                    act.wait_ge(att_mixed, s - 1)
                n = len(step["scores"]) * step["nk"] // P
                last = nc.scalar.activation(PT[s % 2][:, 0:min(n, 4), :],
                                            ps[:, 2, 0:min(n, 4) * P].rearrange("p (b q) -> p b q", q=P), ACT.Copy)
                if n > 4:
                    last = nc.scalar.activation(PT[s % 2][:, 4:n, :],
                                                ps[:, 3, 0:(n - 4) * P].rearrange("p (b q) -> p b q", q=P), ACT.Copy)
                last.then_inc(att_pt, 1)

            def attend(steps, PT, between=None):
                base = st["step"]
                exps(base, steps[0])
                for a, step in enumerate(steps):
                    if a + 1 < len(steps):
                        exps(base + a + 1, steps[a + 1])
                    copy_turned(base + a, step, PT)
                    if between:
                        between(a)
                st["step"] += len(steps)

            def experts(p0):
                def gathered(r, q, m, i=None):
                    act.wait_ge(gath_mm, (0 if i is None else i * 8) + 4 * m + r + 1)
                    dst = (got_h if r < 2 else got_l)[q][:, 4 * (r % 2):4 * (r % 2) + 4, :]
                    nc.scalar.activation(dst, ps[:, 7, :].rearrange("p (k s) -> p k s", k=4),
                                         ACT.Copy).then_inc(gath_act, 1)

                def turned_out(q, m, i=None):
                    act.wait_ge(turn_mm, (0 if i is None else i * 2) + m + 1)
                    nc.scalar.activation(turned[q][:], ps[:, 7, 0:T + 2], ACT.Copy).then_inc(turned_there, 1)

                def silu(u, q, i=None):
                    act.wait_ge(unit_used, (0 if i is None else i * 12) + u)
                    nc.scalar.activation(sil[q], ps[:, 4, :], ACT.Silu).then_inc(r_silu, 1)

                def y_high(half, u, i=None):
                    act.wait_ge(unit_used, (0 if i is None else i * 12) + u + 1)
                    nc.scalar.activation(y_h[half][:], ps[:, 6, :], ACT.Copy).then_inc(r_y_h, 1)

                def hidden_high(q, m, i=None):
                    act.wait_ge(r_hid_mm, (0 if i is None else i * 2) + m + 1)
                    nc.scalar.activation(hid_h[q], ps[:, 7, :].rearrange("p (k s) -> p k s", k=4),
                                         ACT.Copy).then_inc(r_hid_h, 1)

                def tile(u, q, m, i=None, more=True):
                    o = 1 - q
                    turned_out(q, m, i)
                    if more:
                        gathered(0, o, m + 1, i)
                    hi(u + 3, i, 12)
                    if more:
                        gathered(1, o, m + 1, i)
                    hi(u + 4, i, 12)
                    y_high(0, u + 2, i)
                    hi(u + 5, i, 12)
                    if more:
                        gathered(2, o, m + 1, i)
                    hi(u + 6, i, 12)
                    silu(u + 5, q, i)
                    hi(u + 7, i, 12)
                    y_high(1, u + 5, i)
                    hidden_high(q, m, i)
                    hi(u + 8, i, 12)

                for r in range(3):
                    gathered(r, 0, 0)
                ahead(p0)
                turned_out(0, 0)
                gathered(0, 1, 1)
                hi(p0 + 3)
                gathered(1, 1, 1)
                hi(p0 + 4)
                gathered(2, 1, 1)
                hi(p0 + 5)
                silu(p0 + 4, 0)
                hidden_high(0, 0)
                hi(p0 + 6)
                for m in (1, 2):
                    tile(p0 + 6 * m - 2, m % 2, m)
                with act.Fori(0, (N_EXP - 4) // 2) as i:
                    tile(p0 + 16, 1, 3, i)
                    tile(p0 + 22, 0, 4, i)
                for m in range(N_EXP - 1, TILES):
                    tile(p0 + 6 * m - 2, m % 2, m, more=m < TILES - 1)
                y_high(0, p0 + 6 * TILES - 2)
                y_high(1, p0 + 6 * TILES - 1)
                st["hi"] = p0 + 6 * TILES + 1

            def gated(p0, n, trio):
                def gate(u, j, free, i=None):
                    act.wait_ge(unit_used, (0 if i is None else i * 6) + (u + 2))
                    if free is not None:
                        act.wait_ge(hid_ready, free)
                    nc.scalar.activation(sil[j % 2], ps[:, 4 + (2 * j) % 4, :], ACT.Silu).then_inc(silu_done, 1)

                def high(j, ready, used=None, i=None):
                    act.wait_ge(hid_ready, ready)
                    if used is not None:
                        act.wait_ge(unit_used, (0 if i is None else i * 6) + used)
                    nc.scalar.activation(ah[:, 2 * (j % 2):2 * (j % 2) + 2, :],
                                         hid[j % 2].rearrange("p (c t) -> p c t", c=2), ACT.Copy).then_inc(ah_ready, 1)

                ahead(p0)
                gate(p0, 0, None)
                hi(p0 + 3)
                high(0, trio + 1)
                hi(p0 + 4)
                hi(p0 + 5)
                gate(p0 + 2, 1, None)
                hi(p0 + 6)
                high(1, trio + 2)
                body = (n - 2) // 2
                with act.Fori(0, body) as i:
                    for j in (2, 3):
                        u = p0 + 3 * j - 1
                        hi(u + 2, i)
                        hi(u + 3, i)
                        gate(u, j, i * 2 + (trio + j - 1), i)
                        hi(u + 4, i)
                        high(j, i * 2 + (trio + j + 1), u, i)
                for j in range(2 + 2 * body, n):
                    u = p0 + 3 * j - 1
                    hi(u + 2)
                    hi(u + 3)
                    gate(u, j, trio + j - 1)
                    if u + 4 < len(units):
                        hi(u + 4)
                    high(j, trio + j + 1, u)
                st["hi"] = min(p0 + 3 * n + 1, len(units))

            hi(0)
            hi(1)
            st["hi"] = 2
            norm(8)
            stage(u_in[0:6], lambda a: qd[:, 2 * a:2 * a + 2, :])
            stage(u_in[6:12], lambda a: kd[:, 2 * a:2 * a + 2, :])
            stage(u_in[12:18], lambda a: vd[:, :, a * 256:(a + 1) * 256])
            stage(u_in[18:22], lambda a: qs[:, 2 * a:2 * a + 2, :])
            stage(u_in[22:23])

            def gates_out(a):
                k = a // 4
                if a == 21:
                    split_high(qd[:, 0:4, :], ah[:])
                if a % 4 == 2:
                    u = u_in[23 + k]
                    ahead(u)
                    evac(u, st["lin"], sg[:, 2 * k:2 * k + 2, :], ACT.Sigmoid)
                    st["lin"] += 1

            attend(steps_a, PT_first, gates_out)
            split_highs(qs, u_in[-1] + 1)
            stage(range(u_br[0], u_br[-1] + 2))
            split_highs(hbuf, u_br[-1] + 2)
            stage(u_out)
            norm(8)
            stage([u_router])
            act.wait_ge(route_grp, 1)
            nc.scalar.activation(rt[:, :, 4:8], rt[:, :, 4:8], ACT.Exp).then_inc(route_grp_exp, 1)
            act.wait_ge(route_two, 1)
            nc.scalar.activation(rt[:, :, 24:25], rt[:, :, 23:24], ACT.Exp).then_inc(route_two_exp, 1)
            act.wait_ge(ranks_go, 2)
            nc.scalar.activation(gate_hl[:, :, :, 0], gate, ACT.Copy).then_inc(gate_h_there, 1)
            split_high(ps[:, 0:4, :], xh[:].rearrange("p (b c) t -> p b (c t)", b=4), u_router + 1)
            experts(moe)
            norm(8, split=False)
            act.wait_ge(angles, 1)
            nc.scalar.activation(sinr[0:QK, :], sinr[0:QK, :], ACT.Sin)
            nc.scalar.activation(cosr[0:QK, :], cosr[0:QK, :], ACT.Sin).then_inc(trig, 1)
            norm(8)
            stage(u_ev[0:2])
            norm(8, split=False, scale=mem_rstd)
            stage(u_ev[2:])
            norm(2)
            norm(1, at=2)
            ahead(u_qup)
            act.wait_ge(unit_used, u_qup + 1)
            nc.scalar.activation(mq[0:QK, :, :], ps[0:QK, 0:4, :].rearrange("p b (c t) -> p (b c) t", c=2),
                                 ACT.Copy).then_inc(mq_there, 1)
            ahead(u_kvup)
            act.wait_ge(mk_mm, 1)
            act.wait_ge(pooled_there, 1)
            nc.scalar.activation(mk[0:NOPE, :, :], ps[0:NOPE, 0:4, :].rearrange("p b (c t) -> p (b c) t", c=2),
                                 ACT.Copy).then_inc(mk_there, 1)
            split_high(ypool, ah[:])
            ahead(u_pool)
            split_high(mem, xh[:], u_kvup + 1)
            st["lin"] += 2

            def memory_out(l, a):
                u = u_kv[l][a]
                ahead(u)
                evac(u, st["lin"], xk[:, 2 * a:2 * a + 2, :] if a < 4 else xv[l][:, :, (a - 4) * 256:(a - 3) * 256])
                st["lin"] += 1

            attend(steps_m, PT_later, lambda a: memory_out(0, a))
            for src, at in ((ypool, 0), (my, 4)):
                for k in (0, 2):
                    split_high(src[:, k:k + 2, :], xh[:, at + k:at + k + 2, :], u_kv[0][-1] + 1)
            stage(u_evo)

            def cross(l):
                norm(8)
                uq = u_xa[l][0]
                stage(uq[0:2], lambda a: xq[:, 2 * a:2 * a + 2, :], every=True)

                def queries_out(a):
                    if a in (0, 2):
                        h = 2 + a // 2
                        ahead(uq[h])
                        evac(uq[h], st["lin"], xq[:, 2 * h:2 * h + 2, :])
                        st["lin"] += 1

                attend(steps_x[l], PT_later, queries_out)
                split_highs(xq, uq[-1] + 1)
                stage(u_xa[l][1])

            cross(0)
            norm(8)
            gated(ffn[0][0], ffn[0][1], trio0[0])
            act.wait_ge(lam_abs, 1)
            nc.scalar.activation(lsm[:, 1, :], lsm[:, 0, :], ACT.Exp, scale=-1.0).then_inc(lam_exp, 1)
            norm(8)
            for a in range(4):
                stage(u_od[a:a + 1])
                if a in (2, 3):
                    two = slice(2 * a - 4, 2 * a - 2)
                    split_high(lxc[:, two, :], ah[:, two, :])
            stage(u_od[4:8], lambda a: lgate[:, 2 * a:2 * a + 2, :], every=True, func=ACT.Gelu_apprx_tanh)
            for a in (2, 3):
                two = slice(2 * a, 2 * a + 2)
                split_high(lxc[:, two, :], xh[:, two, :], u_od[-1] + 1)
            ahead(u_rg)
            act.wait_ge(unit_used, u_rg + 1)
            for c in range(DC):
                last = nc.scalar.activation(lr[:, c, :], ps[:, c // 2, (c % 2) * T:(c % 2 + 1) * T], ACT.Sigmoid,
                                            bias=vcol("b_r", c))
            last.then_inc(lru_r, 1)
            ahead(u_rg + 1)
            act.wait_ge(unit_used, u_rg + 2)
            for c in range(DC):
                at = (2 + c // 4) % 3 * 2 + c % 4 // 2
                last = nc.scalar.activation(li[:, c, :], ps[:, at, (c % 2) * T:(c % 2 + 1) * T], ACT.Sigmoid,
                                            bias=vcol("b_i", c))
            last.then_inc(lru_i, 1)
            split_highs(mem, u_rg + 2)
            act.wait_ge(lam_scale, 1)
            act.wait_ge(lru_r, 1)
            for c in range(DC):
                last = nc.scalar.activation(lrc[:, c, :], lr[:, c, :], ACT.Exp, scale=lsm[:, 6, c:c + 1])
            last.then_inc(lru_a, 1)
            ahead(u_kv[1][0])
            for c in range(DC):
                last = nc.scalar.activation(lr[:, c, :], lr[:, c, :], ACT.Tanh, scale=lsm[:, 7, c:c + 1])
            last.then_inc(lru_t, 1)
            memory_out(1, 0)
            act.wait_ge(lru_t_max, 1)
            nc.scalar.activation(lr, lr, ACT.Sqrt).then_inc(lru_root, 1)
            for a in range(1, 8):
                memory_out(1, a)
            split_highs(lgate, u_kv[1][-1] + 1)
            stage(u_odo)
            cross(1)
            norm(8)
            gated(ffn[1][0], ffn[1][1], trio0[1])
            norm(8, split=False)

        @block.vector
        def _(dve):
            st = dict(lo=0, lin=0, step=0, split=0, norm=0, chain=0, y=0)
            v = nc.vector

            def link(ins):
                st["chain"] += 1
                ins.then_inc(dve_step, 1)
                dve.wait_ge(dve_step, st["chain"])

            def lo(u, i=None, step=6):
                dve.wait_ge(hi_ready, (0 if i is None else i * step) + (u + 1))
                if i is not None or u >= HL:
                    dve.wait_ge(unit_used, (0 if i is None else i * step) + (u - HL + 1))
                n = usize(u)
                v.tensor_tensor(wlo[u % HL][:, 0:n], raw[u % RAW][:, 0:n], whi[u % HL][:, 0:n].bitcast(F32),
                                ALU.subtract).then_inc(lo_ready, 1)

            def ahead(u):
                while st["lo"] < min(u + HL, len(units)):
                    lo(st["lo"])
                    st["lo"] += 1

            def split_low(src, high, low, used=None):
                st["split"] += 1
                dve.wait_ge(xh_ready, st["split"])
                if used is not None:
                    dve.wait_ge(unit_used, used)
                v.tensor_tensor(low, src, high.bitcast(F32), ALU.subtract).then_inc(xl_ready, 1)

            def split_lows(src, used):
                for k in range(0, DC, 2):
                    split_low(src[:, k:k + 2, :], xh[:, k:k + 2, :], xl[:, k:k + 2, :], used)

            def square(src, a, b):
                v.tensor_tensor(hbuf[:, a:b, :], src[:, a:b, :], src[:, a:b, :], ALU.mult).then_inc(sq_ready, 1)

            def norm(src, c, width, gain, dst=None, squared=False, done=None, at=0, bank=5, between=None):
                for k in range(0, 0 if squared else c, 2):
                    square(src, k, min(k + 2, c))
                root(width, rstd[:], bank)
                if between:
                    between()
                dve.wait_ge(rstd_ready, st["norm"])
                to = hbuf if dst is None else dst
                for k in range(at, at + c, 2):
                    last = scaled(to, src, k, min(k + 2, at + c), gain, rstd[:], k - at, at)
                    if dst is None:
                        last.then_inc(h_ready, 1)
                        if k >= at + 2:
                            split_low(hbuf[:, k - 2:k, :], xh[:, k - 2:k, :], xl[:, k - 2:k, :])
                    elif done is not None:
                        last.then_inc(done, 1)
                if dst is None:
                    split_low(hbuf[:, k:at + c, :], xh[:, k:at + c, :], xl[:, k:at + c, :])
                return last

            def root(width, to, bank=5):
                st["norm"] += 1
                dve.wait_ge(ss_ready, st["norm"])
                link(v.tensor_scalar(to, ps[:, bank, 0:T], 1.0 / width, EPS, ALU.mult, ALU.add))
                v.reciprocal(to, to).then_inc(ms_ready, 1)

            def scaled(to, src, a, b, gain, scale, g=None, off=0):
                g = a if g is None else g
                for j in range(a, b):
                    last = v.scalar_tensor_tensor(out=to[:, j, :], in0=src[:, j, :], scalar=vcol(gain, g + j - a),
                                                  in1=scale, op0=ALU.mult, op1=ALU.mult)
                return last

            def bank(m):
                return ps[:, 6 + m % 2, :].rearrange("p (c t) -> p c t", c=2)

            def stage(us, dst=None):
                for a, u in enumerate(us):
                    ahead(u)
                    m = st["lin"]
                    if dst and m % 2 == 1:
                        dve.wait_ge(unit_used, u + 1)
                        v.tensor_copy(dst(a), bank(m)).then_inc(lin_evac[m % 2], 1)
                    st["lin"] += 1

            def all_out():
                for b in range(2):
                    dve.wait_ge(lin_evac[b], (st["lin"] + 1 - b) // 2)

            def add_sums():
                for b in range(4):
                    two = x[:, 2 * b:2 * b + 2, :]
                    link(v.tensor_tensor(two, ps[:, b, :].rearrange("p (c t) -> p c t", c=2), two, ALU.add))
                    square(x, 2 * b, 2 * b + 2)

            def residual(us):
                for a, u in enumerate(us):
                    ahead(u)
                    m = st["lin"]
                    dve.wait_ge(unit_used, u + 1)
                    v.tensor_tensor(x[:, 2 * a:2 * a + 2, :], bank(m), x[:, 2 * a:2 * a + 2, :],
                                    ALU.add).then_inc(lin_evac[m % 2], 1)
                    dve.wait_ge(lin_evac[m % 2], m // 2 + 1)
                    square(x, 2 * a, 2 * a + 2)
                    st["lin"] += 1
                all_out()

            def bias_max(s, step):
                dve.wait_ge(att_scored, s + 1)
                if s >= 3:
                    dve.wait_ge(att_turned, s - 2)
                b, nk, n = s % 3, step["nk"], len(step["scores"])
                for g in range(n):
                    src = score_bank(step, g)
                    dst = S[b][:, g, 0:nk]
                    if step["bias"] is None:
                        last = v.tensor_copy(dst, src)
                    elif step["bias"] == "causal":
                        last = v.tensor_tensor(dst, src, causal[:, T - nk:T], ALU.add)
                    else:
                        pi, slope = step["bias"][g]
                        last = v.scalar_tensor_tensor(out=dst, in0=pat[:, pi, T - nk:T], scalar=-slope, in1=src,
                                                      op0=ALU.mult, op1=ALU.add)
                last.then_inc(att_biased, 1)
                dve.wait_ge(att_biased, s + 1)
                if step["merged"]:
                    link(v.tensor_reduce(sm[:, b, 0:1], S[b][:, 0:n, 0:nk], AX.XY, ALU.max))
                    n = 1
                else:
                    link(v.tensor_reduce(sm[:, b, 0:n], S[b][:, 0:n, 0:nk], AX.X, ALU.max))
                if step["sink"] is not None:
                    link(v.scalar_tensor_tensor(out=sm[:, b, 0:n], in0=sm[:, b, 0:n], scalar=step["scale"],
                                                in1=sink_row[:, step["sink"]:step["sink"] + n],
                                                op0=ALU.mult, op1=ALU.max))
                    v.tensor_scalar(sm[:, b, 3:3 + n], sm[:, b, 0:n], -1.0, None, ALU.mult).then_inc(att_max, 1)
                else:
                    v.tensor_scalar(sm[:, b, 3:3 + n], sm[:, b, 0:n], -step["scale"], None,
                                    ALU.mult).then_inc(att_max, 1)

            def probs(s, step):
                dve.wait_ge(att_exp, s + 1)
                b, nk, n = s % 3, step["nk"], len(step["scores"])
                k = 1 if step["merged"] else n
                if step["sink"] is not None:
                    link(v.tensor_tensor(sm[:, b, 6:6 + k], sm[:, b, 6:6 + k], sm[:, b, 12:12 + k], ALU.add))
                link(v.reciprocal(sm[:, b, 9:9 + k], sm[:, b, 6:6 + k]))
                if step["merged"]:
                    last = v.tensor_scalar(S[b][:, 0:n, 0:nk], S[b][:, 0:n, 0:nk], sm[:, b, 9:10], None, ALU.mult)
                else:
                    for g in range(n):
                        last = v.tensor_scalar(S[b][:, g, 0:nk], S[b][:, g, 0:nk], sm[:, b, 9 + g:10 + g], None,
                                               ALU.mult)
                last.then_inc(att_probs, 1)

            def attend(steps, y_of, between=None):
                base = st["step"]

                def out(a):
                    step = steps[a]
                    if step["last"]:
                        dve.wait_ge(att_mixed, base + a + 1)
                        w = len(step["y"])
                        v.tensor_copy(y_of(st["yk"], w), ps[:, 4 + st["y"] % 2, 0:w * T].rearrange("p (c t) -> p c t",
                                                                                    c=w)).then_inc(att_out, 1)
                        st["y"] += 1
                        st["yk"] += w

                st["yk"] = 0
                bias_max(base, steps[0])
                bias_max(base + 1, steps[1])
                for a, step in enumerate(steps):
                    probs(base + a, step)
                    if a >= 2:
                        out(a - 2)
                    if a + 2 < len(steps):
                        bias_max(base + a + 2, steps[a + 2])
                    if between:
                        between(a)
                out(len(steps) - 2)
                out(len(steps) - 1)
                dve.wait_ge(att_out, st["y"])
                st["step"] += len(steps)

            def experts(p0):
                def choose(q, m, i=None):
                    add = 0 if i is None else i * 2
                    if i is not None or m >= 2:
                        dve.wait_ge(turn_mm, add + m - 1)
                    for tt in range(2):
                        at = rank[:, tt, bass.ds(add + m, 1)] if i is not None else rank[:, tt, m:m + 1]
                        last = v.tensor_scalar(pick[q][:, tt, :], slot_no, at, None, ALU.is_equal)
                    last.then_inc(pick_ready, 1)

                def gathered(q, m, i=None):
                    dve.wait_ge(gath_mm, (0 if i is None else i * 8) + 4 * m + 4)
                    v.tensor_copy(got_l[q][:, 4:8, :], ps[:, 7, :].rearrange("p (k s) -> p k s",
                                                                          k=4)).then_inc(gath_dve, 1)

                def gate_of_slots(q, m, i=None):
                    dve.wait_ge(turned_there, (0 if i is None else i * 2) + m + 1)
                    v.tensor_reduce(slot_gate[:, q:q + 1], turned[q][:, T:T + 2].bitcast(F32), AX.X,
                                    ALU.add)

                def hidden(u, q, m, i=None):
                    add = 0 if i is None else i * 2
                    dve.wait_ge(unit_used, (0 if i is None else i * 12) + u)
                    dve.wait_ge(r_silu, add + m + 1)
                    v.scalar_tensor_tensor(out=hid[q], in0=ps[:, 5, :], scalar=slot_gate[:, q:q + 1], in1=sil[q],
                                           op0=ALU.mult, op1=ALU.mult).then_inc(r_hid, 1)

                def y_low(half, m, i=None):
                    dve.wait_ge(r_y_h, (0 if i is None else i * 4) + 2 * m + half + 1)
                    v.tensor_tensor(y_l[half][:], ps[:, 6, :], y_h[half][:].bitcast(F32),
                                    ALU.subtract).then_inc(r_y_l, 1)

                def hidden_low(q, m, i=None):
                    dve.wait_ge(r_hid_h, (0 if i is None else i * 2) + m + 1)
                    v.tensor_tensor(hid_l[q], ps[:, 7, :].rearrange("p (k s) -> p k s", k=4), hid_h[q].bitcast(F32),
                                    ALU.subtract).then_inc(r_hid_l, 1)

                def tile(u, q, m, i=None, more=True, after=True):
                    o = 1 - q
                    gate_of_slots(q, m, i)
                    lo(u + 3, i, 12)
                    if after:
                        choose(q, m + 2, i)
                    lo(u + 4, i, 12)
                    y_low(0, m - 1, i)
                    lo(u + 5, i, 12)
                    lo(u + 6, i, 12)
                    if more:
                        gathered(o, m + 1, i)
                    hidden(u + 5, q, m, i)
                    lo(u + 7, i, 12)
                    y_low(1, m - 1, i)
                    hidden_low(q, m, i)
                    lo(u + 8, i, 12)

                choose(0, 0)
                choose(1, 1)
                gathered(0, 0)
                ahead(p0)
                gate_of_slots(0, 0)
                lo(p0 + 3)
                choose(0, 2)
                lo(p0 + 4)
                lo(p0 + 5)
                gathered(1, 1)
                hidden(p0 + 4, 0, 0)
                hidden_low(0, 0)
                lo(p0 + 6)
                for m in (1, 2):
                    tile(p0 + 6 * m - 2, m % 2, m)
                with dve.Fori(0, (N_EXP - 4) // 2) as i:
                    tile(p0 + 16, 1, 3, i)
                    tile(p0 + 22, 0, 4, i)
                for m in range(N_EXP - 1, TILES):
                    tile(p0 + 6 * m - 2, m % 2, m, more=m < TILES - 1, after=m < TILES - 2)
                y_low(0, TILES - 1)
                y_low(1, TILES - 1)
                st["lo"] = p0 + 6 * TILES + 1
                dve.wait_ge(r_hid_mm, TILES + 1)
                add_sums()

            def gated(p0, n, trio):
                def hidden(u, j, g, free=False, i=None):
                    dve.wait_ge(unit_used, (0 if i is None else i * 6) + (u + 2))
                    if free:
                        dve.wait_ge(al_ready, g - 1)
                    o = hid[j % 2].rearrange("p (c t) -> p c t", c=2)
                    up_ps = ps[:, 5 + (2 * j) % 4, :].rearrange("p (c t) -> p c t", c=2)
                    s = sil[j % 2].rearrange("p (c t) -> p c t", c=2)
                    dve.wait_ge(silu_done, g + 1)
                    v.tensor_tensor(o, up_ps, s, ALU.mult).then_inc(hid_ready, 1)

                def low(j, g, used=None, i=None):
                    dve.wait_ge(ah_ready, g + 1)
                    if used is not None:
                        dve.wait_ge(unit_used, (0 if i is None else i * 6) + used)
                    v.tensor_tensor(al[:, 2 * (j % 2):2 * (j % 2) + 2, :],
                                    hid[j % 2].rearrange("p (c t) -> p c t", c=2),
                                    ah[:, 2 * (j % 2):2 * (j % 2) + 2, :].bitcast(F32),
                                    ALU.subtract).then_inc(al_ready, 1)

                ahead(p0)
                hidden(p0, 0, trio)
                lo(p0 + 3)
                low(0, trio)
                lo(p0 + 4)
                lo(p0 + 5)
                hidden(p0 + 2, 1, trio + 1)
                lo(p0 + 6)
                low(1, trio + 1)
                body = (n - 2) // 2
                with dve.Fori(0, body) as i:
                    for j in (2, 3):
                        u = p0 + 3 * j - 1
                        lo(u + 2, i)
                        lo(u + 3, i)
                        hidden(u, j, i * 2 + (trio + j), True, i)
                        lo(u + 4, i)
                        low(j, i * 2 + (trio + j), u, i)
                for j in range(2 + 2 * body, n):
                    u = p0 + 3 * j - 1
                    lo(u + 2)
                    lo(u + 3)
                    hidden(u, j, trio + j, True)
                    if u + 4 < len(units):
                        lo(u + 4)
                    low(j, trio + j, u)
                st["lo"] = min(p0 + 3 * n + 1, len(units))
                dve.wait_ge(unit_used, p0 + 3 * n)
                add_sums()

            v.memset(ones[:], 1.0).then_inc(ones_set, 1)
            dve.wait_ge(x_landed, 16)
            dve.wait_ge(vec_landed, 16)
            for k in range(0, DC, 2):
                square(x, k, k + 2)
            lo(0)
            norm(x[:], 8, D, "g_mix", squared=True, between=lambda: lo(1))
            st["lo"] = 2
            stage(u_in[0:6], lambda a: qd[:, 2 * a:2 * a + 2, :])
            stage(u_in[6:12], lambda a: kd[:, 2 * a:2 * a + 2, :])
            stage(u_in[12:18], lambda a: vd[:, :, a * 256:(a + 1) * 256])
            stage(u_in[18:22], lambda a: qs[:, 2 * a:2 * a + 2, :])
            ahead(u_in[22])
            dve.wait_ge(unit_used, u_in[22] + 1)
            v.tensor_copy(ks, bank(22)[:, 0:1, :])
            v.tensor_copy(vs, bank(22)[:, 1, :].rearrange("p (a b) -> p a b", a=2)).then_inc(lin_evac[0], 1)
            st["lin"] += 1
            dve.wait_ge(consts_landed, 48)
            dve.wait_ge(kswap_mm, 1)
            v.tensor_copy(kswap[:, 0, :], ps[:, 5, 0:T]).then_inc(kswap_there, 1)

            def gates_ahead(a):
                if a == 21:
                    dve.wait_ge(att_out, 4)
                    dve.sem_inc(h_ready, 1)
                    split_low(qd[:, 0:4, :], ah[:], al[:])
                if a % 4 == 3:
                    ahead(u_in[23 + a // 4])
                    st["lin"] += 1

            def y_a(k, w):
                return qd[:, k:k + w, :] if k < 4 else qs[:, k - 4:k - 4 + w, :]

            attend(steps_a, y_a, gates_ahead)
            all_out()
            dve.sem_inc(h_ready, 4)
            split_lows(qs, u_in[-1] + 1)
            for k, u in enumerate(u_br):
                two = slice(2 * k, 2 * k + 2)
                sd, ss = sg[:, two, :], sg[:, 8 + 2 * k:10 + 2 * k, :]
                ahead(u)
                m = st["lin"]
                dve.wait_ge(unit_used, u + 1)
                v.tensor_tensor(hbuf[:, two, :], bank(m), sd, ALU.mult).then_inc(lin_evac[m % 2], 1)
                ahead(u + 1)
                dve.wait_ge(unit_used, u + 2)
                v.tensor_tensor(ss, bank(m + 1), ss, ALU.mult).then_inc(lin_evac[(m + 1) % 2], 1)
                st["lin"] += 2
                all_out()
                v.tensor_tensor(hbuf[:, two, :], hbuf[:, two, :], ss, ALU.add).then_inc(h_ready, 1)
            split_lows(hbuf, u_br[-1] + 2)
            dve.wait_ge(x_again, 16)
            residual(u_out)
            dve.sem_inc(moe_starts, 1)
            norm(x[:], 8, D, "g_ffn", squared=True)

            def col(a, n=1):
                return rt[:, :, a:a + n]

            def wide(a, n):
                return col(a).broadcast_to([P, 2, n])

            gkeys = gkey.unsqueeze(1).broadcast_to([P, 2, N_GRP])
            ekeys = ekey.unsqueeze(1).broadcast_to([P, 2, N_EXP])
            ahead(u_router)
            dve.wait_ge(unit_used, u_router + 1)
            m = st["lin"]
            v.tensor_tensor(lg, bank(m)[:, :, 0:36], bias_row.unsqueeze(1).broadcast_to([P, 2, 36]),
                            ALU.add).then_inc(lin_evac[m % 2], 1)
            st["lin"] += 1
            all_out()
            gl = lg[:, :, 0:N_GRP]
            el = lg[:, :, N_GRP:].rearrange("p a (g e) -> p a g e", g=N_GRP)

            def first_max(dst, src, n, keys, top, key, kmax):
                link(v.tensor_reduce(col(top), src, AX.X, ALU.max))
                link(v.tensor_tensor(col(key, n), src, wide(top, n), ALU.is_equal))
                link(v.tensor_tensor(col(key, n), col(key, n), keys, ALU.mult))
                link(v.tensor_reduce(col(kmax), col(key, n), AX.X, ALU.max))
                link(v.tensor_tensor(dst, col(key, n), wide(kmax, n), ALU.is_equal))

            first_max(col(12, 4), gl, N_GRP, gkeys, 0, 8, 3)
            v.tensor_tensor(col(4, 4), gl, wide(0, 4), ALU.subtract).then_inc(route_grp, 1)
            dve.wait_ge(route_grp_exp, 1)
            link(v.tensor_reduce(col(1), col(4, 4), AX.X, ALU.add))
            link(v.reciprocal(col(2), col(1)))
            link(v.tensor_scalar(col(16, 4), col(12, 4), -FAR, FAR, ALU.mult, ALU.add))
            for a in range(2):
                pen = rt[:, a, 16:20].unsqueeze(2).broadcast_to([P, N_GRP, 8])
                link(v.tensor_tensor(rt[:, a, 32:64].rearrange("p (g e) -> p g e", g=N_GRP), el[:, a], pen, ALU.add))
            first_max(col(96, 32), col(32, 32), N_EXP, ekeys, 20, 64, 21)
            link(v.scalar_tensor_tensor(out=col(128, 32), in0=col(96, 32), scalar=2 * FAR, in1=col(32, 32),
                                        op0=ALU.mult, op1=ALU.add))
            first_max(col(160, 32), col(128, 32), N_EXP, ekeys, 22, 64, 21)
            link(v.tensor_tensor(col(224, 32), col(96, 32), col(160, 32), ALU.add))
            dve.wait_ge(route_landed, 16)
            dve.sem_inc(ranks_go, 1)
            v.tensor_tensor(col(23), col(22), col(20), ALU.subtract).then_inc(route_two, 1)
            dve.wait_ge(route_two_exp, 1)
            link(v.tensor_scalar(col(25), col(24), 1.0, None, ALU.add))
            link(v.reciprocal(col(25), col(25)))
            link(v.tensor_tensor(col(25), col(25), col(2), ALU.mult))
            link(v.tensor_tensor(col(26), col(25), col(24), ALU.mult))
            link(v.tensor_tensor(col(96, 32), col(96, 32), wide(25, 32), ALU.mult))
            link(v.tensor_tensor(col(160, 32), col(160, 32), wide(26, 32), ALU.mult))
            link(v.tensor_tensor(gate[:, :, 0:N_EXP], col(96, 32), col(160, 32), ALU.add))
            dve.wait_ge(ranks_mm, 1)
            link(v.tensor_copy(counts, ps[:, 5, 0:3 * N_EXP].rearrange("p (a e) -> p a e", a=3)))
            link(v.tensor_scalar(counts[:, 0:2, :], counts[:, 0:2, :], 1.0, None, ALU.add))
            link(v.tensor_tensor(counts[:, 0:2, :], counts[:, 0:2, :], col(224, 32), ALU.mult))
            link(v.tensor_scalar(rank[:, :, 0:N_EXP], counts[:, 0:2, :], 1.0, None, ALU.subtract))
            link(v.tensor_scalar(picks[:, 0, :], counts[:, 2, :], float(P), None, ALU.is_gt))
            link(v.memset(picks[:, 1, :], 1.0))
            link(v.tensor_tensor_scan(picks[:, 2, :], picks[:, 1, :], picks[:, 0, :], 0.0, ALU.mult, ALU.add))
            for j in range(EXTRA):
                link(v.tensor_scalar(picks[:, 3 + j, :], picks[:, 2, :], float(j + 1), None, ALU.is_equal))
                link(v.tensor_tensor(picks[:, 3 + j, :], picks[:, 3 + j, :], picks[:, 0, :], ALU.mult))
                link(v.tensor_tensor(picks[:, 6, :], picks[:, 3 + j, :], exp_no, ALU.mult))
                link(v.tensor_reduce(pick_f[:, j:j + 1], picks[:, 6, :], AX.X, ALU.add))
                chosen = picks[:, 3 + j, :].unsqueeze(1).broadcast_to([P, 2, N_EXP])
                link(v.tensor_tensor(weigh[:, 0], counts[:, 0:2, :], chosen, ALU.mult))
                link(v.tensor_tensor(weigh[:, 1], gate[:, :, 0:N_EXP], chosen, ALU.mult))
                at = slice(N_EXP + j, N_EXP + j + 1)
                link(v.tensor_reduce(rank[:, :, at], weigh[:, 0], AX.X, ALU.add))
                link(v.tensor_scalar(rank[:, :, at], rank[:, :, at], float(P + 1), None, ALU.subtract))
                link(v.tensor_reduce(gate[:, :, at], weigh[:, 1], AX.X, ALU.add))
            dve.sem_inc(ranks_go, 1)
            v.tensor_copy(pick_i[:, 0:EXTRA], pick_f[:, 0:EXTRA]).then_inc(extra_there, 1)
            dve.wait_ge(gate_h_there, 1)
            link(v.tensor_tensor(gate_hl[:, :, :, 1], gate, gate_hl[:, :, :, 0].bitcast(F32), ALU.subtract))
            split_low(ps[:, 0:4, :], xh[:].rearrange("p (b c) t -> p b (c t)", b=4),
                      xl[:].rearrange("p (b c) t -> p b (c t)", b=4), u_router + 1)
            experts(moe)
            link(norm(x[:], 8, D, "g_final", dst=x, squared=True))

            norm(x[:], 8, D, "ev_norm")
            dve.wait_ge(second_landed, 48)
            dve.wait_ge(xl_ready, st["split"])
            for k in range(0, DC, 2):
                square(mem, k, k + 2)
            for a, u in enumerate(u_ev):
                ahead(u)
                m = st["lin"]
                dve.wait_ge(unit_used, u + 1)
                if a < 2:
                    last = v.tensor_copy(pooled[0][:, 2 * a:2 * a + 2, 16:], bank(m))
                elif a == 2:
                    last = v.tensor_copy(lat[:, 0:2, :], bank(m))
                else:
                    v.tensor_copy(lat[:, 2, :], bank(m)[:, 0, :])
                    last = v.tensor_copy(kr[0:ROPE, :], bank(m)[0:ROPE, 1, :])
                last.then_inc(lin_evac[m % 2], 1)
                dve.wait_ge(lin_evac[m % 2], m // 2 + 1)
                st["lin"] += 1
                if a == 1:
                    dve.sem_inc(pool_in, 1)
                    dve.wait_ge(angles, 1)
                    root(D, mem_rstd)
                elif a == 2:
                    square(lat, 0, 2)
                elif a == 3:
                    square(lat, 2, 3)
                    dve.sem_inc(kr_there, 1)
            all_out()
            norm(lat[:, 0:2, :], 2, 256, "q_norm", squared=True)
            norm(lat, 1, P, "kv_norm", squared=True, at=2, bank=4)
            ahead(u_qup)
            dve.wait_ge(trig, 1)
            link(v.tensor_scalar(sinr[0:QK, :], sinr[0:QK, :], freq[0:QK, 1:2], None, ALU.mult))
            dve.wait_ge(kr_mm, 1)
            link(v.tensor_tensor(kr[0:QK, :], ps[0:QK, 5, 0:T], cosr[0:QK, :], ALU.mult))
            link(v.tensor_tensor(hbuf[0:QK, 0, :], ps[0:QK, 5, T:2 * T], sinr[0:QK, :], ALU.mult))
            link(v.tensor_tensor(kr[0:QK, :], kr[0:QK, :], hbuf[0:QK, 0, :], ALU.add))
            dve.sem_inc(kr_turned, 1)
            cos8 = cosr[0:QK, :].unsqueeze(1).broadcast_to([QK, MLA_H, T])
            sin8 = sinr[0:QK, :].unsqueeze(1).broadcast_to([QK, MLA_H, T])
            dve.wait_ge(mq_there, 1)
            link(v.tensor_tensor(hbuf[0:QK, :, :], mq[0:QK, :, :], cos8, ALU.mult))
            ahead(u_kvup)
            dve.wait_ge(mq_mm, 1)
            link(v.tensor_tensor(mq[0:QK, :, :], ps[0:QK, 4:8, :].rearrange("p b (c t) -> p (b c) t", c=2), sin8,
                                 ALU.mult))
            v.tensor_tensor(mq[0:QK, :, :], mq[0:QK, :, :], hbuf[0:QK, :, :], ALU.add).then_inc(mq_turned, 1)
            dve.wait_ge(pooled_there, 1)
            dve.sem_inc(h_ready, 1)
            split_low(ypool, ah[:], al[:])
            ahead(u_pool)
            link(scaled(mem, mem, 0, DC, "xa_m0", mem_rstd))
            dve.sem_inc(h_ready, 1)
            dve.wait_ge(unit_used, u_kvup + 1)
            v.tensor_copy(mv, ps[:, 6:8, :]).then_inc(kv_out, 1)
            split_low(mem, xh[:], xl[:])
            dve.wait_ge(unit_used, u_pool + 1)
            for g in range(4):
                last = v.tensor_scalar(ypool[:, g, :], bank(st["lin"] + g // 2)[:, g % 2, :],
                                       vcol("pool_scale", g), None, ALU.mult)
                if g % 2 == 1:
                    last.then_inc(lin_evac[(st["lin"] + g // 2) % 2], 1)
            st["lin"] += 2

            def memory_ahead(l, a):
                ahead(u_kv[l][a])
                st["lin"] += 1

            attend(steps_m, lambda k, w: my[:, k:k + w, :], lambda a: memory_ahead(0, a))
            all_out()
            dve.sem_inc(h_ready, 4)
            for src, at in ((ypool, 0), (my, 4)):
                for k in (0, 2):
                    to = slice(at + k, at + k + 2)
                    split_low(src[:, k:k + 2, :], xh[:, to, :], xl[:, to, :], u_kv[0][-1] + 1)
            residual(u_evo)

            def cross(l):
                norm(x[:], 8, D, f"xa_x{l}", squared=True)
                stage(u_xa[l][0][0:2])

                def queries_ahead(a):
                    if a in (0, 2):
                        ahead(u_xa[l][0][2 + a // 2])
                        st["lin"] += 1

                attend(steps_x[l], lambda k, w: xq[:, k:k + w, :], queries_ahead)
                dve.sem_inc(h_ready, 4)
                split_lows(xq, u_xa[l][0][-1] + 1)
                residual(u_xa[l][1])

            cross(0)
            norm(x[:], 8, D, "ffn0", squared=True)
            gated(ffn[0][0], ffn[0][1], trio0[0])

            lam = vec[:, VECS["lam"][0]:VECS["lam"][0] + 8]
            row = lambda k: lsm[:, k, :]
            link(v.tensor_scalar(row(5), lam, -1.0, None, ALU.mult))
            v.tensor_tensor(row(0), row(5), lam, ALU.max).then_inc(lam_abs, 1)
            link(v.tensor_scalar(row(5), row(5), 0.0, None, ALU.max))
            dve.wait_ge(lam_exp, 1)
            link(v.tensor_scalar(row(2), row(1), 2.0, None, ALU.add))
            link(v.reciprocal(row(2), row(2)))
            link(v.tensor_tensor(row(2), row(2), row(1), ALU.mult))
            link(v.tensor_tensor(row(3), row(2), row(2), ALU.mult))
            link(v.tensor_scalar(row(4), row(3), 1.0 / 17, None, ALU.mult))
            for odd in range(15, 1, -2):
                link(v.scalar_tensor_tensor(out=row(4), in0=row(4), scalar=1.0 / odd, in1=row(3), op0=ALU.add,
                                            op1=ALU.mult))
            link(v.scalar_tensor_tensor(out=row(4), in0=row(4), scalar=1.0, in1=row(2), op0=ALU.add, op1=ALU.mult))
            link(v.scalar_tensor_tensor(out=row(4), in0=row(4), scalar=2.0, in1=row(5), op0=ALU.mult, op1=ALU.add))
            v.tensor_scalar(row(6), row(4), -LRU_C, None, ALU.mult)
            v.tensor_scalar(row(7), row(4), LRU_C / 2, None, ALU.mult).then_inc(lam_scale, 1)
            link(v.tensor_scalar(reset, posf, 0.0, None, ALU.is_equal))
            link(v.tensor_scalar(keep, reset, -1.0, 1.0, ALU.mult, ALU.add))
            link(v.memset(lxb[:, :, 0:4], 0.0))
            norm(x[:], 8, D, "od_norm", squared=True)
            dve.wait_ge(mem_again, 16)
            for a in range(4):
                u, m = u_od[a], st["lin"]
                ahead(u)
                dve.wait_ge(unit_used, u + 1)
                v.tensor_copy(lxb[:, 2 * a:2 * a + 2, 4:], bank(m)).then_inc(lin_evac[m % 2], 1)
                st["lin"] += 1
                dve.wait_ge(lin_evac[m % 2], m // 2 + 1)
                for j in range(4):
                    for c in (2 * a, 2 * a + 1):
                        src = lxb[:, c, 1 + j:1 + j + T]
                        w = vcol("conv_w", j * 8 + c)
                        if j == 0:
                            last = v.tensor_scalar(lxc[:, c, :], src, w, vcol("conv_b", c), ALU.mult, ALU.add)
                        else:
                            last = v.scalar_tensor_tensor(out=lxc[:, c, :], in0=src, scalar=w, in1=lxc[:, c, :],
                                                          op0=ALU.mult, op1=ALU.add)
                    link(last)
                dve.sem_inc(h_ready, 1)
                if a >= 2:
                    two = slice(2 * a - 4, 2 * a - 2)
                    split_low(lxc[:, two, :], ah[:, two, :], al[:, two, :])
            for a in range(4):
                stage(u_od[4 + a:5 + a])
                last = scaled(mem, mem, 2 * a, 2 * a + 2, "xa_m1", mem_rstd)
            link(last)
            for a in (2, 3):
                two = slice(2 * a, 2 * a + 2)
                split_low(lxc[:, two, :], xh[:, two, :], xl[:, two, :], u_od[-1] + 1)
            all_out()
            ahead(u_rg)
            dve.sem_inc(h_ready, 4)
            ahead(u_rg + 1)
            split_lows(mem, u_rg + 2)
            memory_ahead(1, 0)
            dve.wait_ge(lru_t, 1)
            v.tensor_tensor(lr, lr, reset.unsqueeze(1).broadcast_to([P, DC, T]), ALU.max).then_inc(lru_t_max, 1)
            memory_ahead(1, 1)
            dve.wait_ge(lru_kept, 1)
            dve.wait_ge(lru_root, 1)
            link(v.scalar_tensor_tensor(out=lr, in0=lrc, scalar=1.0, in1=lr, op0=ALU.add, op1=ALU.mult))
            memory_ahead(1, 2)
            dve.wait_ge(lru_x, 1)
            link(v.tensor_tensor(li, li, lr, ALU.mult))
            memory_ahead(1, 3)
            for c in range(4):
                last = v.tensor_tensor_scan(lxc[:, c, :], lrc[:, c, :], li[:, c, :], 0.0, ALU.mult, ALU.add)
            memory_ahead(1, 4)
            for c in range(4, DC):
                last = v.tensor_tensor_scan(lxc[:, c, :], lrc[:, c, :], li[:, c, :], 0.0, ALU.mult, ALU.add)
            link(last)
            memory_ahead(1, 5)
            link(v.tensor_tensor(lgate, lgate, lxc, ALU.mult))
            dve.sem_inc(h_ready, 4)
            memory_ahead(1, 6)
            memory_ahead(1, 7)
            split_lows(lgate, u_kv[1][-1] + 1)
            all_out()
            residual(u_odo)
            cross(1)
            norm(x[:], 8, D, "ffn1", squared=True)
            gated(ffn[1][0], ffn[1][1], trio0[1])
            norm(x[:], 8, D, "final", dst=hbuf, squared=True, done=result)

        @block.gpsimd
        def _(pool):
            pool.wait_ge(att_mixed, len(steps_a))
            pool.dma_start(x[:], kview(t["xT"])).then_inc(x_again, 16)
            pool.wait_ge(moe_starts, 1)
            pool.dma_start(route, t["route"]).then_inc(route_landed, 16)
            pool.dma_start(mem, kview(t["memT"])).then_inc(second_landed, 16)
            pool.dma_start(c2, t["const2"]).then_inc(second_landed, 16)
            pool.dma_start(posi.bitcast(I32), t["positions_2"].partition_broadcast(P)).then_inc(second_landed, 16)
            st = dict(step=0)

            def link(ins):
                st["step"] += 1
                ins.then_inc(pool_step, 1)
                pool.wait_ge(pool_step, st["step"])

            g = nc.gpsimd
            pool.wait_ge(second_landed, 48)
            pool.wait_ge(extra_there, 1)
            link(g.tensor_copy(posf, posi.bitcast(I32)))
            two_pi_hi, magic = 6.28125, 12582912.0
            two_pi_lo = 2 * np.pi - two_pi_hi
            a0, a1, n = cosr[0:QK, :], sinr[0:QK, :], turns[0:QK, :]
            link(g.tensor_scalar(a0, posf[0:QK, :], freq[0:QK, 0:1], None, ALU.mult))
            link(g.tensor_copy(a1, a0))
            for dst, quarter in ((a1, 0.0), (a0, 0.25)):
                link(g.tensor_scalar(n, dst, float(1 / (2 * np.pi)), quarter, ALU.mult, ALU.add))
                link(g.tensor_scalar(n, n, magic, None, ALU.add))
                link(g.tensor_scalar(n, n, magic, None, ALU.subtract))
                for part in (-two_pi_hi, -float(two_pi_lo)):
                    link(g.tensor_scalar(spare[0:QK, :], n, part, None, ALU.mult))
                    link(g.tensor_tensor(dst, spare[0:QK, :], dst, ALU.add))
                link(g.tensor_scalar(dst, dst, float(quarter * 2 * np.pi), 3.1415925, ALU.add, ALU.min))
                link(g.tensor_scalar(dst, dst, -3.1415925, None, ALU.max))
            pool.sem_inc(angles, 1)
            pool.wait_ge(r_hid_mm, TILES + 1)
            for b in range(3):
                link(g.memset(pooled[b][:, :, 0:16], 0.0))
            pool.wait_ge(pool_in, 1)
            p0_, p1_, p2_ = pooled
            for k, (dst, src, back) in enumerate(((p1_, p0_, 1), (p2_, p1_, 2), (p1_, p2_, 4), (p2_, p1_, 8))):
                link(g.tensor_tensor(dst[:, k:, 16:], src[:, k:, 16:], src[:, k:, 16 - back:16 - back + T], ALU.add))
            for k in range(4):
                src = (p1_, p2_)[k % 2][:, k, 16:]
                link(g.tensor_tensor(src, src, icnt[:, k, :], ALU.mult))
                link(g.tensor_tensor(ypool[:, k, :], src, p0_[:, k, 16:], ALU.subtract))
            pool.sem_inc(pooled_there, 1)
            pool.wait_ge(kr_turned, 1)
            g.tensor_copy(mk[NOPE:QK, :, :], kr[NOPE:QK, :].unsqueeze(1).broadcast_to([ROPE, MLA_H, T])).then_inc(
                mk_rope_there, 1)
            pool.wait_ge(att_mixed, len(steps_a) + len(steps_m) + len(steps_x[0]))
            pool.dma_start(mem, kview(t["memT"])).then_inc(mem_again, 16)
            pool.wait_ge(lru_i, 1)
            link(g.tensor_tensor(li, li, lxc, ALU.mult))
            pool.sem_inc(lru_x, 1)
            pool.wait_ge(lru_a, 1)
            link(g.tensor_tensor(lrc, lrc, keep.unsqueeze(1).broadcast_to([P, DC, T]), ALU.mult))
            pool.sem_inc(lru_kept, 1)


_BIG = ["w_in", "w_br_dil", "w_br_swa", "w_out", "w_e_gate", "w_e_up", "w_e_down", "ev_w_in_2", "ev_pool_w_2",
        "ev_w_q_up_2", "ev_w_kv_up_2", "ev_w_out_2", "od_w_in_2", "od_w_rgate_2", "od_w_igate_2", "od_w_out_2",
        "xa_w_q_2", "xa_w_kv_2", "xa_w_o_2", "ffn_w_gate_up_2", "ffn_w_down_2"]


def kernel(**inputs):
    import concourse.bacc as _bacc
    from concourse.bass_utils import run_bass_kernel_spmd as _run

    a = {k: np.asarray(v) for k, v in inputs.items()}
    arrays = {k: np.ascontiguousarray(a[k]) for k in _BIG}
    arrays["xT"] = np.ascontiguousarray(a["x"][0].T)
    arrays["memT"] = np.ascontiguousarray(a["mem_2"][0].T)
    arrays["positions_2"] = a["positions_2"].reshape(T)
    arrays["sinks"] = a["sinks"].reshape(SWA_HEADS)
    arrays["b_route"] = np.concatenate([a["b_group"][0], a["b_router"][0]])
    arrays["w_route"] = np.ascontiguousarray(
        np.concatenate([a["w_group"][0], a["w_router"][0]], 1).reshape(DC, P, 36).transpose(1, 0, 2).reshape(P, -1))
    cols = {"g_mix": a["g_mix"], "g_ffn": a["g_ffn"], "g_final": a["g_final"], "ev_norm": a["ev_norm_2"],
            "pool_scale": a["ev_pool_scale_2"], "q_norm": a["ev_q_norm_2"], "kv_norm": a["ev_kv_norm_2"],
            "od_norm": a["od_norm_2"], "conv_w": a["od_conv_w_2"], "conv_b": a["od_conv_b_2"],
            "b_r": a["od_b_rgate_2"], "b_i": a["od_b_igate_2"], "lam": a["od_lambda_2"],
            "xa_x0": a["xa_norm_x_2"][0], "xa_x1": a["xa_norm_x_2"][1], "xa_m0": a["xa_norm_mem_2"][0],
            "xa_m1": a["xa_norm_mem_2"][1], "ffn0": a["ffn_norm_2"][0], "ffn1": a["ffn_norm_2"][1],
            "final": a["final_norm_2"]}
    arrays["vecs"] = np.ascontiguousarray(np.concatenate([cols[n].reshape(-1, P).T for n in VECS], 1))
    arrays["const1"], arrays["const2"], arrays["route"] = shape_constants()

    nc = _bacc.Bacc("TRN2", target_bir_lowering=False, num_devices=1)
    t = {k: nc.dram_tensor(f"{k}_dram", v.shape, mybir.dt.from_np(v.dtype), kind="ExternalInput").ap()
         for k, v in arrays.items()}
    out = nc.dram_tensor("out_dram", (D, T), F32, kind="ExternalOutput").ap()
    build(nc, t, out)
    r = _run(nc, [{f"{k}_dram": v for k, v in arrays.items()}], core_ids=[0])
    return np.ascontiguousarray(r.results[0]["out_dram"].T).reshape(1, T, D)
```

```python
from contextlib import ExitStack

import numpy as np

import concourse.bass as bass
from concourse import mybir

F32 = mybir.dt.float32
F32R = mybir.dt.float32r
I32 = mybir.dt.int32
ALU = mybir.AluOpType
ACT = mybir.ActivationFunctionType
AX = mybir.AxisListType

P = 128
T = 256
D = 1024
DC = D // P
HD = 64
GROUPS = ((128, 1), (512, 4), (2048, 16))
DIL_HEADS = 8
SWA_HEADS = 16
SWA_WINDOW = 128
N_EXP, N_GRP, D_EXP = 32, 4, 512
EXTRA = 2 * T // (P + 1)
TILES = N_EXP + EXTRA
PAIRS = -(-TILES // 2)
LOOP = 4
D_FF = 2816
MLA_H, NOPE, ROPE, QK = 8, 64, 32, 96
XA_H, XA_HD = 4, 256
EPS = 1e-6
LRU_C = 8.0
FAR = -1e30

RAW = 6
HL = 3
UNIT = 2048

VECS = {}
_at = 0
for _n, _c in (("g_mix", 8), ("g_ffn", 8), ("g_final", 8), ("ev_norm", 8), ("pool_scale", 4), ("q_norm", 2),
               ("kv_norm", 1), ("od_norm", 8), ("conv_w", 32), ("conv_b", 8), ("b_r", 8), ("b_i", 8), ("lam", 8),
               ("xa_x0", 8), ("xa_x1", 8), ("xa_m0", 8), ("xa_m1", 8), ("ffn0", 8), ("ffn1", 8), ("final", 8)):
    VECS[_n] = (_at, _c)
    _at += _c
NV = _at


def shape_constants():
    q = np.arange(P)[:, None]
    c = np.arange(T)[None, :]
    back = (q + P - c).astype(np.float32)
    pats = []
    for window, dil in GROUPS:
        ok = (back >= 0) & (back <= (window // dil) * dil) & (back % dil == 0)
        pats.append(np.where(ok, back, 1e30))
    pats.append(np.where((back >= 0) & (back <= SWA_WINDOW - 1), back, 1e30))
    first = np.concatenate([*pats, np.eye(P),
                            np.broadcast_to(np.arange(N_GRP, 0, -1), (P, N_GRP)),
                            np.broadcast_to(np.arange(N_EXP, 0, -1), (P, N_EXP))], 1).astype(np.float32)
    causal = np.where(back >= 0, 0.0, FAR)
    swap = np.zeros((P, QK))
    for m in range(NOPE, QK):
        swap[m + 16 if m < NOPE + 16 else m - 16, m] = 1
    put = np.zeros((P, 2, QK))
    for r in range(ROPE):
        put[r, 0, NOPE + r] = 1
        put[(r + 16) % ROPE, 1, NOPE + r] = 1
    freq = np.zeros((P, 2))
    inv = np.float32(10000.0) ** (-np.arange(0, ROPE, 2, dtype=np.float32) / np.float32(ROPE))
    freq[NOPE:QK, 0] = np.concatenate([inv, inv])
    freq[NOPE:QK, 1] = np.repeat([-1.0, 1.0], 16)
    cnt = np.stack([1.0 / np.minimum(np.arange(T) + 1, w) for w in (2, 4, 8, 16)]).astype(np.float32)
    second = np.concatenate([causal, swap, put.reshape(P, -1), freq,
                             np.broadcast_to(cnt.reshape(1, -1), (P, 4 * T))], 1).astype(np.float32)
    route = np.concatenate([np.broadcast_to(np.arange(P), (P, P)), np.triu(np.ones((P, P)), 1),
                            np.broadcast_to(np.arange(N_EXP), (P, N_EXP))], 1).astype(np.float32)
    return first, second, route


def slopes(n):
    return (2.0 ** (-8.0 * np.arange(1, n + 1) / n)).astype(np.float32)


def build(nc, t, out):
    with ExitStack() as ctx:
        def sb(name, shape, dt=F32):
            return ctx.enter_context(nc.sbuf_tensor(name, shape, dt))

        def sem(name):
            return ctx.enter_context(nc.semaphore(name))

        arena_at = -(-nc.sbuf_base // 32) * 32
        arena = sb("arena", [P, 62 * T])

        def over(name, at, shape, dt):
            return nc.alloc_sbuf_tensor_at(name, shape, dt, offset=arena_at + 4 * at)

        raw = [sb(f"raw{i}", [P, UNIT]) for i in range(RAW)]
        whi = [sb(f"whi{i}", [P, UNIT], F32R) for i in range(HL)]
        wlo = [sb(f"wlo{i}", [P, UNIT], F32R) for i in range(HL)]
        xh = sb("xh", [P, DC, T], F32R)
        xl = sb("xl", [P, DC, T], F32R)
        ah = sb("ah", [P, 4, T], F32R)
        al = sb("al", [P, 4, T], F32R)
        x = sb("x", [P, DC, T])
        scr = sb("scr", [P, 9 * T])
        c1 = sb("c1", [P, 1024 + P + N_GRP + N_EXP])
        vec = sb("vec", [P, NV])
        rows = sb("rows", [P, SWA_HEADS + N_GRP + N_EXP])
        ones = sb("ones", [P, P])
        rstd = sb("rstd", [P, T])
        sm = sb("sm", [P, 3, 24])
        ps = ctx.enter_context(nc.psum_tensor("ps", [P, 8, 512], F32))

        pat = c1[:, 0:1024].rearrange("p (g k) -> p g k", g=4)
        ident = c1[:, 1024:1152]
        gkey = c1[:, 1152:1156]
        ekey = c1[:, 1156:1188]
        sink_row = rows[:, 0:16]
        bias_row = rows[:, 16:52]

        def vcol(name, c):
            a = VECS[name][0] + c
            return vec[:, a:a + 1]

        def area(at, *shape):
            n = int(np.prod(shape))
            v = arena[:, at:at + n]
            if len(shape) == 2:
                v = v.rearrange("p (a b) -> p a b", a=shape[0])
            elif len(shape) == 3:
                v = v.rearrange("p (a b c) -> p a b c", a=shape[0], b=shape[1])
            return v

        def chunks(at, n):
            return area(at, n, T)

        qd, kd = chunks(0, 12), chunks(12 * T, 12)
        vd = area(24 * T, 2, 1536)
        qs = chunks(36 * T, 8)
        ks, vs = chunks(44 * T, 1), area(45 * T, 2, P)
        sg = chunks(46 * T, 16)
        lg, logits = area(40 * T, 2, 36), area(41 * T, T)
        route = area(54 * T, 2 * P + N_EXP)
        slot_no, before, exp_no = route[:, 0:P], route[:, P:2 * P], route[:, 2 * P:]
        counts = area(56 * T, 3, N_EXP)
        rank = area(56 * T + 96, 2, 2 * PAIRS)
        gate = area(56 * T + 200, 2, TILES)
        picks = area(56 * T + 300, 8, N_EXP)
        pick_f, pick_i = area(58 * T + 100, 4), area(58 * T + 108, 4).bitcast(I32)
        weigh = area(58 * T + 116, 4, 2, N_EXP)
        slot_gate = area(60 * T, 2)
        gate_hl = over("gate_hl", 60 * T + 8, [P, 2, TILES, 2], F32R)
        got_h = [over(f"got_h{b}", 16 * b * T, [P, DC, 2, P], F32R) for b in range(2)]
        got_l = [over(f"got_l{b}", (8 + 16 * b) * T, [P, DC, 2, P], F32R) for b in range(2)]
        pick = [over(f"pick{b}", (32 + 2 * b) * T, [P, 2, 2 * P], F32R) for b in range(2)]
        turned = [over(f"turned{b}", 36 * T + b * 272, [P, 258], F32R) for b in range(2)]
        y_h = [over(f"y_h{b}", (39 + 4 * b) * T, [P, 512], F32R) for b in range(2)]
        y_l = [over(f"y_l{b}", (41 + 4 * b) * T, [P, 512], F32R) for b in range(2)]
        hid_h = [ah[:, 2 * b:2 * b + 2, :].rearrange("p a t -> p (a t)").rearrange("p (k s) -> p k s", k=4)
                 for b in range(2)]
        hid_l = [al[:, 2 * b:2 * b + 2, :].rearrange("p a t -> p (a t)").rearrange("p (k s) -> p k s", k=4)
                 for b in range(2)]
        tok_h = xh[:].rearrange("p c t -> p (c t)").rearrange("p (i d) -> p i d", i=2)
        tok_l = xl[:].rearrange("p c t -> p (c t)").rearrange("p (i d) -> p i d", i=2)
        rt = area(42 * T, 2, T)
        mem = chunks(0, 8)
        c2 = area(45 * T, T + QK + 2 * QK + 2 + 4 * T)
        causal = c2[:, 0:T]
        swap = c2[:, T:T + QK]
        put = c2[:, T + QK:T + 3 * QK].rearrange("p (a b) -> p a b", a=2)
        freq = c2[:, T + 3 * QK:T + 3 * QK + 2]
        icnt = c2[:, T + 3 * QK + 2:].rearrange("p (g t) -> p g t", g=4)
        posi, posf = area(52 * T, T), area(53 * T, T)
        mem_rstd = area(52 * T, T)

        raw_landed = [sem(f"raw_landed{i}") for i in range(RAW)]
        hi_ready, lo_ready, unit_used = sem("hi_ready"), sem("lo_ready"), sem("unit_used")
        lin_evac = [sem("lin_evac0"), sem("lin_evac1")]
        x_landed = [sem(f"x_landed{b}") for b in range(4)]
        consts_landed, second_landed = sem("consts_landed"), sem("second_landed")
        vec_landed, out_landed, x_again = sem("vec_landed"), sem("out_landed"), sem("x_again")
        ones_set = sem("ones_set")
        sq_ready, ss_ready, ms_ready, rstd_ready = sem("sq_ready"), sem("ss_ready"), sem("ms_ready"), sem("rstd_ready")
        h_ready, xh_ready, xl_ready = sem("h_ready"), sem("xh_ready"), sem("xl_ready")
        dve_step = sem("dve_step")
        silu_done, hid_ready, ah_ready, al_ready = (sem("silu_done"), sem("hid_ready"),
                                                                sem("ah_ready"), sem("al_ready"))
        att_scored, att_biased, att_max, att_exp, att_probs = (sem("att_scored"), sem("att_biased"), sem("att_max"),
                                                               sem("att_exp"), sem("att_probs"))
        att_turned, att_pt, att_mixed, att_out = sem("att_turned"), sem("att_pt"), sem("att_mixed"), sem("att_out")
        def sems(names):
            return [sem(n) for n in names.split()]

        route_grp, route_grp_exp, route_two, route_two_exp = sems("route_grp route_grp_exp route_two route_two_exp")
        ranks_go, ranks_mm, extra_gates, extra_there, gate_h_there, logits_turned, route_landed, moe_starts = sems(
            "ranks_go ranks_mm extra_gates extra_there gate_h_there logits_turned route_landed moe_starts")
        pick_ready, turn_mm, turned_there, gath_mm, gath_act, gath_dve = sems(
            "pick_ready turn_mm turned_there gath_mm gath_act gath_dve")
        r_silu, r_hid, r_hid_mm, r_hid_h, r_hid_l, r_y_h, r_y_l = sems(
            "r_silu r_hid r_hid_mm r_hid_h r_hid_l r_y_h r_y_l")
        x_summed = sem("x_summed")
        kswap_mm, kswap_there, gates_there = sems("kswap_mm kswap_there gates_there")
        pool_in, pooled_there, angles, trig, kr_there, kr_mm, kr_turned = sems(
            "pool_in pooled_there angles trig kr_there kr_mm kr_turned")
        mq_there, mq_mm, mq_turned, mk_mm, mk_there, mk_rope_there, kv_out = sems(
            "mq_there mq_mm mq_turned mk_mm mk_there mk_rope_there kv_out")
        pool_step = sem("pool_step")
        mem_again = sem("mem_again")
        lam_abs, lam_exp, lam_scale, lru_r, lru_i, lru_x, lru_a, lru_kept, lru_t, lru_t_max, lru_root = sems(
            "lam_abs lam_exp lam_scale lru_r lru_i lru_x lru_a lru_kept lru_t lru_t_max lru_root")
        result = sem("result")

        units = []

        def kview(w):
            return w.rearrange("(k p) n -> p k n", p=P)

        def cut(w, kc, step, n=None):
            v = kview(w)
            n = n or w.shape[-1]
            first = len(units)
            for a in range(0, n, step):
                b = min(a + step, n)
                units.append((v[:, :, a:b], kc, b - a))
            return range(first, len(units))

        u_in = cut(t["w_in"][0], DC, 256)
        u_br = []
        wd_, ws_ = kview(t["w_br_dil"][0]), kview(t["w_br_swa"][0])
        for a in range(0, D, 256):
            u_br.append(len(units))
            units.append((wd_[:, :, a:a + 256], 4, 256))
            units.append((ws_[:, :, a:a + 256], 8, 256))
        u_out = cut(t["w_out"][0], DC, 256)
        u_router = len(units)
        units.append((t["w_route"].rearrange("p (k n) -> p k n", k=DC), DC, 36))
        moe = len(units)
        for j in range(6 * TILES):
            units.append(None)

        def second_attention(l):
            uq = cut(t["xa_w_q_2"][l], DC, 256)
            uo = cut(t["xa_w_o_2"][l], DC, 256)
            return uq, uo

        def gated_ffn(l):
            at = (len(units), D_FF // 256)
            for j in range(3 * (D_FF // 256)):
                units.append(None)
            return at

        pool_w = 4 * P
        u_ev = [*cut(t["ev_w_in_2"][0][:, pool_w:], DC, 256), *cut(t["ev_w_in_2"][0][:, 0:pool_w], DC, 256)]
        u_qup = len(units)
        units.append((kview(t["ev_w_q_up_2"][0]), 2, 768))
        u_kvup = len(units)
        units.append((kview(t["ev_w_kv_up_2"][0]), 1, 1024))
        u_pool = len(units)
        units.append((t["ev_pool_w_2"][0].rearrange("g p n -> p g n"), 4, P))
        u_kv = [cut(t["xa_w_kv_2"][0], DC, 256)]
        u_evo = cut(t["ev_w_out_2"][0], DC, 256)
        u_xa = [second_attention(0)]
        ffn = [gated_ffn(0)]
        u_od = [*cut(t["od_w_in_2"][0][:, D:], DC, 256), *cut(t["od_w_in_2"][0][:, 0:D], DC, 256)]
        u_rg = len(units)
        for w in ("od_w_rgate_2", "od_w_igate_2"):
            units.append((t[w][0].rearrange("h (k p) n -> p (h k) n", p=P), DC, 256))
        u_kv.append(cut(t["xa_w_kv_2"][1], DC, 256))
        u_odo = cut(t["od_w_out_2"][0], DC, 256)
        u_xa.append(second_attention(1))
        ffn.append(gated_ffn(1))

        trio0 = [0, ffn[0][1]]

        def wview(buf, u, kc, n):
            return buf[u % HL][:, 0:kc * n].rearrange("p (k n) -> p k n", k=kc)

        def usize(u):
            return units[u][1] * units[u][2] if units[u] else UNIT

        def score_bank(step, g):
            at = g * T if len(step["scores"]) == 3 else g * 512
            return ps[:, at // 512, at % 512:at % 512 + step["nk"]]

        def gather_bank(r, m):
            return 4 + r if m < 0 else 7

        def attention(kind, l=0):
            steps = []
            if kind == "dil":
                sl = slopes(24)
                for hh in range(DIL_HEADS):
                    lo = HD * (hh % 2)
                    for qt in range(2):
                        nk = P * (qt + 1)
                        sc, bi, pv = [], [], []
                        for g in range(3):
                            c = 4 * g + hh // 2
                            sc.append([(qd[lo:lo + HD, c, qt * P:qt * P + P], kd[lo:lo + HD, c, 0:nk])])
                            bi.append((g, float(sl[8 * g + hh]) * 8.0))
                            for kt in range(qt + 1):
                                pv.append((vd[:, kt, (8 * g + hh) * HD:(8 * g + hh + 1) * HD], g, kt))
                        steps.append(dict(nk=nk, qt=qt, scores=sc, bias=bi, merged=True, sink=None, scale=0.125,
                                          pv=[(lo, 0, pv)], last=hh % 2 == 1 and qt == 1,
                                          y=[qd[:, hh // 2, :]]))
            elif kind == "swa":
                sl = slopes(SWA_HEADS)
                for c in range(8):
                    for qt in range(2):
                        nk = P * (qt + 1)
                        sc, bi, pv = [], [], []
                        for i in range(2):
                            h = 2 * c + i
                            kv = h // 8
                            kk = ks[:, 0, :] if kv == i else kswap[:, 0, :]
                            sc.append([(qs[HD * i:HD * i + HD, c, qt * P:qt * P + P], kk[HD * i:HD * i + HD, 0:nk])])
                            bi.append((3, float(sl[h]) * 8.0))
                            pv.append((HD * i, 0, [(vs[:, kt, kv * HD:(kv + 1) * HD], i, kt) for kt in range(qt + 1)]))
                        steps.append(dict(nk=nk, qt=qt, scores=sc, bias=bi, merged=False, sink=2 * c, scale=0.125,
                                          pv=pv, last=qt == 1, y=[qs[:, c, :]]))
            elif kind == "mla":
                for c in range(4):
                    for qt in range(2):
                        nk = P * (qt + 1)
                        sc, pv = [], []
                        for i in range(2):
                            h = 2 * c + i
                            sc.append([(mq[0:QK, h, qt * P:qt * P + P], mk[0:QK, h, 0:nk])])
                            pv.append((HD * i, 0, [(mv[:, kt, h * HD:(h + 1) * HD], i, kt) for kt in range(qt + 1)]))
                        steps.append(dict(nk=nk, qt=qt, scores=sc, bias="causal", merged=False, sink=None,
                                          scale=float(QK) ** -0.5, pv=pv, last=qt == 1, y=[my[:, c, :]]))
            else:
                for h in range(XA_H):
                    for qt in range(2):
                        sc = [[(xq[:, 2 * h + k, qt * P:qt * P + P], xk[:, 2 * h + k, :]) for k in range(2)]]
                        pv = [(0, k, [(xv[l][:, kt, (2 * h + k) * P:(2 * h + k + 1) * P], 0, kt) for kt in range(2)])
                              for k in range(2)]
                        steps.append(dict(nk=T, qt=qt, scores=sc, bias=None, merged=False, sink=None,
                                          scale=float(XA_HD) ** -0.5, pv=pv, last=qt == 1,
                                          y=[xq[:, 2 * h, :], xq[:, 2 * h + 1, :]]))
            return steps

        lat = chunks(25 * T, 3)
        kr = area(28 * T, T)
        cosr, sinr, turns, spare = area(43 * T, T), area(44 * T, T), area(41 * T, T), area(42 * T, T)
        pooled = [area(8 * T + 1088 * b, 4, 16 + T) for b in range(3)]
        ypool = chunks(21 * T, 4)
        mk, mv = chunks(8 * T, 8), area(16 * T, 2, 512)
        mq, my = chunks(33 * T, 8), chunks(41 * T, 4)
        xq, xk = chunks(8 * T, 8), chunks(0, 8)
        xv = [area(25 * T, 2, 1024), area(16 * T, 2, 1024)]
        lgate, lxb, lxc = chunks(8 * T, 8), area(16 * T, 8, T + 4), chunks(25 * T, 8)
        lr, li, lrc = chunks(33 * T, 8), chunks(41 * T, 8), chunks(54 * T, 8)
        reset, keep, lsm = area(49 * T, T), area(51 * T, T), area(50 * T, 10, 8)
        kswap = rstd[:, :].rearrange("p (a b) -> p a b", a=1)
        S = [scr[:, b * 768:(b + 1) * 768].rearrange("p (g k) -> p g k", g=3) for b in range(3)]
        PT_first = [x[:, 3 * b:3 * b + 3, :].rearrange("p c (b q) -> p (c b) q", q=P) for b in range(2)]
        PT_later = [area((54 + 2 * b) * T, 4, P) for b in range(2)]
        hbuf = scr[:, 0:2048].rearrange("p (c t) -> p c t", c=8)
        sil = [scr[:, 0:512], scr[:, 512:1024]]
        hid = [scr[:, 1024:1536], scr[:, 1536:2048]]

        def lru_in(part, h, k):
            return part[:, 2 * h + k, :]

        steps_a = attention("dil") + attention("swa")
        steps_m = attention("mla")
        steps_x = [attention("xa", l) for l in range(2)]

        block = ctx.enter_context(nc.Block())

        @block.sync
        def _(sp):
            for b in range(4):
                sp.dma_start(x[:, 2 * b:2 * b + 2, :], kview(t["xT"])[:, 2 * b:2 * b + 2, :]).then_inc(x_landed[b], 16)
            sp.dma_start(vec[:], t["vecs"]).then_inc(vec_landed, 16)

            def load(u, src, i=None, step=6):
                if i is not None:
                    sp.wait_ge(lo_ready, i * step + (u - RAW + 1))
                elif u >= RAW:
                    sp.wait_ge(lo_ready, u - RAW + 1)
                kc, n = src.shape[1], src.shape[2]
                sp.dma_start(raw[u % RAW][:, 0:kc * n].rearrange("p (k n) -> p k n", k=kc),
                             src).then_inc(raw_landed[u % RAW], 16)

            def load_gated(p0, n, g, uu, d):
                load(p0, g(0, 0))
                load(p0 + 1, uu(0, 0))
                with sp.Fori(0, (n - 1) // 2) as i:
                    load(p0 + 2, g(i, 1), i=i)
                    load(p0 + 3, uu(i, 1), i=i)
                    load(p0 + 4, d(i, 0), i=i)
                    load(p0 + 5, g(i, 2), i=i)
                    load(p0 + 6, uu(i, 2), i=i)
                    load(p0 + 7, d(i, 1), i=i)
                if n % 2 == 0:
                    load(p0 + 3 * n - 4, g(n // 2 - 1, 1))
                    load(p0 + 3 * n - 3, uu(n // 2 - 1, 1))
                    load(p0 + 3 * n - 2, d(n // 2 - 1, 0))
                    load(p0 + 3 * n - 1, d(n // 2 - 1, 1))
                else:
                    load(p0 + 3 * n - 1, d(n // 2, 0))

            wg = t["w_e_gate"][0].rearrange("e (h k p) n -> h e p k n", p=P, h=2)
            wu = t["w_e_up"][0].rearrange("e (h k p) n -> h e p k n", p=P, h=2)
            wdn = t["w_e_down"][0].rearrange("e (k p) (h n) -> h e p k n", p=P, h=2)

            def load_experts(p0):
                for a in range(2):
                    load(p0 + 2 * a, wg[a][0])
                    load(p0 + 2 * a + 1, wu[a][0])

                def tile(u, e, before, i=None):
                    for a in range(2):
                        load(u + 3 * a, wg[a][e], i=i, step=12)
                        load(u + 3 * a + 1, wu[a][e], i=i, step=12)
                        load(u + 3 * a + 2, wdn[a][before], i=i, step=12)

                with sp.Fori(0, (N_EXP - 2) // 2) as i:
                    tile(p0 + 4, i * 2 + 1, i * 2, i)
                    tile(p0 + 10, i * 2 + 2, i * 2 + 1, i)
                tile(p0 + 6 * (N_EXP - 1) - 2, N_EXP - 1, N_EXP - 2)
                sp.wait_ge(extra_there, 1)
                e = [sp.value_load(pick_i[0:1, j:j + 1], min_val=0, max_val=N_EXP - 1) for j in range(EXTRA)]
                for j in range(EXTRA):
                    tile(p0 + 6 * (N_EXP + j) - 2, e[j], e[j - 1] if j else N_EXP - 1)
                for a in range(2):
                    load(p0 + 6 * TILES - 2 + a, wdn[a][e[-1]])

            def ffn_cols(l, half):
                w = t["ffn_w_gate_up_2"][l][:, half * D_FF:(half + 1) * D_FF]
                first = kview(w[:, 0:256])
                rest = w[:, 256:].rearrange("(k p) (j b n) -> b j p k n", p=P, b=2, n=256)
                return lambda i, c: rest[c - 1][i] if c else first

            def ffn_rows(l):
                w = t["ffn_w_down_2"][l]
                pairs = w[0:D_FF - 256].rearrange("(j b k p) n -> b j p k n", p=P, k=2, b=2)
                last = kview(w[D_FF - 256:])
                return lambda i, c: last if isinstance(i, int) else pairs[c][i]

            u = 0
            while u < len(units):
                if u == moe:
                    load_experts(u)
                    u += 6 * TILES
                elif u in (ffn[0][0], ffn[1][0]):
                    l = 0 if u == ffn[0][0] else 1
                    load_gated(u, ffn[l][1], ffn_cols(l, 0), ffn_cols(l, 1), ffn_rows(l))
                    u += 3 * ffn[l][1]
                else:
                    load(u, units[u][0])
                    u += 1
                if u == RAW:
                    sp.dma_start(c1[:], t["const1"]).then_inc(consts_landed, 16)
                    sp.dma_start(rows[:, 0:16], t["sinks"].partition_broadcast(P)).then_inc(consts_landed, 16)
                    sp.dma_start(rows[:, 16:52], t["b_route"].partition_broadcast(P)).then_inc(consts_landed, 16)
            for b in range(4):
                sp.wait_ge(result, b + 1)
                sp.dma_start(out.rearrange("(c p) t -> p c t", p=P)[:, 2 * b:2 * b + 2, :],
                             hbuf[:, 2 * b:2 * b + 2, :]).then_inc(out_landed, 16)
            sp.wait_ge(out_landed, 64)

        @block.tensor
        def _(pe):
            st = dict(lin=0, sq=0, step=0, xl=0, y=0, fresh=False)

            def weights_in(u, i=None, step=6):
                add = 0 if i is None else i * step
                pe.wait_ge(hi_ready, add + u + 1)
                pe.wait_ge(lo_ready, add + u + 1)

            def triple(o, parts, first=True, last=True, group=True):
                fresh, st["fresh"] = st["fresh"], False
                mm = None
                for a, (wh, wl, h, l) in enumerate(parts):
                    if fresh and a % 2 == 0:
                        split_in()
                    mm = nc.tensor.matmul(o, wh, h, start=first and a == 0, stop=False, skip_group_check=not group)
                    nc.tensor.matmul(o, wh, l, start=False, stop=False, skip_group_check=not group)
                    mm = nc.tensor.matmul(o, wl, h, start=False, stop=last and a == len(parts) - 1,
                                          skip_group_check=not group)
                return mm

            def lin_bank():
                m = st["lin"]
                st["lin"] += 1
                if m >= 2:
                    pe.wait_ge(lin_evac[m % 2], m // 2)
                return ps[:, 6 + m % 2, :].rearrange("p (c t) -> p c t", c=2)

            def feature_unit(u, hsrc=None, lsrc=None, half=None):
                hsrc, lsrc = hsrc or xh, lsrc or xl
                _, kc, n = units[u]
                if half != 1:
                    weights_in(u)
                    st["bank"] = lin_bank()
                o = st["bank"]
                wh, wl = wview(whi, u, kc, n), wview(wlo, u, kc, n)
                for b in range(-(-n // P)) if half is None else [half]:
                    w = min(P, n - b * P)
                    mm = triple(o[0:w, b, :], [(wh[:, k, b * P:b * P + w], wl[:, k, b * P:b * P + w],
                                                hsrc[:, k, :], lsrc[:, k, :]) for k in range(kc)])
                if half != 0:
                    mm.then_inc(unit_used, 1)

            def token_unit(u):
                _, kc, n = units[u]
                weights_in(u)
                o = lin_bank()
                wh, wl = wview(whi, u, kc, n), wview(wlo, u, kc, n)
                fresh, st["fresh"] = st["fresh"], False
                for tt in range(2):
                    for k in range(kc):
                        if fresh and tt == 0 and k % 2 == 0:
                            split_in()
                        h, l = xh[:, k, tt * P:tt * P + P], xl[:, k, tt * P:tt * P + P]
                        nc.tensor.matmul(o[:, tt, 0:n], h, wh[:, k, :], start=k == 0, stop=False)
                        nc.tensor.matmul(o[:, tt, 0:n], l, wh[:, k, :], start=False, stop=False)
                        mm = nc.tensor.matmul(o[:, tt, 0:n], h, wl[:, k, :], start=False, stop=k == kc - 1)
                mm.then_inc(unit_used, 1)

            def squares(k, c, at=0, bank=5, both=False):
                st["sq"] += 1
                pe.wait_ge(sq_ready, st["sq"])
                for a in range(k, min(k + 2, c) if both else k + 1):
                    mm = nc.tensor.matmul(ps[:, bank, 0:T], ones[:], hbuf[:, at + a, :], start=a == 0,
                                          stop=k + 2 >= c and (a > k or not both))
                if k + 2 >= c:
                    mm.then_inc(ss_ready, 1)

            def norm(c, split=True, both=False):
                for k in range(0, c, 2):
                    squares(k, c, both=both)
                st["fresh"] = split

            def residual(us, split=True):
                for a, u in enumerate(us):
                    feature_unit(u)
                    if a >= 1:
                        squares(2 * a - 2, DC)
                squares(DC - 2, DC)
                st["fresh"] = split

            def split_in():
                st["xl"] += 1
                pe.wait_ge(xl_ready, st["xl"])

            def all_out():
                for b in range(2):
                    pe.wait_ge(lin_evac[b], (st["lin"] + 1 - b) // 2)

            def score(s, step):
                if s >= 1:
                    pe.wait_ge(att_biased, s)
                for g, pairs in enumerate(step["scores"]):
                    o = score_bank(step, g)
                    for a, (q, k) in enumerate(pairs):
                        mm = nc.tensor.matmul(o, q, k, start=a == 0, stop=a == len(pairs) - 1)
                mm.then_inc(att_scored, 1)

            def turn(s, step):
                pe.wait_ge(att_probs, s + 1)
                if s >= 1:
                    pe.wait_ge(att_pt, s)
                b = 0
                for g in range(len(step["scores"])):
                    for kt in range(step["nk"] // P):
                        mm = nc.tensor.transpose(ps[:, 2 + b // 4, (b % 4) * P:(b % 4) * P + P],
                                                 S[s % 3][:, g, kt * P:kt * P + P], ident)
                        b += 1
                mm.then_inc(att_turned, 1)

            def mix(s, step, PT):
                y = st["y"]
                pe.wait_ge(att_pt, s + 1)
                if y >= 2:
                    pe.wait_ge(att_out, y - 1)
                per = step["nk"] // P
                for lo, k, pv in step["pv"]:
                    for a, (v, g, kt) in enumerate(pv):
                        w = v.shape[1]
                        mm = nc.tensor.matmul(ps[lo:lo + w, 4 + y % 2, k * T + step["qt"] * P:k * T + step["qt"] * P + P],
                                              v, PT[s % 2][:, g * per + kt, :], start=a == 0, stop=a == len(pv) - 1)
                mm.then_inc(att_mixed, 1)
                if step["last"]:
                    st["y"] += 1

            def attend(steps, PT, between=None):
                base = st["step"]
                score(base, steps[0])
                score(base + 1, steps[1])
                for a, step in enumerate(steps):
                    s = base + a
                    if between:
                        between(a)
                    if a + 2 < len(steps):
                        score(s + 2, steps[a + 2])
                    turn(s, step)
                    if a >= 1:
                        mix(s - 1, steps[a - 1], PT)
                mix(base + len(steps) - 1, steps[-1], PT)
                st["step"] += len(steps)

            def gated(p0, n, trio):
                def gu(u, j, jj, i=None):
                    for w, bank in ((u, 4 + (2 * j) % 4), (u + 1, 5 + (2 * j) % 4)):
                        weights_in(w, i)
                        if w == u and jj is not None:
                            pe.wait_ge(hid_ready, jj)
                        wh, wl = wview(whi, w, DC, T), wview(wlo, w, DC, T)
                        for b in range(2):
                            mm = triple(ps[:, bank, b * T:(b + 1) * T],
                                        [(wh[:, k, b * P:b * P + P], wl[:, k, b * P:b * P + P], xh[:, k, :],
                                          xl[:, k, :]) for k in range(DC)])
                        mm.then_inc(unit_used, 1)

                def down(u, j, jj, i=None, first=False, last=False):
                    weights_in(u, i)
                    pe.wait_ge(al_ready, jj)
                    wh, wl = wview(whi, u, 2, D), wview(wlo, u, 2, D)
                    for c in range(DC):
                        mm = triple(ps[:, c // 2, (c % 2) * T:(c % 2 + 1) * T],
                                    [(wh[:, k, c * P:c * P + P], wl[:, k, c * P:c * P + P],
                                      ah[:, 2 * (j % 2) + k, :], al[:, 2 * (j % 2) + k, :]) for k in range(2)],
                                    first=first and c % 2 == 0, last=last, group=False)
                    mm.then_inc(unit_used, 1)

                gu(p0, 0, None)
                gu(p0 + 2, 1, None)
                down(p0 + 4, 0, trio + 1, first=True)
                body = (n - 2) // 2
                with pe.Fori(0, body) as i:
                    gu(p0 + 5, 2, i * 2 + (trio + 1), i)
                    down(p0 + 7, 1, i * 2 + (trio + 2), i)
                    gu(p0 + 8, 3, i * 2 + (trio + 2), i)
                    down(p0 + 10, 2, i * 2 + (trio + 3), i)
                at = 2 + 2 * body
                while at < n:
                    gu(p0 + 3 * at - 1, at, trio + at - 1)
                    down(p0 + 3 * at + 1, at - 1, trio + at)
                    at += 1
                down(p0 + 3 * n - 1, n - 1, trio + n, last=True)

            def experts(p0):
                def gather(r, m, i=None):
                    add = 0 if i is None else i * LOOP
                    if r == 0:
                        if m >= 0:
                            pe.wait_ge(turned_there, add + m + 1)
                        if m % 2 == 0:
                            pe.wait_ge(pick_ready, (0 if i is None else i * (LOOP // 2)) + m // 2 + 2)
                    elif m >= 0:
                        pe.wait_ge(gath_act, (0 if i is None else i * (3 * LOOP)) + 6 + 3 * m + r)
                    if m == -1:
                        pe.wait_ge(gath_act if r < 3 else gath_dve, r + 1 if r < 3 else 1)
                    o = ps[:, gather_bank(r, m), :]
                    src = tok_l if m % 2 else tok_h
                    for k in range(2):
                        c = 2 * r + k
                        for tt in range(2):
                            mm = nc.tensor.matmul(o[:, k * T:k * T + T], src[:, tt, c * P:c * P + P],
                                                  pick[(m // 2 + 1) % 2][:, tt, :], start=tt == 0, stop=tt == 1)
                    mm.then_inc(gath_mm, 1)

                def product(bank, u, act_h, act_l, first, last, i=None):
                    weights_in(u, i, 6 * LOOP)
                    wh, wl = wview(whi, u, 4, 512), wview(wlo, u, 4, 512)
                    o = ps[:, bank, :]
                    for k in range(4):
                        nc.tensor.matmul(o, act_h[:, k, :], wh[:, k, :], start=first and k == 0, stop=False)
                        nc.tensor.matmul(o, act_h[:, k, :], wl[:, k, :], start=False, stop=False)
                        mm = nc.tensor.matmul(o, act_l[:, k, :], wh[:, k, :], start=False, stop=last and k == 3)
                    mm.then_inc(unit_used, 1)

                def turn_pick(m, i=None):
                    add = 0 if i is None else i * LOOP
                    if i is not None or m >= 1:
                        pe.wait_ge(r_hid_l, add + m)
                    mine = pick[m // 2 % 2][:, :, (m % 2) * P:(m % 2) * P + P]
                    for tt in range(2):
                        nc.tensor.transpose(ps[:, 7, tt * P:tt * P + P], mine[:, tt, :].bitcast(F32), ident)
                    for tt in range(2):
                        gates_ = gate_hl[:, tt, bass.ds(add + m, 1), :] if i is not None else gate_hl[:, tt, m:m + 1, :]
                        mm = nc.tensor.matmul(ps[:, 7, T:T + 2], mine[:, tt, :],
                                              gates_.rearrange("p a b -> p (a b)"), start=tt == 0, stop=tt == 1)
                    mm.then_inc(turn_mm, 1)

                def turn_hidden(q, m, i=None):
                    add = 0 if i is None else i * LOOP
                    pe.wait_ge(r_hid, add + m + 1)
                    pe.wait_ge(turned_there, add + m + 1)
                    if m < TILES - 1:
                        pe.wait_ge(gath_dve, add + m + 3)
                    for k in range(4):
                        mm = nc.tensor.transpose(ps[:, 7, k * P:k * P + P], hid[q][:, k * P:k * P + P], ident)
                    mm.then_inc(r_hid_mm, 1)

                def down(half, u, q, m, i=None):
                    add = 0 if i is None else i * LOOP
                    pe.wait_ge(r_hid_l, add + m + 1)
                    if i is not None or 2 * m + half >= 1:
                        pe.wait_ge(r_y_l, (0 if i is None else i * (2 * LOOP)) + 2 * m + half)
                    product(6, u, hid_h[q], hid_l[q], True, True, i)

                def scatter(half, q, m, i=None, first=False, last=False):
                    pe.wait_ge(r_y_l, (0 if i is None else i * (2 * LOOP)) + 2 * m + half + 1)
                    for c in range(4):
                        o = ps[:, 2 * half + c // 2, (c % 2) * T:(c % 2 + 1) * T]
                        nc.tensor.matmul(o, y_h[half][:, c * P:c * P + P], turned[q][:, 0:T],
                                         start=first and c % 2 == 0, stop=False, skip_group_check=True)
                        mm = nc.tensor.matmul(o, y_l[half][:, c * P:c * P + P], turned[q][:, 0:T], start=False,
                                              stop=last, skip_group_check=True)
                    return mm

                def tile(u, q, m, i=None, older=True, first=False, more=True):
                    o = 1 - q
                    h, l = got_h[m // 2 % 2][:, :, m % 2, :], got_l[m // 2 % 2][:, :, m % 2, :]
                    product(4, u, h[:, 0:4, :], l[:, 0:4, :], True, False, i)
                    if older:
                        scatter(1, q, m - 2, i, first=first)
                    turn_pick(m, i)
                    product(5, u + 1, h[:, 0:4, :], l[:, 0:4, :], True, False, i)
                    if more:
                        gather(0, m, i)
                    down(0, u + 2, o, m - 1, i)
                    if more:
                        gather(1, m, i)
                    product(4, u + 3, h[:, 4:8, :], l[:, 4:8, :], False, True, i)
                    if more:
                        gather(2, m, i)
                    scatter(0, o, m - 1, i, first=not older)
                    product(5, u + 4, h[:, 4:8, :], l[:, 4:8, :], False, True, i)
                    if more:
                        gather(3, m, i)
                    down(1, u + 5, o, m - 1, i)
                    turn_hidden(q, m, i)

                for m in (-2, -1):
                    for r in range(4):
                        gather(r, m)
                pe.wait_ge(gath_act, 6)
                pe.wait_ge(gath_dve, 2)
                h, l = got_h[0][:, :, 0, :], got_l[0][:, :, 0, :]
                product(4, p0, h[:, 0:4, :], l[:, 0:4, :], True, False)
                turn_pick(0)
                gather(0, 0)
                product(5, p0 + 1, h[:, 0:4, :], l[:, 0:4, :], True, False)
                gather(1, 0)
                product(4, p0 + 2, h[:, 4:8, :], l[:, 4:8, :], False, True)
                gather(2, 0)
                product(5, p0 + 3, h[:, 4:8, :], l[:, 4:8, :], False, True)
                gather(3, 0)
                turn_hidden(0, 0)
                tile(p0 + 4, 1, 1, older=False)
                tile(p0 + 10, 0, 2, first=True)
                with pe.Fori(0, (N_EXP - 4) // LOOP) as i:
                    for m in range(3, 3 + LOOP):
                        tile(p0 + 6 * m - 2, m % 2, m, i)
                for m in range(N_EXP - 1, TILES):
                    tile(p0 + 6 * m - 2, m % 2, m, more=m < TILES - 1)
                m = TILES
                q = (m - 1) % 2
                scatter(1, 1 - q, m - 2)
                down(0, p0 + 6 * m - 2, q, m - 1)
                down(1, p0 + 6 * m - 1, q, m - 1)
                scatter(0, q, m - 1, last=True)
                scatter(1, q, m - 1, last=True).then_inc(r_hid_mm, 1)

            pe.wait_ge(ones_set, 1)
            norm(8)
            for u in u_in[0:12]:
                feature_unit(u)
            for u in u_in[12:18]:
                token_unit(u)
            for u in u_in[18:22]:
                feature_unit(u)
            u = u_in[22]
            weights_in(u)
            o = lin_bank()
            wh, wl = wview(whi, u, DC, 256), wview(wlo, u, DC, 256)
            triple(o[:, 0, :], [(wh[:, k, 0:P], wl[:, k, 0:P], xh[:, k, :], xl[:, k, :]) for k in range(DC)])
            for tt in range(2):
                for k in range(DC):
                    h, l = xh[:, k, tt * P:tt * P + P], xl[:, k, tt * P:tt * P + P]
                    oo = o[:, 1, tt * P:tt * P + P]
                    nc.tensor.matmul(oo, h, wh[:, k, P:256], start=k == 0, stop=False)
                    nc.tensor.matmul(oo, l, wh[:, k, P:256], start=False, stop=False)
                    mm = nc.tensor.matmul(oo, h, wl[:, k, P:256], start=False, stop=k == DC - 1)
            mm.then_inc(unit_used, 1)
            all_out()
            pe.wait_ge(consts_landed, 48)
            nc.tensor.matmul(ps[0:HD, 5, 0:T], ident[:, HD:P], ks[:, 0, :], start=True, stop=True)
            nc.tensor.matmul(ps[HD:P, 5, 0:T], ident[:, 0:HD], ks[:, 0, :], start=True,
                             stop=True).then_inc(kswap_mm, 1)
            pe.wait_ge(kswap_there, 1)

            def gates_between(a):
                if a % 2 == 0:
                    feature_unit(u_in[23 + a // 4], half=a % 4 // 2)

            attend(steps_a, PT_first, gates_between)
            split_in()
            for u in u_br:
                feature_unit(u, ah, al)
                if u == u_br[0]:
                    st["fresh"] = True
                feature_unit(u + 1)
            st["fresh"] = True
            residual(u_out)
            weights_in(u_router)
            wh, wl = wview(whi, u_router, DC, 36), wview(wlo, u_router, DC, 36)
            triple(lin_bank()[0:36, 0, :], [(wh[:, k, :], wl[:, k, :], xh[:, k, :], xl[:, k, :])
                                            for k in range(DC)]).then_inc(unit_used, 1)
            all_out()
            for tt in range(2):
                mm = nc.tensor.matmul(ps[:, 5, tt * T:tt * T + 36], logits[0:36, tt * P:tt * P + P], ident[0:36, 0:36],
                                      start=True, stop=True, is_transpose=True)
            mm.then_inc(logits_turned, 1)
            for tt in range(2):
                for c in range(DC):
                    at = tt * D + c * P
                    mm = nc.tensor.transpose(ps[:, at // 512, at % 512:at % 512 + P], hbuf[:, c, tt * P:tt * P + P],
                                             ident)
            mm.then_inc(h_ready, 1)
            pe.wait_ge(ranks_go, 1)
            members = rt[:, :, 224:256]
            o = ps[:, 5, 0:3 * N_EXP].rearrange("p (a e) -> p a e", a=3)
            nc.tensor.matmul(o[:, 0, :], before, members[:, 0, :], start=True, stop=True)
            nc.tensor.matmul(o[:, 1, :], ones[:], members[:, 0, :], start=True, stop=False)
            nc.tensor.matmul(o[:, 1, :], before, members[:, 1, :], start=False, stop=True)
            nc.tensor.matmul(o[:, 2, :], ones[:], members[:, 0, :], start=True, stop=False)
            nc.tensor.matmul(o[:, 2, :], ones[:], members[:, 1, :], start=False, stop=True).then_inc(ranks_mm, 1)
            split_in()
            experts(moe)
            norm(8, split=False, both=True)

            norm(8)
            for a, u in enumerate(u_ev):
                feature_unit(u)
                if a == 0:
                    norm(8, split=False)
                elif a == 2:
                    squares(0, 2)
                    squares(0, 1, at=2, bank=4)
            st["fresh"] = True
            weights_in(u_qup)
            wh, wl = wview(whi, u_qup, 2, 768), wview(wlo, u_qup, 2, 768)
            for h in range(MLA_H):
                mm = triple(ps[0:QK, h // 2, (h % 2) * T:(h % 2 + 1) * T],
                            [(wh[:, k, h * QK:(h + 1) * QK], wl[:, k, h * QK:(h + 1) * QK], ah[:, k, :], al[:, k, :])
                             for k in range(2)])
            mm.then_inc(unit_used, 1)
            pe.wait_ge(kr_there, 1)
            for a in range(2):
                mm = nc.tensor.matmul(ps[0:QK, 5, a * T:(a + 1) * T], put[0:ROPE, a, :], kr[0:ROPE, :],
                                      start=True, stop=True)
            mm.then_inc(kr_mm, 1)
            pe.wait_ge(kr_turned, 1)
            pe.wait_ge(mq_there, 1)
            all_out()
            for h in range(MLA_H):
                mm = nc.tensor.matmul(ps[0:QK, 4 + h // 2, (h % 2) * T:(h % 2 + 1) * T], swap[0:QK, :],
                                      mq[0:QK, h, :], start=True, stop=True)
            mm.then_inc(mq_mm, 1)
            weights_in(u_kvup)
            split_in()
            wh, wl = wview(whi, u_kvup, 1, 1024), wview(wlo, u_kvup, 1, 1024)
            for h in range(MLA_H):
                mm = triple(ps[0:NOPE, h // 2, (h % 2) * T:(h % 2 + 1) * T],
                            [(wh[:, 0, h * P:h * P + NOPE], wl[:, 0, h * P:h * P + NOPE], ah[:, 2, :], al[:, 2, :])])
            mm.then_inc(mk_mm, 1)
            vh = wh[:, 0, :].rearrange("p (h n) -> p h n", h=MLA_H)[:, :, NOPE:P]
            vl = wl[:, 0, :].rearrange("p (h n) -> p h n", h=MLA_H)[:, :, NOPE:P]
            pe.wait_ge(mq_turned, 1)
            for tt in range(2):
                o = ps[:, 6 + tt, :].rearrange("p (h n) -> p h n", h=MLA_H)
                h, l = ah[:, 2, tt * P:tt * P + P], al[:, 2, tt * P:tt * P + P]
                nc.tensor.matmul(o, h, vh, start=True, stop=False)
                nc.tensor.matmul(o, l, vh, start=False, stop=False)
                mm = nc.tensor.matmul(o, h, vl, start=False, stop=True)
            mm.then_inc(unit_used, 1)
            split_in()
            weights_in(u_pool)
            pe.wait_ge(kv_out, 1)
            wh, wl = wview(whi, u_pool, 4, P), wview(wlo, u_pool, 4, P)
            for half in range(2):
                o = lin_bank()
                for b in range(2):
                    g = 2 * half + b
                    mm = triple(o[:, b, :], [(wh[:, g, :], wl[:, g, :], ah[:, g, :], al[:, g, :])])
            mm.then_inc(unit_used, 1)
            pe.wait_ge(mk_there, 1)
            pe.wait_ge(mk_rope_there, 1)

            def memory_unit(l, a):
                if a < 4:
                    feature_unit(u_kv[l][a])
                else:
                    token_unit(u_kv[l][a])

            def memory_between(a):
                if a == 0:
                    split_in()
                memory_unit(0, a)

            attend(steps_m, PT_later, memory_between)
            st["fresh"] = True
            residual(u_evo)

            def cross(l):
                feature_unit(u_xa[l][0][0])
                feature_unit(u_xa[l][0][1])
                all_out()

                def queries_between(a):
                    if a in (2, 4):
                        all_out()
                    if a in (0, 2):
                        feature_unit(u_xa[l][0][2 + a // 2])

                attend(steps_x[l], PT_later, queries_between)
                st["fresh"] = True
                residual(u_xa[l][1])

            cross(0)
            gated(ffn[0][0], ffn[0][1], trio0[0])
            norm(8, both=True)
            for u in u_od:
                feature_unit(u)
            for a in range(2):
                u = u_rg + a
                weights_in(u)
                wh, wl = wview(whi, u, DC, 256), wview(wlo, u, DC, 256)
                for c in range(DC):
                    h = c // 2
                    if a == 0 and c % 2 == 0:
                        split_in()
                    if a == 1 and c == 4:
                        pe.wait_ge(lru_r, 1)
                    sh, sl = (ah, al) if h < 2 else (xh, xl)
                    at = (2 * a + c // 4) % 3 * 2 + c % 4 // 2
                    mm = triple(ps[:, at, (c % 2) * T:(c % 2 + 1) * T],
                                [(wh[:, 2 * h + k, (c % 2) * P:(c % 2) * P + P],
                                  wl[:, 2 * h + k, (c % 2) * P:(c % 2) * P + P], lru_in(sh, h, k),
                                  lru_in(sl, h, k)) for k in range(2)])
                mm.then_inc(unit_used, 1)
            st["fresh"] = True
            for a in range(8):
                memory_unit(1, a)
            st["fresh"] = True
            residual(u_odo)
            cross(1)
            gated(ffn[1][0], ffn[1][1], trio0[1])
            norm(8, split=False, both=True)

        @block.scalar
        def _(act):
            st = dict(hi=0, lin=0, step=0, split=0, norm=0, sums=0)

            def hi(u, i=None, step=6):
                act.wait_ge(raw_landed[u % RAW], (0 if i is None else i * (step // 6 * 16)) + 16 * (u // RAW + 1))
                if i is not None or u >= HL:
                    act.wait_ge(unit_used, (0 if i is None else i * step) + (u - HL + 1))
                n = usize(u)
                nc.scalar.activation(whi[u % HL][:, 0:n], raw[u % RAW][:, 0:n], ACT.Copy).then_inc(hi_ready, 1)

            def ahead(u):
                while st["hi"] < min(u + HL, len(units)):
                    hi(st["hi"])
                    st["hi"] += 1

            def split_high(src, dst, used=None):
                st["split"] += 1
                act.wait_ge(h_ready, st["split"])
                if used is not None:
                    act.wait_ge(unit_used, used)
                nc.scalar.activation(dst, src, ACT.Copy).then_inc(xh_ready, 1)

            def square_sums():
                for b in range(4):
                    st["sums"] += 1
                    act.wait_ge(x_summed, st["sums"])
                    nc.scalar.activation(hbuf[:, 2 * b:2 * b + 2, :], x[:, 2 * b:2 * b + 2, :],
                                         ACT.Square).then_inc(sq_ready, 1)

            def split_highs(src, used):
                for k in range(0, DC, 2):
                    split_high(src[:, k:k + 2, :], xh[:, k:k + 2, :], used)

            def norm(c, split=True, scale=None, at=0, to=None):
                st["norm"] += 1
                act.wait_ge(ms_ready, st["norm"])
                s = rstd[:] if scale is None else scale
                nc.scalar.activation(s, s, ACT.Sqrt).then_inc(rstd_ready, 1)
                for k in range(at, at + c if split else 0, 2):
                    split_high(hbuf[:, k:min(k + 2, at + c), :], (to or xh)[:, k:min(k + 2, at + c), :])

            def evac(u, m, dst, func=ACT.Copy):
                act.wait_ge(unit_used, u + 1)
                nc.scalar.activation(dst, ps[:, 6 + m % 2, :].rearrange("p (c t) -> p c t", c=2),
                                     func).then_inc(lin_evac[m % 2], 1)

            def stage(us, dst=None, every=False, func=ACT.Copy):
                for a, u in enumerate(us):
                    ahead(u)
                    if dst and (every or st["lin"] % 2 == 0):
                        evac(u, st["lin"], dst(a), func)
                    st["lin"] += 1

            def exps(s, step):
                act.wait_ge(att_max, s + 1)
                b, nk = s % 3, step["nk"]
                n = len(step["scores"])
                if step["sink"] is not None:
                    for g in range(2):
                        nc.scalar.activation(sm[:, b, 12 + g:13 + g],
                                             sink_row[:, step["sink"] + g:step["sink"] + g + 1],
                                             ACT.Exp, bias=sm[:, b, 3 + g:4 + g])
                if step["merged"]:
                    last = nc.scalar.activation(S[b][:, 0:n, 0:nk], S[b][:, 0:n, 0:nk], ACT.Exp,
                                                bias=sm[:, b, 3:4], scale=step["scale"], accum_out=sm[:, b, 6:7])
                else:
                    for g in range(n):
                        last = nc.scalar.activation(S[b][:, g, 0:nk], S[b][:, g, 0:nk], ACT.Exp,
                                                    bias=sm[:, b, 3 + g:4 + g], scale=step["scale"],
                                                    accum_out=sm[:, b, 6 + g:7 + g])
                last.then_inc(att_exp, 1)

            def copy_turned(s, step, PT):
                act.wait_ge(att_turned, s + 1)
                if s >= 2:
                    act.wait_ge(att_mixed, s - 1)
                n = len(step["scores"]) * step["nk"] // P
                last = nc.scalar.activation(PT[s % 2][:, 0:min(n, 4), :],
                                            ps[:, 2, 0:min(n, 4) * P].rearrange("p (b q) -> p b q", q=P), ACT.Copy)
                if n > 4:
                    last = nc.scalar.activation(PT[s % 2][:, 4:n, :],
                                                ps[:, 3, 0:(n - 4) * P].rearrange("p (b q) -> p b q", q=P), ACT.Copy)
                last.then_inc(att_pt, 1)

            def attend(steps, PT, between=None):
                base = st["step"]
                exps(base, steps[0])
                for a, step in enumerate(steps):
                    if a + 1 < len(steps):
                        exps(base + a + 1, steps[a + 1])
                    copy_turned(base + a, step, PT)
                    if between:
                        between(a)
                st["step"] += len(steps)

            def experts(p0):
                def gathered(r, m, i=None):
                    act.wait_ge(gath_mm, (0 if i is None else i * (4 * LOOP)) + 8 + 4 * m + r + 1)
                    dst = (got_l if m % 2 else got_h)[(m // 2 + 1) % 2][:, 2 * r:2 * r + 2, :, :]
                    nc.scalar.activation(dst.rearrange("p k a s -> p (k a s)"), ps[:, gather_bank(r, m), :],
                                         ACT.Copy).then_inc(gath_act, 1)

                def turned_out(q, m, i=None):
                    act.wait_ge(turn_mm, (0 if i is None else i * LOOP) + m + 1)
                    nc.scalar.activation(turned[q][:], ps[:, 7, 0:T + 2], ACT.Copy).then_inc(turned_there, 1)

                def silu(u, q, i=None):
                    act.wait_ge(unit_used, (0 if i is None else i * (6 * LOOP)) + u)
                    nc.scalar.activation(sil[q], ps[:, 4, :], ACT.Silu).then_inc(r_silu, 1)

                def y_high(half, u, i=None):
                    act.wait_ge(unit_used, (0 if i is None else i * (6 * LOOP)) + u + 1)
                    nc.scalar.activation(y_h[half][:], ps[:, 6, :], ACT.Copy).then_inc(r_y_h, 1)

                def hidden_high(q, m, i=None):
                    act.wait_ge(r_hid_mm, (0 if i is None else i * LOOP) + m + 1)
                    nc.scalar.activation(hid_h[q], ps[:, 7, :].rearrange("p (k s) -> p k s", k=4),
                                         ACT.Copy).then_inc(r_hid_h, 1)

                def tile(u, q, m, i=None, more=True):
                    turned_out(q, m, i)
                    hi(u + 3, i, 6 * LOOP)
                    if more:
                        gathered(0, m, i)
                    hi(u + 4, i, 6 * LOOP)
                    y_high(0, u + 2, i)
                    if more:
                        gathered(1, m, i)
                    hi(u + 5, i, 6 * LOOP)
                    if more:
                        gathered(2, m, i)
                    hi(u + 6, i, 6 * LOOP)
                    silu(u + 5, q, i)
                    hi(u + 7, i, 6 * LOOP)
                    y_high(1, u + 5, i)
                    hidden_high(q, m, i)
                    hi(u + 8, i, 6 * LOOP)

                for m in (-2, -1):
                    for r in range(3):
                        gathered(r, m)
                ahead(p0)
                turned_out(0, 0)
                gathered(0, 0)
                hi(p0 + 3)
                gathered(1, 0)
                hi(p0 + 4)
                gathered(2, 0)
                hi(p0 + 5)
                silu(p0 + 4, 0)
                hidden_high(0, 0)
                hi(p0 + 6)
                for m in (1, 2):
                    tile(p0 + 6 * m - 2, m % 2, m)
                act.wait_ge(extra_gates, 1)
                nc.scalar.activation(gate_hl[:, :, N_EXP:TILES, 0], gate[:, :, N_EXP:],
                                     ACT.Copy).then_inc(gate_h_there, 1)
                with act.Fori(0, (N_EXP - 4) // LOOP) as i:
                    for m in range(3, 3 + LOOP):
                        tile(p0 + 6 * m - 2, m % 2, m, i)
                for m in range(N_EXP - 1, TILES):
                    tile(p0 + 6 * m - 2, m % 2, m, more=m < TILES - 1)
                y_high(0, p0 + 6 * TILES - 2)
                y_high(1, p0 + 6 * TILES - 1)
                st["hi"] = p0 + 6 * TILES + 1

            def gated(p0, n, trio):
                def gate(u, j, free, i=None):
                    act.wait_ge(unit_used, (0 if i is None else i * 6) + (u + 2))
                    if free is not None:
                        act.wait_ge(hid_ready, free)
                    nc.scalar.activation(sil[j % 2], ps[:, 4 + (2 * j) % 4, :], ACT.Silu).then_inc(silu_done, 1)

                def high(j, ready, used=None, i=None):
                    act.wait_ge(hid_ready, ready)
                    if used is not None:
                        act.wait_ge(unit_used, (0 if i is None else i * 6) + used)
                    nc.scalar.activation(ah[:, 2 * (j % 2):2 * (j % 2) + 2, :],
                                         hid[j % 2].rearrange("p (c t) -> p c t", c=2), ACT.Copy).then_inc(ah_ready, 1)

                ahead(p0)
                gate(p0, 0, None)
                hi(p0 + 3)
                high(0, trio + 1)
                hi(p0 + 4)
                hi(p0 + 5)
                gate(p0 + 2, 1, None)
                hi(p0 + 6)
                high(1, trio + 2)
                body = (n - 2) // 2
                with act.Fori(0, body) as i:
                    for j in (2, 3):
                        u = p0 + 3 * j - 1
                        hi(u + 2, i)
                        hi(u + 3, i)
                        gate(u, j, i * 2 + (trio + j - 1), i)
                        hi(u + 4, i)
                        high(j, i * 2 + (trio + j + 1), u, i)
                for j in range(2 + 2 * body, n):
                    u = p0 + 3 * j - 1
                    hi(u + 2)
                    hi(u + 3)
                    gate(u, j, trio + j - 1)
                    if u + 4 < len(units):
                        hi(u + 4)
                    high(j, trio + j + 1, u)
                st["hi"] = min(p0 + 3 * n + 1, len(units))

            hi(0)
            hi(1)
            st["hi"] = 2
            norm(8)
            stage(u_in[0:6], lambda a: qd[:, 2 * a:2 * a + 2, :])
            stage(u_in[6:12], lambda a: kd[:, 2 * a:2 * a + 2, :])
            stage(u_in[12:18], lambda a: vd[:, :, a * 256:(a + 1) * 256])
            stage(u_in[18:22], lambda a: qs[:, 2 * a:2 * a + 2, :])
            stage(u_in[22:23])

            def gates_out(a):
                k = a // 4
                if a == 21:
                    split_high(qd[:, 0:4, :], ah[:])
                if a % 4 == 2:
                    u = u_in[23 + k]
                    ahead(u)
                    evac(u, st["lin"], sg[:, 2 * k:2 * k + 2, :])
                    st["lin"] += 1

            attend(steps_a, PT_first, gates_out)
            split_highs(qs, u_in[-1] + 1)
            nc.scalar.activation(sg, sg, ACT.Sigmoid).then_inc(gates_there, 1)
            stage(range(u_br[0], u_br[-1] + 2))
            split_highs(hbuf, u_br[-1] + 2)
            stage(u_out)
            norm(8)
            stage([u_router])
            act.wait_ge(route_grp, 1)
            nc.scalar.activation(rt[:, :, 4:8], rt[:, :, 4:8], ACT.Exp).then_inc(route_grp_exp, 1)
            act.wait_ge(route_two, 1)
            nc.scalar.activation(rt[:, :, 24:25], rt[:, :, 23:24], ACT.Exp).then_inc(route_two_exp, 1)
            split_high(ps[:, 0:4, :], xh[:].rearrange("p (b c) t -> p b (c t)", b=4), u_router + 1)
            act.wait_ge(ranks_go, 2)
            nc.scalar.activation(gate_hl[:, :, 0:N_EXP, 0], gate[:, :, 0:N_EXP], ACT.Copy).then_inc(gate_h_there, 1)
            experts(moe)
            square_sums()
            norm(8, split=False)
            norm(8)
            stage(u_ev[0:2])
            norm(8, split=False, scale=mem_rstd)
            stage(u_ev[2:3])
            norm(2, to=ah)
            norm(1, at=2, to=ah)
            stage(u_ev[3:])
            act.wait_ge(angles, 1)
            nc.scalar.activation(sinr[0:QK, :], sinr[0:QK, :], ACT.Sin)
            nc.scalar.activation(cosr[0:QK, :], cosr[0:QK, :], ACT.Sin).then_inc(trig, 1)
            ahead(u_qup)
            act.wait_ge(unit_used, u_qup + 1)
            nc.scalar.activation(mq[0:QK, :, :], ps[0:QK, 0:4, :].rearrange("p b (c t) -> p (b c) t", c=2),
                                 ACT.Copy).then_inc(mq_there, 1)
            ahead(u_kvup)
            act.wait_ge(mk_mm, 1)
            act.wait_ge(pooled_there, 1)
            nc.scalar.activation(mk[0:NOPE, :, :], ps[0:NOPE, 0:4, :].rearrange("p b (c t) -> p (b c) t", c=2),
                                 ACT.Copy).then_inc(mk_there, 1)
            split_high(ypool, ah[:], u_kvup + 1)
            split_high(mem, xh[:], u_ev[-1] + 1)
            ahead(u_pool)
            act.wait_ge(unit_used, u_pool + 1)
            for half in range(2):
                m = st["lin"] + half
                for b in range(2):
                    last = nc.scalar.activation(ypool[:, 2 * half + b, :],
                                                ps[:, 6 + m % 2, b * T:b * T + T], ACT.Identity,
                                                scale=vcol("pool_scale", 2 * half + b))
                last.then_inc(lin_evac[m % 2], 1)
            st["lin"] += 2

            def memory_out(l, a):
                u = u_kv[l][a]
                ahead(u)
                evac(u, st["lin"], xk[:, 2 * a:2 * a + 2, :] if a < 4 else xv[l][:, :, (a - 4) * 256:(a - 3) * 256])
                st["lin"] += 1

            attend(steps_m, PT_later, lambda a: memory_out(0, a))
            for src, at in ((ypool, 0), (my, 4)):
                for k in (0, 2):
                    split_high(src[:, k:k + 2, :], xh[:, at + k:at + k + 2, :], u_kv[0][-1] + 1)
            stage(u_evo)

            def cross(l):
                norm(8)
                uq = u_xa[l][0]
                stage(uq[0:2], lambda a: xq[:, 2 * a:2 * a + 2, :], every=True)

                def queries_out(a):
                    if a in (0, 2):
                        h = 2 + a // 2
                        evac(uq[h], st["lin"], xq[:, 2 * h:2 * h + 2, :])
                        ahead(uq[h])
                        st["lin"] += 1

                attend(steps_x[l], PT_later, queries_out)
                split_highs(xq, uq[-1] + 1)
                stage(u_xa[l][1])

            cross(0)
            norm(8)
            act.wait_ge(lam_abs, 1)
            nc.scalar.activation(lsm[:, 1, :], lsm[:, 0, :], ACT.Exp, scale=-1.0).then_inc(lam_exp, 1)
            gated(ffn[0][0], ffn[0][1], trio0[0])
            square_sums()
            norm(8)
            for a in range(4):
                stage(u_od[a:a + 1])
                if a in (2, 3):
                    two = slice(2 * a - 4, 2 * a - 2)
                    split_high(lxc[:, two, :], ah[:, two, :])
            stage(u_od[4:8], lambda a: lgate[:, 2 * a:2 * a + 2, :], every=True, func=ACT.Gelu_apprx_tanh)
            for a in (2, 3):
                two = slice(2 * a, 2 * a + 2)
                split_high(lxc[:, two, :], xh[:, two, :], u_od[-1] + 1)
            ahead(u_rg)
            act.wait_ge(unit_used, u_rg + 1)
            for c in range(DC):
                last = nc.scalar.activation(lr[:, c, :], ps[:, c // 2, (c % 2) * T:(c % 2 + 1) * T], ACT.Sigmoid,
                                            bias=vcol("b_r", c))
            last.then_inc(lru_r, 1)
            ahead(u_rg + 1)
            act.wait_ge(unit_used, u_rg + 2)
            for c in range(DC):
                at = (2 + c // 4) % 3 * 2 + c % 4 // 2
                last = nc.scalar.activation(li[:, c, :], ps[:, at, (c % 2) * T:(c % 2 + 1) * T], ACT.Sigmoid,
                                            bias=vcol("b_i", c))
            last.then_inc(lru_i, 1)
            split_highs(mem, u_rg + 2)
            act.wait_ge(lam_scale, 1)
            act.wait_ge(lru_r, 1)
            for c in range(DC):
                last = nc.scalar.activation(lrc[:, c, :], lr[:, c, :], ACT.Exp, scale=lsm[:, 6, c:c + 1])
            last.then_inc(lru_a, 1)
            ahead(u_kv[1][0])
            for c in range(DC):
                last = nc.scalar.activation(lr[:, c, :], lr[:, c, :], ACT.Tanh, scale=lsm[:, 7, c:c + 1])
            last.then_inc(lru_t, 1)
            memory_out(1, 0)
            act.wait_ge(lru_t_max, 1)
            nc.scalar.activation(lr, lr, ACT.Sqrt).then_inc(lru_root, 1)
            for a in range(1, 8):
                memory_out(1, a)
            split_highs(lgate, u_kv[1][-1] + 1)
            stage(u_odo)
            cross(1)
            norm(8)
            gated(ffn[1][0], ffn[1][1], trio0[1])
            square_sums()
            norm(8, split=False)

        @block.vector
        def _(dve):
            st = dict(lo=0, lin=0, step=0, split=0, norm=0, chain=0, y=0, sums=0)
            v = nc.vector

            def link(ins):
                st["chain"] += 1
                ins.then_inc(dve_step, 1)
                dve.wait_ge(dve_step, st["chain"])

            def lo(u, i=None, step=6):
                dve.wait_ge(hi_ready, (0 if i is None else i * step) + (u + 1))
                if i is not None or u >= HL:
                    dve.wait_ge(unit_used, (0 if i is None else i * step) + (u - HL + 1))
                n = usize(u)
                v.tensor_tensor(wlo[u % HL][:, 0:n], raw[u % RAW][:, 0:n], whi[u % HL][:, 0:n].bitcast(F32),
                                ALU.subtract).then_inc(lo_ready, 1)

            def ahead(u):
                while st["lo"] < min(u + HL, len(units)):
                    lo(st["lo"])
                    st["lo"] += 1

            def split_low(src, high, low, used=None):
                st["split"] += 1
                dve.wait_ge(xh_ready, st["split"])
                if used is not None:
                    dve.wait_ge(unit_used, used)
                v.tensor_tensor(low, src, high.bitcast(F32), ALU.subtract).then_inc(xl_ready, 1)

            def split_lows(src, used):
                for k in range(0, DC, 2):
                    split_low(src[:, k:k + 2, :], xh[:, k:k + 2, :], xl[:, k:k + 2, :], used)

            def square(src, a, b):
                sq = v.tensor_tensor(hbuf[:, a:b, :], src[:, a:b, :], src[:, a:b, :], ALU.mult)
                if b - a == 2:
                    link(sq)
                    sq = v.tensor_tensor(hbuf[:, a, :], hbuf[:, a, :], hbuf[:, a + 1, :], ALU.add)
                sq.then_inc(sq_ready, 1)

            def norm(src, c, width, gain, dst=None, squared=False, done=None, at=0, bank=5, between=None,
                     parts=None):
                for k in range(0, 0 if squared else c, 2):
                    square(src, k, min(k + 2, c))
                root(width, rstd[:], bank)
                if between:
                    between()
                dve.wait_ge(rstd_ready, st["norm"])
                to = hbuf if dst is None else dst
                high, low = parts or (xh, xl)
                for k in range(at, at + c, 2):
                    last = scaled(to, src, k, min(k + 2, at + c), gain, rstd[:], k - at)
                    if dst is None:
                        last.then_inc(h_ready, 1)
                        if k >= at + 2:
                            split_low(hbuf[:, k - 2:k, :], high[:, k - 2:k, :], low[:, k - 2:k, :])
                    elif done is not None:
                        last.then_inc(done, 1)
                if dst is None:
                    split_low(hbuf[:, k:at + c, :], high[:, k:at + c, :], low[:, k:at + c, :])
                return last

            def root(width, to, bank=5):
                st["norm"] += 1
                dve.wait_ge(ss_ready, st["norm"])
                link(v.tensor_scalar(to, ps[:, bank, 0:T], 1.0 / width, EPS, ALU.mult, ALU.add))
                v.reciprocal(to, to).then_inc(ms_ready, 1)

            def scaled(to, src, a, b, gain, scale, g=None):
                g = a if g is None else g
                for j in range(a, b):
                    last = v.scalar_tensor_tensor(out=to[:, j, :], in0=src[:, j, :], scalar=vcol(gain, g + j - a),
                                                  in1=scale, op0=ALU.mult, op1=ALU.mult)
                return last

            def bank(m):
                return ps[:, 6 + m % 2, :].rearrange("p (c t) -> p c t", c=2)

            def stage(us, dst=None):
                for a, u in enumerate(us):
                    ahead(u)
                    m = st["lin"]
                    if dst and m % 2 == 1:
                        dve.wait_ge(unit_used, u + 1)
                        v.tensor_copy(dst(a), bank(m)).then_inc(lin_evac[m % 2], 1)
                    st["lin"] += 1

            def all_out():
                for b in range(2):
                    dve.wait_ge(lin_evac[b], (st["lin"] + 1 - b) // 2)

            def add_sums():
                for b in range(4):
                    two = x[:, 2 * b:2 * b + 2, :]
                    v.tensor_tensor(two, ps[:, b, :].rearrange("p (c t) -> p c t", c=2), two,
                                    ALU.add).then_inc(x_summed, 1)
                st["sums"] += 4
                dve.wait_ge(x_summed, st["sums"])

            def residual(us):
                for a, u in enumerate(us):
                    ahead(u)
                    m = st["lin"]
                    dve.wait_ge(unit_used, u + 1)
                    v.tensor_tensor(x[:, 2 * a:2 * a + 2, :], bank(m), x[:, 2 * a:2 * a + 2, :],
                                    ALU.add).then_inc(lin_evac[m % 2], 1)
                    dve.wait_ge(lin_evac[m % 2], m // 2 + 1)
                    square(x, 2 * a, 2 * a + 2)
                    st["lin"] += 1
                all_out()

            def bias_max(s, step):
                dve.wait_ge(att_scored, s + 1)
                if s >= 3:
                    dve.wait_ge(att_turned, s - 2)
                b, nk, n = s % 3, step["nk"], len(step["scores"])
                for g in range(n):
                    src = score_bank(step, g)
                    dst = S[b][:, g, 0:nk]
                    if step["bias"] is None:
                        last = v.tensor_copy(dst, src)
                    elif step["bias"] == "causal":
                        last = v.tensor_tensor(dst, src, causal[:, T - nk:T], ALU.add)
                    else:
                        pi, slope = step["bias"][g]
                        last = v.scalar_tensor_tensor(out=dst, in0=pat[:, pi, T - nk:T], scalar=-slope, in1=src,
                                                      op0=ALU.mult, op1=ALU.add)
                last.then_inc(att_biased, 1)
                dve.wait_ge(att_biased, s + 1)
                if step["merged"]:
                    link(v.tensor_reduce(sm[:, b, 0:1], S[b][:, 0:n, 0:nk], AX.XY, ALU.max))
                    n = 1
                else:
                    link(v.tensor_reduce(sm[:, b, 0:n], S[b][:, 0:n, 0:nk], AX.X, ALU.max))
                if step["sink"] is not None:
                    link(v.scalar_tensor_tensor(out=sm[:, b, 0:n], in0=sm[:, b, 0:n], scalar=step["scale"],
                                                in1=sink_row[:, step["sink"]:step["sink"] + n],
                                                op0=ALU.mult, op1=ALU.max))
                    v.tensor_scalar(sm[:, b, 3:3 + n], sm[:, b, 0:n], -1.0, None, ALU.mult).then_inc(att_max, 1)
                else:
                    v.tensor_scalar(sm[:, b, 3:3 + n], sm[:, b, 0:n], -step["scale"], None,
                                    ALU.mult).then_inc(att_max, 1)

            def probs(s, step):
                dve.wait_ge(att_exp, s + 1)
                b, nk, n = s % 3, step["nk"], len(step["scores"])
                k = 1 if step["merged"] else n
                if step["sink"] is not None:
                    link(v.tensor_tensor(sm[:, b, 6:6 + k], sm[:, b, 6:6 + k], sm[:, b, 12:12 + k], ALU.add))
                link(v.reciprocal(sm[:, b, 9:9 + k], sm[:, b, 6:6 + k]))
                if step["merged"]:
                    last = v.tensor_scalar(S[b][:, 0:n, 0:nk], S[b][:, 0:n, 0:nk], sm[:, b, 9:10], None, ALU.mult)
                else:
                    for g in range(n):
                        last = v.tensor_scalar(S[b][:, g, 0:nk], S[b][:, g, 0:nk], sm[:, b, 9 + g:10 + g], None,
                                               ALU.mult)
                last.then_inc(att_probs, 1)

            def attend(steps, y_of, between=None):
                base = st["step"]

                def out(a):
                    step = steps[a]
                    if step["last"]:
                        dve.wait_ge(att_mixed, base + a + 1)
                        w = len(step["y"])
                        v.tensor_copy(y_of(st["yk"], w), ps[:, 4 + st["y"] % 2, 0:w * T].rearrange("p (c t) -> p c t",
                                                                                    c=w)).then_inc(att_out, 1)
                        st["y"] += 1
                        st["yk"] += w

                st["yk"] = 0
                bias_max(base, steps[0])
                bias_max(base + 1, steps[1])
                for a, step in enumerate(steps):
                    probs(base + a, step)
                    if a >= 2:
                        out(a - 2)
                    if a + 2 < len(steps):
                        bias_max(base + a + 2, steps[a + 2])
                    if between:
                        between(a)
                out(len(steps) - 2)
                out(len(steps) - 1)
                dve.wait_ge(att_out, st["y"])
                st["step"] += len(steps)

            def experts(p0):
                def choose(pair, i=None):
                    if pair >= 2:
                        dve.wait_ge(turn_mm, (0 if i is None else i * LOOP) + 2 * pair - 2)
                    for a in range(2):
                        m = 2 * pair + a
                        for tt in range(2):
                            at = rank[:, tt, bass.ds(i * LOOP + m, 1)] if i is not None else rank[:, tt, m:m + 1]
                            last = v.tensor_scalar(pick[pair % 2][:, tt, a * P:a * P + P], slot_no, at, None,
                                                   ALU.is_equal)
                    last.then_inc(pick_ready, 1)

                def gathered(m, i=None):
                    dve.wait_ge(gath_mm, (0 if i is None else i * (4 * LOOP)) + 8 + 4 * m + 4)
                    dst = (got_l if m % 2 else got_h)[(m // 2 + 1) % 2][:, 6:8, :, :]
                    v.tensor_copy(dst.rearrange("p k a s -> p (k a s)"),
                                  ps[:, gather_bank(3, m), :]).then_inc(gath_dve, 1)

                def gate_of_slots(q, m, i=None):
                    dve.wait_ge(turned_there, (0 if i is None else i * LOOP) + m + 1)
                    v.tensor_reduce(slot_gate[:, q:q + 1], turned[q][:, T:T + 2].bitcast(F32), AX.X,
                                    ALU.add)

                def hidden(u, q, m, i=None):
                    add = 0 if i is None else i * LOOP
                    dve.wait_ge(unit_used, (0 if i is None else i * (6 * LOOP)) + u)
                    dve.wait_ge(r_silu, add + m + 1)
                    v.scalar_tensor_tensor(out=hid[q], in0=ps[:, 5, :], scalar=slot_gate[:, q:q + 1], in1=sil[q],
                                           op0=ALU.mult, op1=ALU.mult).then_inc(r_hid, 1)

                def y_low(half, m, i=None):
                    dve.wait_ge(r_y_h, (0 if i is None else i * (2 * LOOP)) + 2 * m + half + 1)
                    v.tensor_tensor(y_l[half][:], ps[:, 6, :], y_h[half][:].bitcast(F32),
                                    ALU.subtract).then_inc(r_y_l, 1)

                def hidden_low(q, m, i=None):
                    dve.wait_ge(r_hid_h, (0 if i is None else i * LOOP) + m + 1)
                    v.tensor_tensor(hid_l[q], ps[:, 7, :].rearrange("p (k s) -> p k s", k=4), hid_h[q].bitcast(F32),
                                    ALU.subtract).then_inc(r_hid_l, 1)

                def tile(u, q, m, i=None, more=True):
                    gate_of_slots(q, m, i)
                    lo(u + 3, i, 6 * LOOP)
                    if m % 2 == 1 and (m + 3) // 2 < PAIRS:
                        choose((m + 3) // 2, i)
                    lo(u + 4, i, 6 * LOOP)
                    y_low(0, m - 1, i)
                    lo(u + 5, i, 6 * LOOP)
                    lo(u + 6, i, 6 * LOOP)
                    if more:
                        gathered(m, i)
                    hidden(u + 5, q, m, i)
                    lo(u + 7, i, 6 * LOOP)
                    y_low(1, m - 1, i)
                    hidden_low(q, m, i)
                    lo(u + 8, i, 6 * LOOP)

                choose(0)
                choose(1)
                gathered(-2)
                gathered(-1)
                ahead(p0)
                gate_of_slots(0, 0)
                lo(p0 + 3)
                lo(p0 + 4)
                lo(p0 + 5)
                gathered(0)
                hidden(p0 + 4, 0, 0)
                hidden_low(0, 0)
                lo(p0 + 6)
                for m in (1, 2):
                    tile(p0 + 6 * m - 2, m % 2, m)
                dve.wait_ge(extra_gates, 1)
                dve.wait_ge(gate_h_there, 2)
                link(v.tensor_tensor(gate_hl[:, :, N_EXP:TILES, 1], gate[:, :, N_EXP:],
                                     gate_hl[:, :, N_EXP:TILES, 0].bitcast(F32), ALU.subtract))
                with dve.Fori(0, (N_EXP - 4) // LOOP) as i:
                    for m in range(3, 3 + LOOP):
                        tile(p0 + 6 * m - 2, m % 2, m, i)
                for m in range(N_EXP - 1, TILES):
                    tile(p0 + 6 * m - 2, m % 2, m, more=m < TILES - 1)
                y_low(0, TILES - 1)
                y_low(1, TILES - 1)
                st["lo"] = p0 + 6 * TILES + 1
                dve.wait_ge(r_hid_mm, TILES + 1)
                add_sums()

            def gated(p0, n, trio):
                def hidden(u, j, g, free=False, i=None):
                    dve.wait_ge(unit_used, (0 if i is None else i * 6) + (u + 2))
                    if free:
                        dve.wait_ge(al_ready, g - 1)
                    o = hid[j % 2].rearrange("p (c t) -> p c t", c=2)
                    up_ps = ps[:, 5 + (2 * j) % 4, :].rearrange("p (c t) -> p c t", c=2)
                    s = sil[j % 2].rearrange("p (c t) -> p c t", c=2)
                    dve.wait_ge(silu_done, g + 1)
                    v.tensor_tensor(o, up_ps, s, ALU.mult).then_inc(hid_ready, 1)

                def low(j, g, used=None, i=None):
                    dve.wait_ge(ah_ready, g + 1)
                    if used is not None:
                        dve.wait_ge(unit_used, (0 if i is None else i * 6) + used)
                    v.tensor_tensor(al[:, 2 * (j % 2):2 * (j % 2) + 2, :],
                                    hid[j % 2].rearrange("p (c t) -> p c t", c=2),
                                    ah[:, 2 * (j % 2):2 * (j % 2) + 2, :].bitcast(F32),
                                    ALU.subtract).then_inc(al_ready, 1)

                ahead(p0)
                hidden(p0, 0, trio)
                lo(p0 + 3)
                low(0, trio)
                lo(p0 + 4)
                lo(p0 + 5)
                hidden(p0 + 2, 1, trio + 1)
                lo(p0 + 6)
                low(1, trio + 1)
                body = (n - 2) // 2
                with dve.Fori(0, body) as i:
                    for j in (2, 3):
                        u = p0 + 3 * j - 1
                        lo(u + 2, i)
                        lo(u + 3, i)
                        hidden(u, j, i * 2 + (trio + j), True, i)
                        lo(u + 4, i)
                        low(j, i * 2 + (trio + j), u, i)
                for j in range(2 + 2 * body, n):
                    u = p0 + 3 * j - 1
                    lo(u + 2)
                    lo(u + 3)
                    hidden(u, j, trio + j, True)
                    if u + 4 < len(units):
                        lo(u + 4)
                    low(j, trio + j, u)
                st["lo"] = min(p0 + 3 * n + 1, len(units))
                dve.wait_ge(unit_used, p0 + 3 * n)
                add_sums()

            v.memset(ones[:], 1.0).then_inc(ones_set, 1)
            for k in range(0, DC, 2):
                dve.wait_ge(x_landed[k // 2], 16)
                square(x, k, k + 2)
            lo(0)
            dve.wait_ge(vec_landed, 16)
            norm(x[:], 8, D, "g_mix", squared=True, between=lambda: lo(1))
            st["lo"] = 2
            stage(u_in[0:6], lambda a: qd[:, 2 * a:2 * a + 2, :])
            stage(u_in[6:12], lambda a: kd[:, 2 * a:2 * a + 2, :])
            stage(u_in[12:18], lambda a: vd[:, :, a * 256:(a + 1) * 256])
            stage(u_in[18:22], lambda a: qs[:, 2 * a:2 * a + 2, :])
            ahead(u_in[22])
            dve.wait_ge(unit_used, u_in[22] + 1)
            v.tensor_copy(ks, bank(22)[:, 0:1, :])
            v.tensor_copy(vs, bank(22)[:, 1, :].rearrange("p (a b) -> p a b", a=2)).then_inc(lin_evac[0], 1)
            st["lin"] += 1
            dve.wait_ge(consts_landed, 48)
            dve.wait_ge(kswap_mm, 1)
            v.tensor_copy(kswap[:, 0, :], ps[:, 5, 0:T]).then_inc(kswap_there, 1)

            def gates_ahead(a):
                if a == 21:
                    dve.wait_ge(att_out, 4)
                    dve.sem_inc(h_ready, 1)
                    split_low(qd[:, 0:4, :], ah[:], al[:])
                if a % 4 == 3:
                    ahead(u_in[23 + a // 4])
                    st["lin"] += 1

            def y_a(k, w):
                return qd[:, k:k + w, :] if k < 4 else qs[:, k - 4:k - 4 + w, :]

            attend(steps_a, y_a, gates_ahead)
            all_out()
            dve.sem_inc(h_ready, 4)
            split_lows(qs, u_in[-1] + 1)
            dve.wait_ge(gates_there, 1)
            for k, u in enumerate(u_br):
                two = slice(2 * k, 2 * k + 2)
                sd, ss = sg[:, two, :], sg[:, 8 + 2 * k:10 + 2 * k, :]
                ahead(u)
                m = st["lin"]
                dve.wait_ge(unit_used, u + 1)
                v.tensor_tensor(hbuf[:, two, :], bank(m), sd, ALU.mult).then_inc(lin_evac[m % 2], 1)
                ahead(u + 1)
                dve.wait_ge(unit_used, u + 2)
                v.tensor_tensor(ss, bank(m + 1), ss, ALU.mult).then_inc(lin_evac[(m + 1) % 2], 1)
                st["lin"] += 2
                all_out()
                v.tensor_tensor(hbuf[:, two, :], hbuf[:, two, :], ss, ALU.add).then_inc(h_ready, 1)
            split_lows(hbuf, u_br[-1] + 2)
            dve.wait_ge(x_again, 16)
            residual(u_out)
            dve.sem_inc(moe_starts, 1)
            norm(x[:], 8, D, "g_ffn", squared=True)

            def col(a, n=1):
                return rt[:, :, a:a + n]

            def wide(a, n):
                return col(a).broadcast_to([P, 2, n])

            gkeys = gkey.unsqueeze(1).broadcast_to([P, 2, N_GRP])
            ekeys = ekey.unsqueeze(1).broadcast_to([P, 2, N_EXP])
            ahead(u_router)
            dve.wait_ge(unit_used, u_router + 1)
            m = st["lin"]
            v.tensor_copy(logits[0:36, :], bank(m)[0:36, 0, :]).then_inc(lin_evac[m % 2], 1)
            st["lin"] += 1
            dve.wait_ge(logits_turned, 1)
            link(v.tensor_tensor(lg, ps[:, 5, :].rearrange("p (a n) -> p a n", a=2)[:, :, 0:36],
                                 bias_row.unsqueeze(1).broadcast_to([P, 2, 36]), ALU.add))
            gl = lg[:, :, 0:N_GRP]
            el = lg[:, :, N_GRP:].rearrange("p a (g e) -> p a g e", g=N_GRP)

            def first_max(dst, src, n, keys, top, key, kmax):
                link(v.tensor_reduce(col(top), src, AX.X, ALU.max))
                link(v.tensor_tensor(col(key, n), src, wide(top, n), ALU.is_equal))
                link(v.tensor_tensor(col(key, n), col(key, n), keys, ALU.mult))
                link(v.tensor_reduce(col(kmax), col(key, n), AX.X, ALU.max))
                link(v.tensor_tensor(dst, col(key, n), wide(kmax, n), ALU.is_equal))

            first_max(col(12, 4), gl, N_GRP, gkeys, 0, 8, 3)
            v.tensor_tensor(col(4, 4), gl, wide(0, 4), ALU.subtract).then_inc(route_grp, 1)
            dve.wait_ge(route_grp_exp, 1)
            link(v.tensor_reduce(col(1), col(4, 4), AX.X, ALU.add))
            link(v.reciprocal(col(2), col(1)))
            link(v.tensor_scalar(col(16, 4), col(12, 4), -FAR, FAR, ALU.mult, ALU.add))
            for a in range(2):
                pen = rt[:, a, 16:20].unsqueeze(2).broadcast_to([P, N_GRP, 8])
                link(v.tensor_tensor(rt[:, a, 32:64].rearrange("p (g e) -> p g e", g=N_GRP), el[:, a], pen, ALU.add))
            first_max(col(96, 32), col(32, 32), N_EXP, ekeys, 20, 64, 21)
            link(v.scalar_tensor_tensor(out=col(128, 32), in0=col(96, 32), scalar=2 * FAR, in1=col(32, 32),
                                        op0=ALU.mult, op1=ALU.add))
            first_max(col(160, 32), col(128, 32), N_EXP, ekeys, 22, 64, 21)
            link(v.tensor_tensor(col(224, 32), col(96, 32), col(160, 32), ALU.add))
            dve.wait_ge(route_landed, 16)
            dve.sem_inc(ranks_go, 1)
            v.tensor_tensor(col(23), col(22), col(20), ALU.subtract).then_inc(route_two, 1)
            dve.wait_ge(route_two_exp, 1)
            link(v.tensor_scalar(col(25), col(24), 1.0, None, ALU.add))
            link(v.reciprocal(col(25), col(25)))
            link(v.tensor_tensor(col(25), col(25), col(2), ALU.mult))
            link(v.tensor_tensor(col(26), col(25), col(24), ALU.mult))
            link(v.tensor_tensor(col(96, 32), col(96, 32), wide(25, 32), ALU.mult))
            link(v.tensor_tensor(col(160, 32), col(160, 32), wide(26, 32), ALU.mult))
            link(v.tensor_tensor(gate[:, :, 0:N_EXP], col(96, 32), col(160, 32), ALU.add))
            split_low(ps[:, 0:4, :], xh[:].rearrange("p (b c) t -> p b (c t)", b=4),
                      xl[:].rearrange("p (b c) t -> p b (c t)", b=4), u_router + 1)
            dve.wait_ge(ranks_mm, 1)
            link(v.tensor_copy(counts, ps[:, 5, 0:3 * N_EXP].rearrange("p (a e) -> p a e", a=3)))
            link(v.tensor_scalar(counts[:, 0:2, :], counts[:, 0:2, :], 1.0, None, ALU.add))
            link(v.tensor_tensor(counts[:, 0:2, :], counts[:, 0:2, :], col(224, 32), ALU.mult))
            link(v.tensor_scalar(rank[:, :, 0:N_EXP], counts[:, 0:2, :], 1.0, None, ALU.subtract))
            dve.sem_inc(ranks_go, 1)
            dve.wait_ge(gate_h_there, 1)
            link(v.tensor_tensor(gate_hl[:, :, 0:N_EXP, 1], gate[:, :, 0:N_EXP],
                                 gate_hl[:, :, 0:N_EXP, 0].bitcast(F32), ALU.subtract))
            experts(moe)
            link(norm(x[:], 8, D, "g_final", dst=x, squared=True))

            norm(x[:], 8, D, "ev_norm")
            dve.wait_ge(second_landed, 48)
            dve.wait_ge(xl_ready, st["split"])
            for k in range(0, DC, 2):
                square(mem, k, k + 2)
            for a, u in enumerate(u_ev):
                ahead(u)
                m = st["lin"]
                dve.wait_ge(unit_used, u + 1)
                if a >= 2:
                    last = v.tensor_copy(pooled[0][:, 2 * a - 4:2 * a - 2, 16:], bank(m))
                elif a == 0:
                    last = v.tensor_copy(lat[:, 0:2, :], bank(m))
                else:
                    v.tensor_copy(lat[:, 2, :], bank(m)[:, 0, :])
                    last = v.tensor_copy(kr[0:ROPE, :], bank(m)[0:ROPE, 1, :])
                last.then_inc(lin_evac[m % 2], 1)
                dve.wait_ge(lin_evac[m % 2], m // 2 + 1)
                st["lin"] += 1
                if a == 1:
                    dve.wait_ge(angles, 1)
                    root(D, mem_rstd)
                    square(lat, 0, 2)
                    square(lat, 2, 3)
                    dve.sem_inc(kr_there, 1)
                elif a == 2:
                    norm(lat[:, 0:2, :], 2, 256, "q_norm", squared=True, parts=(ah, al))
                    norm(lat, 1, P, "kv_norm", squared=True, at=2, bank=4, parts=(ah, al))
            dve.sem_inc(pool_in, 1)
            all_out()
            ahead(u_qup)
            dve.wait_ge(trig, 1)
            link(v.tensor_scalar(sinr[0:QK, :], sinr[0:QK, :], freq[0:QK, 1:2], None, ALU.mult))
            dve.wait_ge(kr_mm, 1)
            link(v.tensor_tensor(kr[0:QK, :], ps[0:QK, 5, 0:T], cosr[0:QK, :], ALU.mult))
            link(v.tensor_tensor(hbuf[0:QK, 0, :], ps[0:QK, 5, T:2 * T], sinr[0:QK, :], ALU.mult))
            link(v.tensor_tensor(kr[0:QK, :], kr[0:QK, :], hbuf[0:QK, 0, :], ALU.add))
            dve.sem_inc(kr_turned, 1)
            cos8 = cosr[0:QK, :].unsqueeze(1).broadcast_to([QK, MLA_H, T])
            sin8 = sinr[0:QK, :].unsqueeze(1).broadcast_to([QK, MLA_H, T])
            dve.wait_ge(mq_there, 1)
            link(v.tensor_tensor(hbuf[0:QK, :, :], mq[0:QK, :, :], cos8, ALU.mult))
            ahead(u_kvup)
            link(scaled(mem, mem, 0, DC, "xa_m0", mem_rstd))
            dve.wait_ge(mq_mm, 1)
            link(v.tensor_tensor(mq[0:QK, :, :], ps[0:QK, 4:8, :].rearrange("p b (c t) -> p (b c) t", c=2), sin8,
                                 ALU.mult))
            v.tensor_tensor(mq[0:QK, :, :], mq[0:QK, :, :], hbuf[0:QK, :, :], ALU.add).then_inc(mq_turned, 1)
            dve.wait_ge(pooled_there, 1)
            dve.sem_inc(h_ready, 2)
            dve.wait_ge(unit_used, u_kvup + 1)
            v.tensor_copy(mv, ps[:, 6:8, :]).then_inc(kv_out, 1)
            split_low(ypool, ah[:], al[:], u_kvup + 1)
            split_low(mem, xh[:], xl[:], u_ev[-1] + 1)
            ahead(u_pool)
            st["lin"] += 2

            def memory_ahead(l, a):
                ahead(u_kv[l][a])
                st["lin"] += 1

            attend(steps_m, lambda k, w: my[:, k:k + w, :], lambda a: memory_ahead(0, a))
            all_out()
            dve.sem_inc(h_ready, 4)
            for src, at in ((ypool, 0), (my, 4)):
                for k in (0, 2):
                    to = slice(at + k, at + k + 2)
                    split_low(src[:, k:k + 2, :], xh[:, to, :], xl[:, to, :], u_kv[0][-1] + 1)
            residual(u_evo)

            def cross(l):
                norm(x[:], 8, D, f"xa_x{l}", squared=True)
                stage(u_xa[l][0][0:2])

                def queries_ahead(a):
                    if a in (1, 3):
                        ahead(u_xa[l][0][2 + a // 2])
                        st["lin"] += 1

                attend(steps_x[l], lambda k, w: xq[:, k:k + w, :], queries_ahead)
                dve.sem_inc(h_ready, 4)
                split_lows(xq, u_xa[l][0][-1] + 1)
                residual(u_xa[l][1])

            cross(0)
            norm(x[:], 8, D, "ffn0", squared=True)
            lam = vec[:, VECS["lam"][0]:VECS["lam"][0] + 8]
            row = lambda k: lsm[:, k, :]
            link(v.tensor_scalar(row(5), lam, -1.0, None, ALU.mult))
            v.tensor_tensor(row(0), row(5), lam, ALU.max).then_inc(lam_abs, 1)
            link(v.tensor_scalar(row(5), row(5), 0.0, None, ALU.max))
            dve.wait_ge(lam_exp, 1)
            link(v.tensor_scalar(row(2), row(1), 2.0, None, ALU.add))
            link(v.reciprocal(row(2), row(2)))
            link(v.tensor_tensor(row(2), row(2), row(1), ALU.mult))
            link(v.tensor_tensor(row(3), row(2), row(2), ALU.mult))
            link(v.tensor_scalar(row(4), row(3), 1.0 / 17, None, ALU.mult))
            for odd in range(15, 1, -2):
                link(v.scalar_tensor_tensor(out=row(4), in0=row(4), scalar=1.0 / odd, in1=row(3), op0=ALU.add,
                                            op1=ALU.mult))
            link(v.scalar_tensor_tensor(out=row(4), in0=row(4), scalar=1.0, in1=row(2), op0=ALU.add, op1=ALU.mult))
            link(v.scalar_tensor_tensor(out=row(4), in0=row(4), scalar=2.0, in1=row(5), op0=ALU.mult, op1=ALU.add))
            v.tensor_scalar(row(6), row(4), -LRU_C, None, ALU.mult)
            v.tensor_scalar(row(7), row(4), LRU_C / 2, None, ALU.mult).then_inc(lam_scale, 1)
            link(v.tensor_scalar(reset, posf, 0.0, None, ALU.is_equal))
            link(v.tensor_scalar(keep, reset, -1.0, 1.0, ALU.mult, ALU.add))
            link(v.memset(lxb[:, :, 0:4], 0.0))
            gated(ffn[0][0], ffn[0][1], trio0[0])

            norm(x[:], 8, D, "od_norm", squared=True)
            dve.wait_ge(mem_again, 16)
            for a in range(4):
                u, m = u_od[a], st["lin"]
                ahead(u)
                dve.wait_ge(unit_used, u + 1)
                v.tensor_copy(lxb[:, 2 * a:2 * a + 2, 4:], bank(m)).then_inc(lin_evac[m % 2], 1)
                st["lin"] += 1
                dve.wait_ge(lin_evac[m % 2], m // 2 + 1)
                for j in range(4):
                    for c in (2 * a, 2 * a + 1):
                        src = lxb[:, c, 1 + j:1 + j + T]
                        w = vcol("conv_w", j * 8 + c)
                        if j == 0:
                            last = v.tensor_scalar(lxc[:, c, :], src, w, vcol("conv_b", c), ALU.mult, ALU.add)
                        else:
                            last = v.scalar_tensor_tensor(out=lxc[:, c, :], in0=src, scalar=w, in1=lxc[:, c, :],
                                                          op0=ALU.mult, op1=ALU.add)
                    link(last)
                dve.sem_inc(h_ready, 1)
                if a >= 2:
                    two = slice(2 * a - 4, 2 * a - 2)
                    split_low(lxc[:, two, :], ah[:, two, :], al[:, two, :])
            for a in range(4):
                stage(u_od[4 + a:5 + a])
                last = scaled(mem, mem, 2 * a, 2 * a + 2, "xa_m1", mem_rstd)
            link(last)
            for a in (2, 3):
                two = slice(2 * a, 2 * a + 2)
                split_low(lxc[:, two, :], xh[:, two, :], xl[:, two, :], u_od[-1] + 1)
            all_out()
            ahead(u_rg)
            dve.sem_inc(h_ready, 4)
            ahead(u_rg + 1)
            split_lows(mem, u_rg + 2)
            memory_ahead(1, 0)
            dve.wait_ge(lru_t, 1)
            v.tensor_tensor(lr, lr, reset.unsqueeze(1).broadcast_to([P, DC, T]), ALU.max).then_inc(lru_t_max, 1)
            memory_ahead(1, 1)
            dve.wait_ge(lru_kept, 1)
            dve.wait_ge(lru_root, 1)
            link(v.scalar_tensor_tensor(out=lr, in0=lrc, scalar=1.0, in1=lr, op0=ALU.add, op1=ALU.mult))
            memory_ahead(1, 2)
            dve.wait_ge(lru_x, 1)
            link(v.tensor_tensor(li, li, lr, ALU.mult))
            memory_ahead(1, 3)
            for c in range(4):
                last = v.tensor_tensor_scan(lxc[:, c, :], lrc[:, c, :], li[:, c, :], 0.0, ALU.mult, ALU.add)
            memory_ahead(1, 4)
            for c in range(4, DC):
                last = v.tensor_tensor_scan(lxc[:, c, :], lrc[:, c, :], li[:, c, :], 0.0, ALU.mult, ALU.add)
            link(last)
            memory_ahead(1, 5)
            link(v.tensor_tensor(lgate, lgate, lxc, ALU.mult))
            dve.sem_inc(h_ready, 4)
            memory_ahead(1, 6)
            memory_ahead(1, 7)
            split_lows(lgate, u_kv[1][-1] + 1)
            all_out()
            residual(u_odo)
            cross(1)
            norm(x[:], 8, D, "ffn1", squared=True)
            gated(ffn[1][0], ffn[1][1], trio0[1])
            norm(x[:], 8, D, "final", dst=hbuf, squared=True, done=result)

        @block.gpsimd
        def _(pool):
            pool.wait_ge(att_mixed, len(steps_a))
            pool.dma_start(x[:], kview(t["xT"])).then_inc(x_again, 16)
            pool.wait_ge(moe_starts, 1)
            pool.dma_start(route, t["route"]).then_inc(route_landed, 16)
            st = dict(step=0)

            def link(ins):
                st["step"] += 1
                ins.then_inc(pool_step, 1)
                pool.wait_ge(pool_step, st["step"])

            g = nc.gpsimd
            pool.wait_ge(route_landed, 16)
            pool.wait_ge(ranks_go, 2)
            link(g.tensor_scalar(picks[:, 0, :], counts[:, 2, :], float(P), None, ALU.is_gt))
            link(g.tensor_copy(picks[:, 2, :], picks[:, 0, :]))
            a, b = 2, 7
            for back in (1, 2, 4, 8, 16):
                link(g.tensor_copy(picks[:, b, 0:back], picks[:, a, 0:back]))
                link(g.tensor_tensor(picks[:, b, back:], picks[:, a, back:], picks[:, a, 0:N_EXP - back], ALU.add))
                a, b = b, a
            for j in range(EXTRA):
                link(g.tensor_scalar(picks[:, 3 + j, :], picks[:, a, :], float(j + 1), None, ALU.is_equal))
                link(g.tensor_tensor(picks[:, 3 + j, :], picks[:, 3 + j, :], picks[:, 0, :], ALU.mult))
                chosen = picks[:, 3 + j, :].unsqueeze(1).broadcast_to([P, 2, N_EXP])
                link(g.tensor_tensor(weigh[:, 0, 0], picks[:, 3 + j, :], exp_no, ALU.mult))
                link(g.tensor_tensor(weigh[:, 1], counts[:, 0:2, :], chosen, ALU.mult))
                link(g.tensor_tensor(weigh[:, 2], gate[:, :, 0:N_EXP], chosen, ALU.mult))
                half = N_EXP // 2
                while half:
                    link(g.tensor_tensor(weigh[:, 0:3, :, 0:half], weigh[:, 0:3, :, 0:half],
                                         weigh[:, 0:3, :, half:2 * half], ALU.add))
                    half //= 2
                at = slice(N_EXP + j, N_EXP + j + 1)
                link(g.tensor_copy(pick_f[:, j:j + 1], weigh[:, 0, 0, 0:1]))
                link(g.tensor_scalar(rank[:, :, at], weigh[:, 1, :, 0:1], float(P + 1), None, ALU.subtract))
                link(g.tensor_copy(gate[:, :, at], weigh[:, 2, :, 0:1]))
            link(g.memset(rank[:, :, TILES:], -1.0))
            pool.sem_inc(extra_gates, 1)
            g.tensor_copy(pick_i[:, 0:EXTRA], pick_f[:, 0:EXTRA]).then_inc(extra_there, 1)
            pool.wait_ge(r_hid_mm, TILES + 1)
            pool.dma_start(mem, kview(t["memT"])).then_inc(second_landed, 16)
            pool.dma_start(c2, t["const2"]).then_inc(second_landed, 16)
            pool.dma_start(posi.bitcast(I32), t["positions_2"].partition_broadcast(P)).then_inc(second_landed, 16)
            pool.wait_ge(second_landed, 48)
            link(g.tensor_copy(posf, posi.bitcast(I32)))
            two_pi_hi, magic = 6.28125, 12582912.0
            two_pi_lo = 2 * np.pi - two_pi_hi
            a0, a1, n = cosr[0:QK, :], sinr[0:QK, :], turns[0:QK, :]
            link(g.tensor_scalar(a0, posf[0:QK, :], freq[0:QK, 0:1], None, ALU.mult))
            link(g.tensor_copy(a1, a0))
            for dst, quarter in ((a1, 0.0), (a0, 0.25)):
                link(g.tensor_scalar(n, dst, float(1 / (2 * np.pi)), quarter, ALU.mult, ALU.add))
                link(g.tensor_scalar(n, n, magic, None, ALU.add))
                link(g.tensor_scalar(n, n, magic, None, ALU.subtract))
                for part in (-two_pi_hi, -float(two_pi_lo)):
                    link(g.tensor_scalar(spare[0:QK, :], n, part, None, ALU.mult))
                    link(g.tensor_tensor(dst, spare[0:QK, :], dst, ALU.add))
                link(g.tensor_scalar(dst, dst, float(quarter * 2 * np.pi), 3.1415925, ALU.add, ALU.min))
                link(g.tensor_scalar(dst, dst, -3.1415925, None, ALU.max))
            pool.sem_inc(angles, 1)
            for b in range(3):
                link(g.memset(pooled[b][:, :, 0:16], 0.0))
            pool.wait_ge(pool_in, 1)
            p0_, p1_, p2_ = pooled
            for k, (dst, src, back) in enumerate(((p1_, p0_, 1), (p2_, p1_, 2), (p1_, p2_, 4), (p2_, p1_, 8))):
                link(g.tensor_tensor(dst[:, k:, 16:], src[:, k:, 16:], src[:, k:, 16 - back:16 - back + T], ALU.add))
            for k in range(4):
                src = (p1_, p2_)[k % 2][:, k, 16:]
                link(g.tensor_tensor(src, src, icnt[:, k, :], ALU.mult))
                link(g.tensor_tensor(ypool[:, k, :], src, p0_[:, k, 16:], ALU.subtract))
            pool.sem_inc(pooled_there, 1)
            pool.wait_ge(kr_turned, 1)
            g.tensor_copy(mk[NOPE:QK, :, :], kr[NOPE:QK, :].unsqueeze(1).broadcast_to([ROPE, MLA_H, T])).then_inc(
                mk_rope_there, 1)
            pool.wait_ge(att_mixed, len(steps_a) + len(steps_m) + len(steps_x[0]))
            pool.dma_start(mem, kview(t["memT"])).then_inc(mem_again, 16)
            pool.wait_ge(lru_i, 1)
            link(g.tensor_tensor(li, li, lxc, ALU.mult))
            pool.sem_inc(lru_x, 1)
            pool.wait_ge(lru_a, 1)
            link(g.tensor_tensor(lrc, lrc, keep.unsqueeze(1).broadcast_to([P, DC, T]), ALU.mult))
            pool.sem_inc(lru_kept, 1)


_BIG = ["w_in", "w_br_dil", "w_br_swa", "w_out", "w_e_gate", "w_e_up", "w_e_down", "ev_w_in_2", "ev_pool_w_2",
        "ev_w_q_up_2", "ev_w_kv_up_2", "ev_w_out_2", "od_w_in_2", "od_w_rgate_2", "od_w_igate_2", "od_w_out_2",
        "xa_w_q_2", "xa_w_kv_2", "xa_w_o_2", "ffn_w_gate_up_2", "ffn_w_down_2"]


def kernel(**inputs):
    import concourse.bacc as _bacc
    from concourse.bass_utils import run_bass_kernel_spmd as _run

    a = {k: np.asarray(v) for k, v in inputs.items()}
    arrays = {k: np.ascontiguousarray(a[k]) for k in _BIG}
    arrays["xT"] = np.ascontiguousarray(a["x"][0].T)
    arrays["memT"] = np.ascontiguousarray(a["mem_2"][0].T)
    arrays["positions_2"] = a["positions_2"].reshape(T)
    arrays["sinks"] = a["sinks"].reshape(SWA_HEADS)
    arrays["b_route"] = np.concatenate([a["b_group"][0], a["b_router"][0]])
    arrays["w_route"] = np.ascontiguousarray(
        np.concatenate([a["w_group"][0], a["w_router"][0]], 1).reshape(DC, P, 36).transpose(1, 0, 2).reshape(P, -1))
    cols = {"g_mix": a["g_mix"], "g_ffn": a["g_ffn"], "g_final": a["g_final"], "ev_norm": a["ev_norm_2"],
            "pool_scale": a["ev_pool_scale_2"], "q_norm": a["ev_q_norm_2"], "kv_norm": a["ev_kv_norm_2"],
            "od_norm": a["od_norm_2"], "conv_w": a["od_conv_w_2"], "conv_b": a["od_conv_b_2"],
            "b_r": a["od_b_rgate_2"], "b_i": a["od_b_igate_2"], "lam": a["od_lambda_2"],
            "xa_x0": a["xa_norm_x_2"][0], "xa_x1": a["xa_norm_x_2"][1], "xa_m0": a["xa_norm_mem_2"][0],
            "xa_m1": a["xa_norm_mem_2"][1], "ffn0": a["ffn_norm_2"][0], "ffn1": a["ffn_norm_2"][1],
            "final": a["final_norm_2"]}
    arrays["vecs"] = np.ascontiguousarray(np.concatenate([cols[n].reshape(-1, P).T for n in VECS], 1))
    arrays["const1"], arrays["const2"], arrays["route"] = shape_constants()

    nc = _bacc.Bacc("TRN2", target_bir_lowering=False, num_devices=1)
    t = {k: nc.dram_tensor(f"{k}_dram", v.shape, mybir.dt.from_np(v.dtype), kind="ExternalInput").ap()
         for k, v in arrays.items()}
    out = nc.dram_tensor("out_dram", (D, T), F32, kind="ExternalOutput").ap()
    build(nc, t, out)
    r = _run(nc, [{f"{k}_dram": v for k, v in arrays.items()}], core_ids=[0])
    return np.ascontiguousarray(r.results[0]["out_dram"].T).reshape(1, T, D)
```
